# Optimizing a Trainium2 kernel written in Bass

```python
import math
import jax
import jax.numpy as jnp
from jax import lax
import numpy as np
import jax, jax.numpy as jnp

D_MODEL = 1024
BATCH = 1
SEQ = 256
DEPTH = 1

GROUP_HEADS = 4
HEAD_DIM = 64
GROUP_WIDTH = GROUP_HEADS * HEAD_DIM
N_GROUPS = 4
D_MIX = N_GROUPS * GROUP_WIDTH
IN_SIZES = (GROUP_WIDTH, GROUP_WIDTH, GROUP_WIDTH, GROUP_WIDTH, GROUP_HEADS, GROUP_HEADS, GROUP_WIDTH, GROUP_WIDTH, GROUP_WIDTH, GROUP_WIDTH, GROUP_WIDTH, GROUP_WIDTH, GROUP_WIDTH, GROUP_WIDTH, GROUP_WIDTH, GROUP_WIDTH)
N_IN = sum(IN_SIZES)
MLSTM_F_OFFSET = 4 * GROUP_WIDTH + GROUP_HEADS
MLSTM_CHUNK = 64
HGRN_CHUNK = 64
SCONV_WIDTH = 3
MOBA_BLOCK = 256
MOBA_TOPK = 3
MOBA_QCHUNK = 32
REL_BUCKETS = 32
REL_MAX_DIST = 128
N_MEM = 256
CROSS_HEADS = 4
CROSS_HEAD_DIM = 128
CROSS_WIDTH = CROSS_HEADS * CROSS_HEAD_DIM
D_FF = 2816
FFN_CONV_WIDTH = 3
RMS_EPS = 1e-6
NEG_BIG = -1e30


def rmsnorm(x, gain):
    x32 = x.astype(jnp.float32)
    y = x32 * lax.rsqrt(jnp.mean(x32 * x32, axis=-1, keepdims=True) + RMS_EPS)
    return (y * gain.astype(jnp.float32)).astype(x.dtype)

def head_rmsnorm(h, gain):
    b, nh, s, d = h.shape
    h32 = h.astype(jnp.float32).transpose(0, 2, 1, 3)
    h32 = h32 * lax.rsqrt(jnp.mean(h32 * h32, axis=-1, keepdims=True) + RMS_EPS)
    return h32.reshape(b, s, nh * d) * gain.astype(jnp.float32)

def causal_dwconv(x, w):
    width, ch = w.shape
    return lax.conv_general_dilated(x, w.astype(x.dtype)[:, None, :], window_strides=(1,), padding=[(width - 1, 0)], dimension_numbers=('NWC', 'WIO', 'NWC'), feature_group_count=ch)

def to_heads(a, n_heads):
    b, s, _ = a.shape
    return a.reshape(b, s, n_heads, -1).transpose(0, 2, 1, 3)

def _chunks(a, size):
    b, h, s = a.shape[:3]
    return jnp.moveaxis(a.reshape(b, h, s // size, size, *a.shape[3:]), 2, 0)

def _unchunk(a):
    nc, b, h, l, d = a.shape
    return jnp.moveaxis(a, 0, 2).reshape(b, h, nc * l, d)

def rel_bucket(dist):
    n = jnp.maximum(dist, 0)
    exact = REL_BUCKETS // 2
    nf = jnp.maximum(n, 1).astype(jnp.float32)
    large = exact + (jnp.log(nf / exact) / math.log(REL_MAX_DIST / exact) * (REL_BUCKETS - exact)).astype(jnp.int32)
    large = jnp.minimum(large, REL_BUCKETS - 1)
    return jnp.where(n < exact, n, large)

def mlstm_chunkwise(q, k, v, i_pre, f_pre):
    b, nh, s, d = q.shape
    f32 = jnp.float32
    q = q.astype(f32)
    k = k.astype(f32) * (d ** -0.5)
    v = v.astype(f32)
    log_i = i_pre.astype(f32)
    log_f = jax.nn.log_sigmoid(f_pre.astype(f32))
    causal = jnp.tril(jnp.ones((MLSTM_CHUNK, MLSTM_CHUNK), dtype=bool))

    def step(carry, xs):
        c_mat, n_vec, m_prev = carry
        qc, kc, vc, lic, lfc = xs
        g = jnp.cumsum(lfc, axis=-1)
        dlog = jnp.where(causal, g[..., :, None] - g[..., None, :] + lic[..., None, :], NEG_BIG)
        a = g + m_prev[..., None]
        m_t = jnp.maximum(a, jnp.max(dlog, axis=-1))
        w = jnp.exp(dlog - m_t[..., None]) * jnp.einsum('bhtd,bhsd->bhts', qc, kc)
        inter = jnp.exp(a - m_t)
        num = jnp.einsum('bhts,bhsd->bhtd', w, vc) + inter[..., None] * jnp.einsum('bhvk,bhtk->bhtv', c_mat, qc)
        den = jnp.sum(w, axis=-1) + inter * jnp.einsum('bhk,bhtk->bht', n_vec, qc)
        h = num / jnp.maximum(jnp.abs(den), jnp.exp(-m_t))[..., None]
        g_last = g[..., -1]
        u = g_last[..., None] - g + lic
        m_new = jnp.maximum(g_last + m_prev, jnp.max(u, axis=-1))
        ws = jnp.exp(u - m_new[..., None])
        decay = jnp.exp(g_last + m_prev - m_new)
        c_new = decay[..., None, None] * c_mat + jnp.einsum('bhs,bhsv,bhsk->bhvk', ws, vc, kc)
        n_new = decay[..., None] * n_vec + jnp.einsum('bhs,bhsk->bhk', ws, kc)
        return (c_new, n_new, m_new), h

    init = (jnp.zeros((b, nh, d, d), f32), jnp.zeros((b, nh, d), f32), jnp.zeros((b, nh), f32))
    _, hs = lax.scan(step, init, tuple(_chunks(a, MLSTM_CHUNK) for a in (q, k, v, log_i, log_f)))
    return _unchunk(hs)

def hgrn2_chunkwise(q, k, log_f, v):
    b, nh, s, dk = q.shape
    dv = v.shape[-1]
    causal = jnp.tril(jnp.ones((HGRN_CHUNK, HGRN_CHUNK), dtype=bool))[:, :, None]

    def step(state, xs):
        qc, kc, lfc, vc = xs
        g = jnp.cumsum(lfc, axis=2)
        rel = jnp.exp(jnp.where(causal, g[:, :, :, None, :] - g[:, :, None, :, :], NEG_BIG))
        attn = jnp.einsum('bhtk,bhtsk,bhsk->bhts', qc, rel, kc)
        out = jnp.einsum('bhts,bhsv->bhtv', attn, vc) + jnp.einsum('bhtk,bhkv->bhtv', qc * jnp.exp(g), state)
        g_last = g[:, :, -1:, :]
        new_state = jnp.exp(g_last[:, :, 0, :])[..., None] * state + jnp.einsum('bhsk,bhsv->bhkv', kc * jnp.exp(g_last - g), vc)
        return new_state, out

    init = jnp.zeros((b, nh, dk, dv), jnp.float32)
    _, outs = lax.scan(step, init, tuple(_chunks(a, HGRN_CHUNK) for a in (q, k, log_f, v)))
    return _unchunk(outs)

def moba_attention(q, k, v, rel_bias):
    b, nh, s, d = q.shape
    f32 = jnp.float32
    nb = -(-s // MOBA_BLOCK)
    s_pad = nb * MOBA_BLOCK
    padw = ((0, 0), (0, 0), (0, s_pad - s), (0, 0))
    q, k, v = jnp.pad(q, padw), jnp.pad(k, padw), jnp.pad(v, padw)
    kb = k.reshape(b, nh, nb, MOBA_BLOCK, d)
    vb = v.reshape(b, nh, nb, MOBA_BLOCK, d)
    n_sel = min(MOBA_TOPK, nb - 1)
    scale = d ** -0.5
    bias_t = rel_bias.astype(f32).T
    blk_of = jnp.arange(s_pad, dtype=jnp.int32) // MOBA_BLOCK
    if n_sel > 0:
        kmean = jnp.mean(kb.astype(f32), axis=3)
        gate = jnp.einsum('bhsd,bhnd->bhsn', q.astype(f32), kmean)
        past = jnp.arange(nb, dtype=jnp.int32)[None, :] < blk_of[:, None]
        gate = jnp.where(past, gate, NEG_BIG)
        _, sel = lax.top_k(gate, n_sel)
        sel = sel.astype(jnp.int32)
        sel_valid = sel < blk_of[:, None]
    b_ix = jnp.arange(b)[:, None, None, None]
    h_ix = jnp.arange(nh)[None, :, None, None]
    key_off = jnp.arange(MOBA_BLOCK, dtype=jnp.int32)

    def attend_chunk(c):
        start = c * MOBA_QCHUNK
        qc = lax.dynamic_slice_in_dim(q, start, MOBA_QCHUNK, axis=2)
        t = start + jnp.arange(MOBA_QCHUNK, dtype=jnp.int32)
        j = start // MOBA_BLOCK
        k_own = lax.dynamic_index_in_dim(kb, j, axis=2, keepdims=False)
        v_own = lax.dynamic_index_in_dim(vb, j, axis=2, keepdims=False)
        dist_own = t[:, None] - (j * MOBA_BLOCK + key_off)[None, :]
        s_own = jnp.einsum('bhqd,bhkd->bhqk', qc, k_own).astype(f32) * scale + bias_t[:, rel_bucket(dist_own)][None]
        s_own = jnp.where(dist_own >= 0, s_own, NEG_BIG)
        if n_sel == 0:
            p = jax.nn.softmax(s_own, axis=-1)
            out = jnp.einsum('bhqk,bhkd->bhqd', p, v_own.astype(f32))
        else:
            sel_c = lax.dynamic_slice_in_dim(sel, start, MOBA_QCHUNK, axis=2)
            valid_c = lax.dynamic_slice_in_dim(sel_valid, start, MOBA_QCHUNK, axis=2)
            k_sel = kb[b_ix, h_ix, sel_c]
            v_sel = vb[b_ix, h_ix, sel_c]
            dist = t[None, None, :, None, None] - (sel_c[..., None] * MOBA_BLOCK + key_off)
            bias = bias_t[h_ix[..., None], rel_bucket(dist)]
            s_past = jnp.einsum('bhqd,bhqnkd->bhqnk', qc, k_sel).astype(f32) * scale + bias
            s_past = jnp.where(valid_c[..., None], s_past, NEG_BIG)
            n_past = n_sel * MOBA_BLOCK
            p = jax.nn.softmax(jnp.concatenate([s_past.reshape(b, nh, MOBA_QCHUNK, n_past), s_own], axis=-1), axis=-1)
            p_past = p[..., :n_past].reshape(b, nh, MOBA_QCHUNK, n_sel, MOBA_BLOCK)
            out = jnp.einsum('bhqnk,bhqnkd->bhqd', p_past, v_sel.astype(f32)) + jnp.einsum('bhqk,bhkd->bhqd', p[..., n_past:], v_own.astype(f32))
        return out.astype(q.dtype)

    outs = lax.map(attend_chunk, jnp.arange(s_pad // MOBA_QCHUNK, dtype=jnp.int32))
    return _unchunk(outs)[:, :, :s]

def token_mixer(xn, w_in, b_in, mlstm_norm, sconv_w, rel_bias, hgrn_lb, hgrn_norm, w_out):
    b, s, _ = xn.shape
    f32 = jnp.float32
    dt = xn.dtype
    proj = xn @ w_in + b_in
    splits = np.cumsum(IN_SIZES)[:-1].tolist()
    (m_q, m_k, m_v, m_o, m_i, m_f, c_b, c_c, c_h, a_q, a_k, a_v, h_q, h_f, h_i, h_g) = jnp.split(proj, splits, axis=-1)
    h_m = mlstm_chunkwise(to_heads(m_q, GROUP_HEADS), to_heads(m_k, GROUP_HEADS), to_heads(m_v, GROUP_HEADS), m_i.transpose(0, 2, 1), m_f.transpose(0, 2, 1))
    y_m = head_rmsnorm(h_m, mlstm_norm) * jax.nn.sigmoid(m_o.astype(f32))
    y_c = c_b * causal_dwconv(c_c * c_h, sconv_w)
    y_a = moba_attention(to_heads(a_q, GROUP_HEADS), to_heads(a_k, GROUP_HEADS), to_heads(a_v, GROUP_HEADS), rel_bias)
    y_a = y_a.transpose(0, 2, 1, 3).reshape(b, s, GROUP_WIDTH)
    lb = hgrn_lb.astype(f32).reshape(1, GROUP_HEADS, 1, HEAD_DIM)
    z = to_heads(h_f, GROUP_HEADS).astype(f32)
    f_gate = lb + (1.0 - lb) * jax.nn.sigmoid(z)
    log_f = jnp.log(f_gate)
    k_h = 1.0 - f_gate
    q_h = jax.nn.silu(to_heads(h_q, GROUP_HEADS).astype(f32))
    o_h = hgrn2_chunkwise(q_h, k_h, log_f, to_heads(h_i, GROUP_HEADS).astype(f32))
    y_h = head_rmsnorm(o_h, hgrn_norm) * jax.nn.silu(h_g.astype(f32))
    y = jnp.concatenate([y_m.astype(dt), y_c.astype(dt), y_a.astype(dt), y_h.astype(dt)], axis=-1)
    return y @ w_out

def memory_cross_attention(xn, memn, wq, wk, wv, wo):
    b, s, _ = xn.shape
    m = memn.shape[1]
    q = (xn @ wq).reshape(b, s, CROSS_HEADS, CROSS_HEAD_DIM)
    k = (memn @ wk).reshape(b, m, CROSS_HEADS, CROSS_HEAD_DIM)
    v = (memn @ wv).reshape(b, m, CROSS_HEADS, CROSS_HEAD_DIM)
    logits = jnp.einsum('bshd,bmhd->bhsm', q, k).astype(jnp.float32) * (CROSS_HEAD_DIM ** -0.5)
    p = jax.nn.softmax(logits, axis=-1)
    o = jnp.einsum('bhsm,bmhd->bshd', p, v.astype(jnp.float32)).astype(xn.dtype).reshape(b, s, CROSS_WIDTH)
    return o @ wo

def conv_glu_ffn(xn, w_up, conv_w, conv_b, w_down):
    gu = xn @ w_up
    gate, up = jnp.split(gu, 2, axis=-1)
    gate = causal_dwconv(gate, conv_w) + conv_b.astype(gate.dtype)
    return (jax.nn.silu(gate) * up) @ w_down

def first_inputs(seed: int = 0) -> dict:
    key = jax.random.key(seed)
    ks = jax.random.split(key, 26)
    f32 = jnp.float32

    def nrm(k, shape, scale):
        return scale * jax.random.normal(k, shape, f32)

    def gain(k, shape):
        return 1.0 + 0.05 * jax.random.normal(k, shape, f32)

    b_in = nrm(ks[3], (DEPTH, N_IN), 0.01)
    b_in = b_in.at[:, MLSTM_F_OFFSET:MLSTM_F_OFFSET + GROUP_HEADS].add(jnp.linspace(3.0, 6.0, GROUP_HEADS))
    return {
        'x': nrm(ks[0], (BATCH, SEQ, D_MODEL), 1.0),
        'mem': nrm(ks[1], (BATCH, N_MEM, D_MODEL), 1.0),
        'w_in': nrm(ks[2], (DEPTH, D_MODEL, N_IN), D_MODEL ** -0.5),
        'b_in': b_in,
        'mlstm_norm': gain(ks[4], (DEPTH, GROUP_WIDTH)),
        'sconv_w': nrm(ks[5], (DEPTH, SCONV_WIDTH, GROUP_WIDTH), SCONV_WIDTH ** -0.5),
        'rel_bias': nrm(ks[6], (REL_BUCKETS, GROUP_HEADS), 0.5),
        'hgrn_lb_logits': nrm(ks[7], (DEPTH, GROUP_WIDTH), 0.5),
        'hgrn_norm': gain(ks[8], (DEPTH, GROUP_WIDTH)),
        'w_mix_out': nrm(ks[9], (DEPTH, D_MIX, D_MODEL), D_MIX ** -0.5),
        'norm_mix_pre': gain(ks[10], (DEPTH, D_MODEL)),
        'norm_mix_post': gain(ks[11], (DEPTH, D_MODEL)),
        'mem_norm': gain(ks[12], (DEPTH, D_MODEL)),
        'w_cq': nrm(ks[13], (DEPTH, D_MODEL, CROSS_WIDTH), D_MODEL ** -0.5),
        'w_ck': nrm(ks[14], (DEPTH, D_MODEL, CROSS_WIDTH), D_MODEL ** -0.5),
        'w_cv': nrm(ks[15], (DEPTH, D_MODEL, CROSS_WIDTH), D_MODEL ** -0.5),
        'w_co': nrm(ks[16], (DEPTH, CROSS_WIDTH, D_MODEL), CROSS_WIDTH ** -0.5),
        'norm_cross_pre': gain(ks[17], (DEPTH, D_MODEL)),
        'norm_cross_post': gain(ks[18], (DEPTH, D_MODEL)),
        'w_ffn_in': nrm(ks[19], (DEPTH, D_MODEL, 2 * D_FF), D_MODEL ** -0.5),
        'ffn_conv_w': nrm(ks[20], (DEPTH, FFN_CONV_WIDTH, D_FF), FFN_CONV_WIDTH ** -0.5),
        'ffn_conv_b': nrm(ks[21], (DEPTH, D_FF), 0.01),
        'w_ffn_out': nrm(ks[22], (DEPTH, D_FF, D_MODEL), D_FF ** -0.5),
        'norm_ffn_pre': gain(ks[23], (DEPTH, D_MODEL)),
        'norm_ffn_post': gain(ks[24], (DEPTH, D_MODEL)),
    }

def first_block(x, mem, w_in, b_in, mlstm_norm, sconv_w, rel_bias, hgrn_lb_logits, hgrn_norm, w_mix_out, norm_mix_pre, norm_mix_post, mem_norm, w_cq, w_ck, w_cv, w_co, norm_cross_pre, norm_cross_post, w_ffn_in, ffn_conv_w, ffn_conv_b, w_ffn_out, norm_ffn_pre, norm_ffn_post):
    lb_soft = jax.nn.softmax(hgrn_lb_logits.astype(jnp.float32), axis=0)
    lb_all = jnp.cumsum(lb_soft, axis=0) - lb_soft[0]
    for l in range(DEPTH):
        h = token_mixer(rmsnorm(x, norm_mix_pre[l]), w_in[l], b_in[l], mlstm_norm[l], sconv_w[l], rel_bias, lb_all[l], hgrn_norm[l], w_mix_out[l])
        x = x + rmsnorm(h, norm_mix_post[l])
        h = memory_cross_attention(rmsnorm(x, norm_cross_pre[l]), rmsnorm(mem, mem_norm[l]), w_cq[l], w_ck[l], w_cv[l], w_co[l])
        x = x + rmsnorm(h, norm_cross_post[l])
        h = conv_glu_ffn(rmsnorm(x, norm_ffn_pre[l]), w_ffn_in[l], ffn_conv_w[l], ffn_conv_b[l], w_ffn_out[l])
        x = x + rmsnorm(h, norm_ffn_post[l])
    return x


FOX_HEADS = 8
NSA_HEADS = 8
NSA_GROUPS = 2
NSA_HPG = NSA_HEADS // NSA_GROUPS
BRANCH_WIDTH = 512
N_BRANCH = 2
N_NSA_BRANCH = 3
ROPE_DIM = HEAD_DIM // 4
ROPE_THETA = 500000.0
Q_BLOCK = 128
CMP_LEN = 32
CMP_STRIDE = 16
CMP_HIDDEN = 2 * HEAD_DIM
SLC_LEN = 64
SLC_TOP = 16
WINDOW = 512
FORGET_BIAS_INIT = 4.0
FORCED_SCORE = 1e9
NEG_INF = -1e30
PEER_HEADS = 8
N_KEYS = 128
N_EXPERTS = N_KEYS * N_KEYS
PEER_QDIM = 256
PEER_TOPK = 16
PEER_CHUNK = 128

KV_WIDTH = NSA_GROUPS * HEAD_DIM
IN_SPLITS = (BRANCH_WIDTH, BRANCH_WIDTH, BRANCH_WIDTH, FOX_HEADS, BRANCH_WIDTH,
             KV_WIDTH, KV_WIDTH, KV_WIDTH, KV_WIDTH, KV_WIDTH, KV_WIDTH,
             NSA_HEADS * N_NSA_BRANCH, N_BRANCH * D_MODEL)
D_IN = sum(IN_SPLITS)


def rmsnorm_2(x, g):
    xf = x.astype(jnp.float32)
    y = xf * lax.rsqrt(jnp.mean(xf * xf, axis=-1, keepdims=True) + RMS_EPS)
    return (y * g.astype(jnp.float32)).astype(x.dtype)

def split_columns(t, sizes):
    offs = np.cumsum((0,) + tuple(sizes))
    return [t[..., int(a):int(b)] for a, b in zip(offs[:-1], offs[1:])]

def rope_tables(pos):
    inv = jnp.power(ROPE_THETA, -jnp.arange(0, ROPE_DIM, 2, dtype=jnp.float32) / ROPE_DIM)
    ang = pos[:, None] * inv[None, :]
    return jnp.cos(ang), jnp.sin(ang)

def apply_partial_rope(x, cos, sin):
    half = ROPE_DIM // 2
    xr = x[..., :ROPE_DIM].astype(jnp.float32)
    x1, x2 = xr[..., :half], xr[..., half:]
    c, s = cos[:, None, :], sin[:, None, :]
    rot = jnp.concatenate([x1 * c - x2 * s, x1 * s + x2 * c], axis=-1)
    return jnp.concatenate([rot.astype(x.dtype), x[..., ROPE_DIM:]], axis=-1)

def fox_attention(q, k, v, log_f):
    B_, S_, H, Dh = q.shape
    scale = Dh ** -0.5
    c = jnp.swapaxes(jnp.cumsum(log_f, axis=1), 1, 2)
    k_pos = jnp.arange(S_)

    def block(i):
        q0 = i * Q_BLOCK
        q_pos = q0 + jnp.arange(Q_BLOCK)
        qb = lax.dynamic_slice_in_dim(q, q0, Q_BLOCK, axis=1)
        cb = lax.dynamic_slice_in_dim(c, q0, Q_BLOCK, axis=2)
        logits = jnp.einsum('bqhd,bkhd->bhqk', qb, k).astype(jnp.float32) * scale
        logits = logits + (cb[..., :, None] - c[..., None, :])
        mask = k_pos[None, :] <= q_pos[:, None]
        p = jax.nn.softmax(jnp.where(mask, logits, NEG_INF), axis=-1)
        return jnp.einsum('bhqk,bkhd->bqhd', p.astype(v.dtype), v).reshape(B_, Q_BLOCK, H * Dh)

    out = lax.map(block, jnp.arange(S_ // Q_BLOCK))
    return jnp.moveaxis(out, 0, 1).reshape(B_, S_, H * Dh)

def compress_kv(k, v, cmp_pos, w1, w2):
    B_, S_ = k.shape[0], k.shape[1]
    n_cmp = (S_ - CMP_LEN) // CMP_STRIDE + 1
    starts = np.arange(n_cmp) * CMP_STRIDE
    idx = starts[:, None] + np.arange(CMP_LEN)[None, :]

    def phi(t, j):
        blocks = t[:, idx] + cmp_pos[j][None, None, :, None, :]
        flat = jnp.swapaxes(blocks, 2, 3).reshape(B_, n_cmp, NSA_GROUPS, CMP_LEN * HEAD_DIM)
        return jax.nn.gelu(flat @ w1[j], approximate=False) @ w2[j]

    return phi(k, 0), phi(v, 1), jnp.asarray(starts + CMP_LEN - 1, dtype=jnp.int32)

def nsa_attention(q, k_cmp, v_cmp, cmp_end, k_slc, v_slc, k_win, v_win, gates):
    B_, S_, H, Dh = q.shape
    G = NSA_GROUPS
    scale = Dh ** -0.5
    n_cmp = k_cmp.shape[1]
    n_slc = S_ // SLC_LEN
    top = min(SLC_TOP, n_slc)
    cs = np.arange(n_cmp)[:, None] * CMP_STRIDE
    ss = np.arange(n_slc)[None, :] * SLC_LEN
    ov = np.clip(np.minimum(cs + CMP_LEN, ss + SLC_LEN) - np.maximum(cs, ss), 0, None) / CMP_LEN
    overlap = jnp.asarray(ov, dtype=jnp.float32)
    kb = k_slc.reshape(B_, n_slc, SLC_LEN, G, Dh).transpose(0, 3, 1, 2, 4)
    vb = v_slc.reshape(B_, n_slc, SLC_LEN, G, Dh).transpose(0, 3, 1, 2, 4)
    pad = ((0, 0), (WINDOW, 0), (0, 0), (0, 0))
    kwp, vwp = jnp.pad(k_win, pad), jnp.pad(v_win, pad)
    bi = jnp.arange(B_)[:, None, None, None]
    gi = jnp.arange(G)[None, :, None, None]
    blk_ids = jnp.arange(n_slc)

    def block(i):
        q0 = i * Q_BLOCK
        q_pos = q0 + jnp.arange(Q_BLOCK)
        qb = lax.dynamic_slice_in_dim(q, q0, Q_BLOCK, axis=1).reshape(B_, Q_BLOCK, G, NSA_HPG, Dh)
        gb = lax.dynamic_slice_in_dim(gates, q0, Q_BLOCK, axis=1).reshape(B_, Q_BLOCK, G, NSA_HPG, N_NSA_BRANCH)
        lc = jnp.einsum('bqghd,bngd->bghqn', qb, k_cmp).astype(jnp.float32) * scale
        mc = cmp_end[None, :] <= q_pos[:, None]
        pc = jax.nn.softmax(jnp.where(mc, lc, NEG_INF), axis=-1) * mc
        o_cmp = jnp.einsum('bghqn,bngd->bqghd', pc.astype(v_cmp.dtype), v_cmp)
        imp = jnp.einsum('bghqn,nj->bgqj', pc, overlap)
        q_blk = q_pos // SLC_LEN
        forced = (blk_ids[None, :] == 0) | (blk_ids[None, :] == q_blk[:, None]) | (blk_ids[None, :] == q_blk[:, None] - 1)
        causal = blk_ids[None, :] <= q_blk[:, None]
        score = jnp.where(forced, FORCED_SCORE, jnp.where(causal, imp, -1.0))
        _, sel = lax.top_k(score, top)
        k_sel = kb[bi, gi, sel]
        v_sel = vb[bi, gi, sel]
        ls = jnp.einsum('bqghd,bgqkld->bghqkl', qb, k_sel).astype(jnp.float32) * scale
        tok = sel[..., None] * SLC_LEN + jnp.arange(SLC_LEN)
        ms = (tok <= q_pos[None, None, :, None, None])[:, :, None]
        ls = jnp.where(ms, ls, NEG_INF).reshape(B_, G, NSA_HPG, Q_BLOCK, top * SLC_LEN)
        ps = jax.nn.softmax(ls, axis=-1).reshape(B_, G, NSA_HPG, Q_BLOCK, top, SLC_LEN)
        o_slc = jnp.einsum('bghqkl,bgqkld->bqghd', ps.astype(v_sel.dtype), v_sel)
        kwb = lax.dynamic_slice_in_dim(kwp, q0, WINDOW + Q_BLOCK, axis=1)
        vwb = lax.dynamic_slice_in_dim(vwp, q0, WINDOW + Q_BLOCK, axis=1)
        k_pos = q0 - WINDOW + jnp.arange(WINDOW + Q_BLOCK)
        lw = jnp.einsum('bqghd,bkgd->bghqk', qb, kwb).astype(jnp.float32) * scale
        rel = q_pos[:, None] - k_pos[None, :]
        mw = (rel >= 0) & (rel < WINDOW) & (k_pos[None, :] >= 0)
        pw = jax.nn.softmax(jnp.where(mw, lw, NEG_INF), axis=-1)
        o_win = jnp.einsum('bghqk,bkgd->bqghd', pw.astype(vwb.dtype), vwb)
        o = gb[..., 0:1] * o_cmp + gb[..., 1:2] * o_slc + gb[..., 2:3] * o_win
        return o.astype(q.dtype).reshape(B_, Q_BLOCK, H * Dh)

    out = lax.map(block, jnp.arange(S_ // Q_BLOCK))
    return jnp.moveaxis(out, 0, 1).reshape(B_, S_, H * Dh)

def hybrid_mixer(h, w_in, fox_f_bias, cmp_pos, cmp_w1, cmp_w2, w_branch, w_out):
    B_, S_, _ = h.shape
    proj = h @ w_in
    (fq, fk, fv, f_logit, nq, kc, vc, ksl, vsl, kwn, vwn,
     nsa_gate_logit, merge_logit) = split_columns(proj, IN_SPLITS)
    heads = lambda t, n: t.reshape(B_, S_, n, HEAD_DIM)
    log_f = jax.nn.log_sigmoid(f_logit.astype(jnp.float32) + fox_f_bias.astype(jnp.float32))
    y_fox = fox_attention(heads(fq, FOX_HEADS), heads(fk, FOX_HEADS), heads(fv, FOX_HEADS), log_f)
    cos, sin = rope_tables(jnp.arange(S_, dtype=jnp.float32))
    q_nsa = apply_partial_rope(heads(nq, NSA_HEADS), cos, sin)
    k_slc = apply_partial_rope(heads(ksl, NSA_GROUPS), cos, sin)
    k_win = apply_partial_rope(heads(kwn, NSA_GROUPS), cos, sin)
    k_cmp, v_cmp, cmp_end = compress_kv(heads(kc, NSA_GROUPS), heads(vc, NSA_GROUPS), cmp_pos, cmp_w1, cmp_w2)
    k_cmp = apply_partial_rope(k_cmp, *rope_tables(cmp_end.astype(jnp.float32)))
    gates = jax.nn.sigmoid(nsa_gate_logit.astype(jnp.float32)).reshape(B_, S_, NSA_HEADS, N_NSA_BRANCH)
    y_nsa = nsa_attention(q_nsa, k_cmp, v_cmp, cmp_end, k_slc, heads(vsl, NSA_GROUPS),
                          k_win, heads(vwn, NSA_GROUPS), gates)
    g = jax.nn.sigmoid(merge_logit.astype(jnp.float32)).reshape(B_, S_, N_BRANCH, D_MODEL).astype(h.dtype)
    ys = jnp.stack([y_fox, y_nsa], axis=2)
    up = jnp.einsum('bsnc,ncd->bsnd', ys, w_branch)
    merged = jnp.sum(g * up, axis=2)
    return merged @ w_out

def peer_ffn(h, wq, subkeys, u, v):
    B_, S_, D = h.shape
    T = B_ * S_
    hf = h.reshape(T, D)
    q = (hf @ wq).reshape(T, PEER_HEADS, 2, PEER_QDIM // 2)
    s = jnp.einsum('thpd,hpnd->thpn', q, subkeys).astype(jnp.float32)
    s1, i1 = lax.top_k(s[:, :, 0], PEER_TOPK)
    s2, i2 = lax.top_k(s[:, :, 1], PEER_TOPK)
    cand = (s1[..., :, None] + s2[..., None, :]).reshape(T, PEER_HEADS, PEER_TOPK * PEER_TOPK)
    cand_idx = (i1[..., :, None] * N_KEYS + i2[..., None, :]).reshape(T, PEER_HEADS, PEER_TOPK * PEER_TOPK)
    top_s, pos = lax.top_k(cand, PEER_TOPK)
    idx = jnp.take_along_axis(cand_idx, pos, axis=-1)
    w = jax.nn.softmax(top_s, axis=-1)

    def chunk(args):
        x_c, idx_c, w_c = args
        act = jax.nn.gelu(jnp.einsum('cd,chkd->chk', x_c, u[idx_c]).astype(jnp.float32), approximate=False)
        coef = (w_c * act).astype(v.dtype)
        return jnp.einsum('chk,chkd->cd', coef, v[idx_c])

    nc = T // PEER_CHUNK
    out = lax.map(chunk, (hf.reshape(nc, PEER_CHUNK, D),
                          idx.reshape(nc, PEER_CHUNK, PEER_HEADS, PEER_TOPK),
                          w.reshape(nc, PEER_CHUNK, PEER_HEADS, PEER_TOPK)))
    return out.reshape(B_, S_, D)

def second_inputs(seed: int = 0) -> dict:
    key = jax.random.key(seed)
    ks = jax.random.split(key, 16)
    f32 = jnp.float32
    nrm = lambda k, shape, scale: scale * jax.random.normal(k, shape, f32)
    L = DEPTH
    return {
        "x": jax.random.normal(ks[0], (BATCH, SEQ, D_MODEL), f32),
        "norm_mix": 1.0 + nrm(ks[1], (L, D_MODEL), 0.02),
        "w_in": nrm(ks[2], (L, D_MODEL, D_IN), D_MODEL ** -0.5),
        "fox_f_bias": FORGET_BIAS_INIT + nrm(ks[3], (L, FOX_HEADS), 0.1),
        "nsa_cmp_pos": nrm(ks[4], (L, 2, CMP_LEN, HEAD_DIM), 0.02),
        "nsa_cmp_w1": nrm(ks[5], (L, 2, CMP_LEN * HEAD_DIM, CMP_HIDDEN), (CMP_LEN * HEAD_DIM) ** -0.5),
        "nsa_cmp_w2": nrm(ks[6], (L, 2, CMP_HIDDEN, HEAD_DIM), CMP_HIDDEN ** -0.5),
        "w_branch": nrm(ks[7], (L, N_BRANCH, BRANCH_WIDTH, D_MODEL), BRANCH_WIDTH ** -0.5),
        "w_out": nrm(ks[8], (L, D_MODEL, D_MODEL), D_MODEL ** -0.5),
        "norm_ffn": 1.0 + nrm(ks[9], (L, D_MODEL), 0.02),
        "peer_wq": nrm(ks[10], (L, D_MODEL, PEER_HEADS * PEER_QDIM), D_MODEL ** -0.5),
        "peer_subkeys": nrm(ks[11], (L, PEER_HEADS, 2, N_KEYS, PEER_QDIM // 2), (PEER_QDIM // 2) ** -0.5),
        "peer_u": nrm(ks[12], (L, N_EXPERTS, D_MODEL), D_MODEL ** -0.5),
        "peer_v": nrm(ks[13], (L, N_EXPERTS, D_MODEL), (PEER_HEADS * PEER_TOPK) ** -0.5),
        "norm_final": 1.0 + nrm(ks[14], (D_MODEL,), 0.02),
    }

def second_block(x, norm_mix, w_in, fox_f_bias, nsa_cmp_pos, nsa_cmp_w1, nsa_cmp_w2, w_branch, w_out,
              norm_ffn, peer_wq, peer_subkeys, peer_u, peer_v, norm_final):
    h = x
    for l in range(DEPTH):
        h = h + hybrid_mixer(rmsnorm_2(h, norm_mix[l]), w_in[l], fox_f_bias[l], nsa_cmp_pos[l],
                             nsa_cmp_w1[l], nsa_cmp_w2[l], w_branch[l], w_out[l])
        h = h + peer_ffn(rmsnorm_2(h, norm_ffn[l]), peer_wq[l], peer_subkeys[l], peer_u[l], peer_v[l])
    return rmsnorm_2(h, norm_final)


def setup_inputs(seed=0):
    out = dict(first_inputs(seed))
    for name, value in second_inputs(seed + 1).items():
        if name != "x":
            out[name + "_2"] = value
    return out


def reference(
    x, mem, w_in, b_in, mlstm_norm, sconv_w, rel_bias, hgrn_lb_logits, hgrn_norm, w_mix_out,
    norm_mix_pre, norm_mix_post, mem_norm, w_cq, w_ck, w_cv, w_co, norm_cross_pre,
    norm_cross_post, w_ffn_in, ffn_conv_w, ffn_conv_b, w_ffn_out, norm_ffn_pre, norm_ffn_post,
    norm_mix_2, w_in_2, fox_f_bias_2, nsa_cmp_pos_2, nsa_cmp_w1_2, nsa_cmp_w2_2, w_branch_2,
    w_out_2, norm_ffn_2, peer_wq_2, peer_subkeys_2, peer_u_2, peer_v_2, norm_final_2,
):
    x = first_block(
        x, mem, w_in, b_in, mlstm_norm, sconv_w, rel_bias, hgrn_lb_logits, hgrn_norm, w_mix_out,
        norm_mix_pre, norm_mix_post, mem_norm, w_cq, w_ck, w_cv, w_co, norm_cross_pre,
        norm_cross_post, w_ffn_in, ffn_conv_w, ffn_conv_b, w_ffn_out, norm_ffn_pre,
        norm_ffn_post,
    )
    return second_block(
        x, norm_mix_2, w_in_2, fox_f_bias_2, nsa_cmp_pos_2, nsa_cmp_w1_2, nsa_cmp_w2_2,
        w_branch_2, w_out_2, norm_ffn_2, peer_wq_2, peer_subkeys_2, peer_u_2, peer_v_2,
        norm_final_2,
    )


_drawn_inputs = setup_inputs


def setup_inputs(seed=0):
    import zlib

    import numpy as np

    out = dict(_drawn_inputs(seed))
    spreads = {}
    factors = {'mlstm_norm': 3.443,
     'hgrn_norm': 3.324,
     'ffn_conv_b': 8.0,
     'norm_mix_2': 8.0,
     'fox_f_bias_2': 64.0,
     'nsa_cmp_pos_2': 8.0,
     'norm_ffn_2': 8.0,
     'peer_u_2': 2.932,
     'norm_final_2': 8.122}
    for name, (base, spread) in spreads.items():
        noise = np.random.default_rng([zlib.crc32(name.encode()), seed]).standard_normal(out[name].shape)
        drawn = base * np.exp(spread * noise) if base else spread * noise
        out[name] = jnp.asarray(drawn.astype(out[name].dtype))
    for name, factor in factors.items():
        out[name] = (out[name] * factor).astype(out[name].dtype)
    return out
```

```python
from contextlib import ExitStack

import numpy as np
import concourse.bass as bass
from concourse import mybir

P = 128
T = 256
NT = T // P
DM = 1024
KC = DM // P
SLOT = 2048
NR = 6
NB = 4
HD = 64
EPS = 1e-6
NEG = -1e30
DFF = 2816
FC = DFF // P
NCMP = 15
NKEY = 128
PH = 8
TOPK = 16
NE = NKEY * NKEY

F32 = mybir.dt.float32
U32 = mybir.dt.uint32
ALU = mybir.AluOpType
ACT = mybir.ActivationFunctionType
AX = mybir.AxisListType

GW = 256
O_MQ, O_MK, O_MV, O_MO = 0, GW, 2 * GW, 3 * GW
O_GI, O_GF = 4 * GW, 4 * GW + 4
O_C = 4 * GW + 8
O_CB, O_CC, O_CH, O_AQ, O_AK, O_AV, O_HQ, O_HF, O_HI, O_HG = (O_C + k * GW for k in range(10))
T1 = [("hf", O_HF), ("hq", O_HQ), ("mq", O_MQ), ("mk", O_MK), ("aq", O_AQ), ("ak", O_AK),
      ("cb", O_CB), ("cc", O_CC), ("ch", O_CH)]
R1 = [("mv", O_MV), ("hi", O_HI), ("av", O_AV), ("mo", O_MO), ("hg", O_HG)]
BW = 512
Q_FQ, Q_FK, Q_FV, Q_FL = 0, BW, 2 * BW, 3 * BW
Q_NQ = 3 * BW + 8
Q_KC, Q_VC, Q_KS, Q_VS, Q_KW, Q_VW = (Q_NQ + BW + k * 128 for k in range(6))
Q_GATE = Q_NQ + BW + 768
Q_MERGE = Q_GATE + 24

CONST = {}
_at = 0
for _name, _w in [("ident", 128), ("maskR", 2 * 256), ("maskT", 256), ("oh", 512), ("lvl", 8 * 128),
                  ("reset", 512), ("cosq", 256), ("sinq", 256), ("rot", 128), ("cosc", 30), ("sinc", 30),
                  ("iota", 128), ("iota16", 16), ("maskC", 2 * NCMP), ("valid", 2)]:
    CONST[_name] = (_at, _w)
    _at += _w
NCONST = _at

COLS = {}
_at = 0
for _name, _w in [("b1", 18), ("bi", 1), ("bf", 1), ("g_mix", 8), ("g_mem", 8), ("g_cross", 8), ("g_ffn", 8),
                  ("g_mix2", 8), ("g_ffn2", 8), ("sconv", 6), ("lb", 2), ("fconv", 66), ("fb", 22), ("foxb", 1), ("rel", 4), ("w2k", 128), ("w2v", 64), ("pos", 32)]:
    COLS[_name] = (_at, _w)
    _at += _w
NCOLS = _at


def slots():
    s = [("gate",)] + [("T1", i) for i in range(len(T1))] + [("R1", i) for i in range(len(R1))]
    s += [("ck", i) for i in range(2)] + [("cv", i) for i in range(2)]
    s += [("mix", i) for i in range(4)]
    s += [("cq", i) for i in range(2)] + [("co", i) for i in range(2)]
    s += [("up", i) for i in range(FC)] + [("down", i) for i in range(FC // 2)]
    s += [("flog",)] + [("fq", i) for i in range(2)] + [("fk", i) for i in range(2)] + [("nq", i) for i in range(2)]
    s += [("kk",), ("kc",), ("vc",)] + [("fv", i) for i in range(2)] + [("vv",), ("ngate",)]
    s += [("cw1", j) for j in range(2)]
    s += [("merge", i) for i in range(8)]
    s += [("branch", i) for i in range(4)] + [("wout", i) for i in range(4)]
    s += [("pq", i) for i in range(8)] + [("keys",)]
    return s


SLOTS = slots()
SLOT_AT = {k: n for n, k in enumerate(SLOTS)}


def att_units(kind):
    if kind == "moba":
        return [(kind, 0, [0, 1, 2, 3], 128), (kind, 1, [0, 1], 256), (kind, 1, [2, 3], 256)]
    if kind == "cross":
        return [(kind, t, [2 * i, 2 * i + 1], 256) for t in range(2) for i in range(2)]
    if kind == "cmp":
        return [(kind, t, list(range(4 * g, 4 * g + 4)), NCMP) for t in range(2) for g in range(2)]
    return [(kind, 0, list(range(4 * g, 4 * g + 4)), 128) for g in range(2)] + \
        [(kind, 1, [2 * i, 2 * i + 1], 256) for i in range(4)]


ATT1 = att_units("moba")
ATT2 = att_units("cross")
ATT3 = att_units("fox") + att_units("cmp") + att_units("slc") + att_units("win")
UNITS = ATT1 + ATT2 + ATT3
LV = 8
EVEN_ODD = {2: (0, 1), 4: (0, 2, 1, 3)}


def jobs():
    out = []
    n = {}

    def job(name, sem):
        n[sem] = n.get(sem, 0) + 1
        out.append((name, sem, n[sem]))

    def attention(units, u0):
        for i in range(len(units) + 2):
            if i < len(units):
                job(("score", u0 + i), "att_scaled")
            if 1 <= i <= len(units):
                job(("turn", u0 + i - 1), "att_turned")
            if i >= 2:
                job(("pv", u0 + i - 2), "att_out")

    def norm(k):
        for c in range(4):
            job(("xn", k, c), "xT_ready")

    norm(0)
    job(("gate",), "gates_copied")
    for i in range(len(T1)):
        job(("T1", i), "t1_copied")
    norm(1)
    for i in range(len(R1)):
        job(("R1", i), "r1_copied")
    for i in range(2):
        job(("ck", i), "ckv_copied")
    for i in range(2):
        job(("cv", i), "ckv_copied")
    job(("bias",), "relvec_copied")
    job(("mgT",), "mgT_copied")
    for u in range(3):
        job(("mD", u), "ml_arg")
        job(("mQK", u), "ml_w")
    for t in range(NT):
        job(("mO", t), "ml_h")
    for lv in range(LV):
        for t in range(NT):
            job(("hG", lv, t), "hg_kept")
    job(("hOff",), "hg_off")
    for t in range(NT):
        job(("hO", t), "hg_out")
    attention(ATT1, 0)
    for i in range(3):
        job(("yT", i), "yT_ready")
    norm(2)
    for i in range(2):
        job(("cq", i), "cq_copied")
    attention(ATT2, len(ATT1))
    job(("coT", 0), "coT_ready")
    job(("coT", 1), "coT_ready")
    norm(3)
    for f in range(FC):
        job(("up", f), "ffn_hidden")
    norm(4)
    job(("flog",), "flog_copied")
    for i in range(7):
        job(("T2", i), "t2_copied")
    job(("kc",), "t2_copied")
    job(("vc",), "t2_copied")
    for i in range(2):
        job(("fv", i), "r2_copied")
    job(("vv",), "r2_copied")
    job(("ngate",), "r2_copied")
    for i in range(3):
        job(("rope", i), "roped")
    for j in range(2):
        job(("chid", j), "chid_done")
    job(("ck2",), "ck2_done")
    job(("crot",), "crot_done")
    job(("cv2",), "cv2_done")
    for i in range(8):
        job(("merge", i), "merge_gated")
    attention(ATT3, len(ATT1) + len(ATT2))
    for i in range(4):
        job(("ysT", i), "ysT_ready")
    for i in range(4):
        job(("mT", i), "mT_ready")
    norm(5)
    for i in range(8):
        job(("pq", i), "pq_copied")
    for t in range(NT):
        for b in range(4):
            job(("ps", t, b), "ps_copied")
    for t in range(NT):
        job(("rT", t), "rT_copied")
    while len(out) % NB:
        job(("pad", len(out)), "pad_free")
    return out


JOBS = jobs()
JOB = {name: n for n, (name, _, _) in enumerate(JOBS)}


def build(nc, a):
    with ExitStack() as ctx:
        sems = {}

        def S(name):
            if name not in sems:
                sems[name] = ctx.enter_context(nc.semaphore(name))
            return sems[name]

        def sb(name, n):
            return ctx.enter_context(nc.sbuf_tensor("sb_" + name, [P, n], F32))

        x = sb("x", NT * DM)[:].rearrange("p (t d) -> p t d", t=NT)
        const = sb("const", NCONST)[:]
        cols = sb("cols", NCOLS)[:]
        small = sb("small", 160)[:]
        xT = sb("xT", KC * T)[:].rearrange("p (c t) -> p c t", c=KC)
        AREA = 44592
        area = sb("area", AREA)[:]
        ring = ctx.enter_context(nc.psum_tensor("ring", [P, NB, 512], F32))[:]
        acc = ctx.enter_context(nc.psum_tensor("acc", [P, NT, 2, 512], F32))[:]
        accf = acc.rearrange("p t n c -> p t (n c)")

        class Place:
            def __init__(self, at):
                self.at = at

            def take(self, n):
                self.at += n
                assert self.at <= AREA, self.at
                return area[:, self.at - n:self.at]

        def K(name, lo=0, n=None):
            at, w = CONST[name]
            return const[:, at + lo:at + (w if n is None else lo + n)]

        def C(name, lo=0, n=1):
            at, _ = COLS[name]
            return cols[:, at + lo:at + lo + n]

        ident = K("ident")

        pl = Place(0)
        wring = pl.take(NR * SLOT).rearrange("p (r n) -> p r n", r=NR)
        xn = pl.take(NT * DM).rearrange("p (t d) -> p t d", t=NT)
        tmp = pl.take(DM)
        gain = pl.take(DM)
        att = pl.take(3 * 1024)
        attS, attP, attT = (att[:, k * 1024:(k + 1) * 1024].rearrange("p (b n) -> p b n", b=2) for k in range(3))
        yT = pl.take(KC * T).rearrange("p (c t) -> p c t", c=KC)
        stage = pl.at
        memT = pl.take(KC * T).rearrange("p (c t) -> p c t", c=KC)
        t1 = pl.take(18 * T).rearrange("p (k t) -> p k t", k=18)
        TT = {name: t1[:, 2 * i:2 * i + 2, :] for i, (name, _) in enumerate(T1)}
        v1 = pl.take(NT * 4 * 65).rearrange("p (t h d) -> p t h d", t=NT, h=4)
        r1 = pl.take(4 * NT * GW).rearrange("p (k t n) -> p k t n", k=4, t=NT)
        RR = {"hi": r1[:, 0], "av": r1[:, 1], "mo": r1[:, 2], "hg": r1[:, 3]}
        rows1 = pl.take(7 * GW)
        relb = pl.take(4 * 384)
        rel0 = relb[:, 0:512].rearrange("p (h s) -> p h s", h=4)
        rel1 = relb[:, 512:1536].rearrange("p (h s) -> p h s", h=4)
        ckT = pl.take(4 * T).rearrange("p (k t) -> p k t", k=4)
        cv = pl.take(NT * 512).rearrange("p (t n) -> p t n", t=NT)
        ya = pl.take(NT * GW).rearrange("p (t n) -> p t n", t=NT)
        gi = pl.take(8 * T).rearrange("p (k t) -> p k t", k=8)
        ml = att[:, 0:5 * 512].rearrange("p (k n) -> p k n", k=5)
        EW, WT = ml[:, 0:2], ml[:, 2:5]
        hm = pl.take(NT * GW).rearrange("p (t n) -> p t n", t=NT)
        ho = pl.take(NT * GW).rearrange("p (t n) -> p t n", t=NT)
        hgD = pl.take(1024).rearrange("p (b n) -> p b n", b=2)
        hgX = pl.take(1024).rearrange("p (b n) -> p b n", b=2)
        hgA = pl.take(3 * 512).rearrange("p (k h t) -> p k h t", k=3, h=4)
        hk = pl.take(512)
        memr = area[:, pl.at - 2048:pl.at].rearrange("p (t d) -> p t d", t=NT)
        pad = pl.take(2 * 258).rearrange("p (k t) -> p k t", k=2)
        oc = hgD
        relv = gain[:, 0:512]
        sel4 = yT[:, 0:2, :].rearrange("p a b -> p (a b)").rearrange("p (h t) -> p h t", h=4)
        pl = Place(stage)
        hid = pl.take(FC * T).rearrange("p (k t) -> p k t", k=FC)
        gpad = pl.take(2 * 258).rearrange("p (k t) -> p k t", k=2)
        fa = pl.take(2 * T).rearrange("p (k t) -> p k t", k=2)
        pl = Place(stage)
        t2 = pl.take(14 * T).rearrange("p (k t) -> p k t", k=14)
        fqT, fkT, nqT, kkT = t2[:, 0:4], t2[:, 4:8], t2[:, 8:12], t2[:, 12:14]
        kc2 = pl.take(4 * T).rearrange("p (j g t) -> p j g t", j=2, g=2)
        fv = pl.take(NT * 512).rearrange("p (t n) -> p t n", t=NT)
        vv = pl.take(NT * 256).rearrange("p (t n) -> p t n", t=NT)
        ng = pl.take(NT * 24).rearrange("p (t n) -> p t n", t=NT)
        rt = pl.take(2 * 512).rearrange("p (b n) -> p b n", b=2)
        cb = pl.take(6 * T).rearrange("p (k t) -> p k t", k=6)
        sel8 = pl.take(8 * T).rearrange("p (h t) -> p h t", h=8)
        chid = pl.take(64).rearrange("p (j n) -> p j n", j=2)
        ckc = pl.take(96).rearrange("p (k n) -> p k n", k=3)
        cvr = pl.take(128).rearrange("p (g d) -> p g d", g=2)
        ofox = pl.take(NT * 512).rearrange("p (t n) -> p t n", t=NT)
        onsa = pl.take(NT * 512).rearrange("p (t n) -> p t n", t=NT)
        ott = pl.take(512)
        mg = pl.take(NT * 2 * DM).rearrange("p (t b n) -> p t b n", t=NT, b=2)
        pl = Place(stage)
        pqT = pl.take(16 * T).rearrange("p (k t) -> p k t", k=16)
        ps = pl.take(NT * 16 * NKEY).rearrange("p (t k n) -> p t k n", t=NT, k=16)
        pw = pl.take(NKEY)
        top = pl.take(16 * TOPK).rearrange("p (k n) -> p k n", k=16)
        topi = pl.take(16 * TOPK).rearrange("p (k n) -> p k n", k=16)
        best = pl.take(PH * TOPK).rearrange("p (h n) -> p h n", h=PH)
        besti = pl.take(PH * TOPK).rearrange("p (h n) -> p h n", h=PH)
        part = pl.take(2 * PH * TOPK).rearrange("p (k h n) -> p k h n", k=2, h=PH)
        pick = pl.take(PH * TOPK * TOPK).rearrange("p (h k j) -> p h k j", h=PH, k=TOPK)
        cand = pick.rearrange("p h k j -> p h (k j)")
        rout = pl.take(3 * PH * TOPK).rearrange("p (k n) -> p k n", k=3)
        pl = Place(0)
        table = pl.take(T * NKEY).rearrange("p (t j) -> p t j", t=T)
        EU = 4
        uring = pl.take(EU * DM).rearrange("p (r c i) -> p r c i", r=EU, c=KC)
        vring = pl.take(EU * DM).rearrange("p (r d) -> p r d", r=EU)
        coef = pl.take(2 * T).rearrange("p (r t) -> p r t", r=2)
        rT = pl.take(3 * T).rearrange("p (k t) -> p k t", k=3)
        zrow = coef[:, 0:2, :].rearrange("p r t -> p (r t)")
        hot = pl.take(2 * 2 * 4 * NKEY).rearrange("p (b s q n) -> p b s q n", b=2, s=2, q=4)

        hm3 = hm.rearrange("p t (h d) -> p t h d", h=4)
        relvec = nc.dram_tensor("relvec", [4, P, 512], F32).ap()
        ss, ms, rms, rstd = small[:, 0:4], small[:, 4:6], small[:, 6:8], small[:, 8:10]
        lbw = small[:, 10:18]
        hnm, hnr = small[:, 18:26], small[:, 26:34]
        amx = small[:, 36:68].rearrange("p (b n) -> p b n", b=4)
        asum = small[:, 68:100].rearrange("p (b n) -> p b n", b=4)
        ars = small[:, 100:108]
        rc = small[:, 108:124].rearrange("p (q t h) -> p q t h", q=2, t=2)
        den = small[:, 124:132]
        cbias = small[:, 132:134]
        wsum, wrec, wneg = small[:, 134:142], small[:, 142:150], small[:, 150:158]
        zero = small[0:1, 158:159]

        bank_ready = [S(f"bank{b}_ready") for b in range(NB)]

        def got(eng, name):
            n = JOB[name]
            eng.wait_ge(bank_ready[n % NB], n // NB + 1)
            return ring[:, n % NB, :]

        def stepper(eng, chain):
            counts = {}

            def link(ins, name=chain):
                counts[name] = counts.get(name, 0) + 1
                ins.then_inc(S(name), 1)
                eng.wait_ge(S(name), counts[name])
            return link

        block = ctx.enter_context(nc.Block())
        nslots = len(SLOTS)

        @block.sync
        def _(sp):
            sp.dma_start(x, a["x"].rearrange("o (t p) d -> p (o t) d", p=P)).then_inc(S("ld_x"), 16)
            sp.dma_start(const, a["consts"]).then_inc(S("ld_const"), 16)
            sp.dma_start(cols, a["cols"]).then_inc(S("ld_cols"), 16)
            for n in range(min(NR, nslots)):
                sp.dma_start(wring[:, n, :], a["wstream"][n]).then_inc(S(f"w{n}"), 16)
            rounds = (nslots - NR) // NR
            if rounds > 0:
                with sp.Fori(0, rounds) as i:
                    for b in range(NR):
                        sp.wait_ge(S("slot_free"), NR * i + b + 1)
                        sp.dma_start(wring[:, b, :], a["wstream"][NR * i + NR + b]).then_inc(S(f"w{b}"), 16)
            for n in range(NR + max(rounds, 0) * NR, nslots):
                sp.wait_ge(S("slot_free"), n - NR + 1)
                sp.dma_start(wring[:, n % NR, :], a["wstream"][n]).then_inc(S(f"w{n % NR}"), 16)
            sp.wait_ge(S("rT_copied"), 2)
            for b in range(EU):
                sp.dma_start(uring[:, b], a["u"][b].rearrange("p (c i) -> p c i", c=KC)).then_inc(S(f"u{b}"), 16)
                sp.dma_start(vring[:, b], a["v"][b]).then_inc(S(f"v{b}"), 16)
            with sp.Fori(0, NKEY // EU - 1) as i:
                for b in range(EU):
                    sp.wait_ge(S("ex_used"), EU * i + b + 3)
                    sp.dma_start(uring[:, b], a["u"][EU * i + EU + b].rearrange("p (c i) -> p c i", c=KC)
                                 ).then_inc(S(f"u{b}"), 16)
                    sp.dma_start(vring[:, b], a["v"][EU * i + EU + b]).then_inc(S(f"v{b}"), 16)
            sp.wait_ge(S("out_rows"), 1)
            sp.dma_start(a["out"].rearrange("o (t p) d -> p (o t) d", p=P), x).then_inc(S("stored"), 16)
            sp.wait_ge(S("stored"), 16)

        @block.gpsimd
        def _(pool):
            pool.dma_start(memr, a["mem"].rearrange("o (t p) d -> p (o t) d", p=P)).then_inc(S("ld_mem"), 16)
            pool.dma_start(rows1, bass.AP(a["rows1"].tensor, 0, [[0, P], [1, 7 * GW]])).then_inc(S("ld_rows1"), 16)

            def load_gain(k):
                pool.dma_start(gain, bass.AP(a["gains"].tensor, k * DM, [[0, P], [1, DM]])).then_inc(S("ld_gain"), 16)
            pool.wait_ge(S("relvec_copied"), 1)
            pool.dma_start(relvec, relv[0:4, :].unsqueeze(1).to_broadcast([4, P, 512])).then_inc(S("relvec_out"), 16)
            pool.wait_ge(S("relvec_out"), 16)
            for h in range(4):
                for tt, tile_, n in ((0, rel0, 128), (1, rel1, 256)):
                    pool.dma_start(tile_[:, h, :], bass.AP(relvec.tensor, h * P * 512 + 255 - tt * P, [[511, P], [1, n]])
                                   ).then_inc(S("ld_rel"), 16)
            pool.wait_ge(S("ld_rel"), 16 * 8)
            load_gain(0)
            pool.wait_ge(S("resid"), 1)
            load_gain(1)
            pool.wait_ge(S("resid"), 2)
            load_gain(2)
            pool.wait_ge(S("ld_rel"), 16 * 8)
            pool.wait_ge(S("resid"), 5)
            pool.dma_start(area[:, 0:DM], bass.AP(a["gains"].tensor, 3 * DM, [[0, P], [1, DM]])
                           ).then_inc(S("ld_gain"), 16)
            pool.wait_ge(S("ld_gain"), 64)

        @block.tensor
        def _(pe):
            mm = nc.tensor.matmul

            def bank(name):
                n = JOB[name]
                if n >= NB:
                    _, sem, value = JOBS[n - NB]
                    pe.wait_ge(S(sem), value)
                return ring[:, n % NB, :]

            def done(ins, name):
                ins.then_inc(bank_ready[JOB[name] % NB], 1)

            fences = [0]

            def fence(ins):
                fences[0] += 1
                ins.then_inc(S("pe_fence"), 1)
                pe.wait_ge(S("pe_fence"), fences[0])

            def slot(key):
                n = SLOT_AT[key]
                pe.wait_ge(S(f"w{n % NR}"), 16 * (n // NR + 1))
                return wring[:, n % NR, :]

            def next_slot(ins, key):
                if SLOT_AT[key] > 0:
                    ins.then_inc(S("slot_free"), 1)

            def norm_T(k):
                pe.wait_ge(S("xn_ready"), k + 1)
                for c in range(4):
                    b = bank(("xn", k, c)).rearrange("p (c t) -> p c t", c=2)
                    for ci in range(2):
                        for t in range(NT):
                            ins = nc.tensor.transpose(b[:, ci, t * P:(t + 1) * P],
                                                      xn[:, t, (2 * c + ci) * P:(2 * c + ci + 1) * P], ident)
                    done(ins, ("xn", k, c))

            def proj_T(name, key, src, n=256):
                w = slot(key)[:, 0:KC * n].rearrange("p (c n) -> p c n", c=KC)
                b = bank(name).rearrange("p (k t) -> p k t", k=2)
                m = min(n // 2, P)
                for k in range(2):
                    for c in range(KC):
                        ins = mm(b[0:m, k, :], w[:, c, k * m:(k + 1) * m], src[:, c, :], start=c == 0, stop=c == KC - 1)
                        if k == 0 and c == 0:
                            next_slot(ins, key)
                done(ins, name)

            def proj_R(name, key, src, n=256):
                w = slot(key)[:, 0:KC * n].rearrange("p (c n) -> p c n", c=KC)
                b = bank(name).rearrange("p (t n) -> p t n", t=2)
                for t in range(NT):
                    for c in range(KC):
                        ins = mm(b[:, t, 0:n], src[:, c, t * P:(t + 1) * P], w[:, c, :], start=c == 0, stop=c == KC - 1)
                        if t == 0 and c == 0:
                            next_slot(ins, key)
                done(ins, name)

            def proj_acc(use, keys, src, wait_free=True):
                if use > 1:
                    pe.wait_ge(S("acc_free"), use - 1)
                last = 2 * len(keys) - 1
                for i, key in enumerate(keys):
                    w = slot(key).rearrange("p (k n) -> p k n", k=2)
                    for k in range(2):
                        c = 2 * i + k
                        for t in range(NT):
                            for n in range(2):
                                ins = mm(acc[:, t, n, :], src[:, c, t * P:(t + 1) * P], w[:, k, n * 512:(n + 1) * 512],
                                         start=c == 0, stop=c == last)
                                if k == 0 and t == 0 and n == 0:
                                    next_slot(ins, key)
                ins.then_inc(S("acc_ready"), 1)

            def rows_to_T(name, src, c0, n=2):
                b = bank(name).rearrange("p (c t) -> p c t", c=2)
                for ci in range(n):
                    for t in range(NT):
                        ins = nc.tensor.transpose(b[:, ci, t * P:(t + 1) * P],
                                                  src[:, t, (c0 + ci) * P:(c0 + ci + 1) * P], ident)
                done(ins, name)

            def score(u):
                kind, t, heads, n = UNITS[u]
                b = bank(("score", u))
                tok = slice(t * P, (t + 1) * P)
                for i in EVEN_ODD[len(heads)]:
                    h = heads[i]
                    if i == 1 and kind in ("moba", "fox"):
                        fence(ins)
                    o = b[:, i * n:(i + 1) * n]
                    r = slice((h % 2) * HD, (h % 2) * HD + HD)
                    if kind == "moba":
                        ins = mm(o, TT["aq"][r, h // 2, tok], TT["ak"][r, h // 2, 0:n], start=True, stop=True)
                    elif kind == "cross":
                        ins = mm(o, memT[:, h, tok], ckT[:, h, :], start=True, stop=True)
                    elif kind == "fox":
                        mm(o, fqT[r, h // 2, tok], fkT[r, h // 2, 0:n], start=True, stop=False)
                        e = slice((h % 2) * HD, (h % 2) * HD + 8)
                        mm(o, cb[e, 4, tok], sel8[e, h, 0:n], start=False, stop=False)
                        ins = mm(o, sel8[e, h, 0:P], cb[e, 5, 0:n], start=False, stop=True)
                    else:
                        g, hp = h // 4, h % 4
                        r = slice(g * HD, g * HD + HD)
                        if kind == "cmp":
                            k = ckc[r, 2, g * NCMP:(g + 1) * NCMP]
                        else:
                            k = kkT[r, 0 if kind == "slc" else 1, 0:n]
                        ins = mm(o, nqT[r, hp, tok], k, start=True, stop=True)
                done(ins, ("score", u))

            def turn(u):
                kind, t, heads, n = UNITS[u]
                b = bank(("turn", u))
                pe.wait_ge(S("att_exp"), u + 1)
                k = min(n, P)
                for i in range(len(heads) * n // k):
                    ins = nc.tensor.transpose(b[0:k, i * P:(i + 1) * P], attP[:, u % 2, i * k:(i + 1) * k], ident)
                done(ins, ("turn", u))

            def pv(u):
                kind, t, heads, n = UNITS[u]
                b = bank(("pv", u))
                pe.wait_ge(S("att_turned"), u + 1)
                k = min(n, P)
                nk = n // k
                d = P if kind == "cross" else HD
                for i, h in enumerate(heads):
                    for j in range(nk):
                        if kind == "moba":
                            v = RR["av"][:, j, h * HD:(h + 1) * HD]
                        elif kind == "cross":
                            v = cv[:, j, h * P:(h + 1) * P]
                        elif kind == "fox":
                            v = fv[:, j, h * HD:(h + 1) * HD]
                        elif kind == "cmp":
                            v = cvr[0:NCMP, h // 4, :]
                        else:
                            at = (0 if kind == "slc" else P) + (h // 4) * HD
                            v = vv[:, j, at:at + HD]
                        ins = mm(b[:, i * d:(i + 1) * d], attT[0:k, u % 2, (i * nk + j) * P:(i * nk + j + 1) * P], v,
                                 start=j == 0, stop=j == nk - 1)
                done(ins, ("pv", u))

            def attention(units, u0):
                for i in range(len(units) + 2):
                    if i < len(units):
                        score(u0 + i)
                    if 1 <= i <= len(units):
                        turn(u0 + i - 1)
                    if i >= 2:
                        pv(u0 + i - 2)

            pe.wait_ge(S("ld_const"), 16)
            norm_T(0)
            pe.wait_ge(S("xT_ready"), 4)
            w = slot(("gate",))[:, 0:64].rearrange("p (c n) -> p c n", c=KC)
            b = bank(("gate",)).rearrange("p (k t) -> p k t", k=2)
            for k in range(2):
                for c in range(KC):
                    ins = mm(b[0:4, k, :], w[:, c, 4 * k:4 * k + 4], xT[:, c, :], start=c == 0, stop=c == KC - 1)
            done(ins, ("gate",))
            for i in range(len(T1)):
                proj_T(("T1", i), ("T1", i), xT)
            norm_T(1)
            for i in range(len(R1)):
                proj_R(("R1", i), ("R1", i), xT)
            pe.wait_ge(S("xT_ready"), 8)
            for i in range(2):
                proj_T(("ck", i), ("ck", i), memT)
            for i in range(2):
                proj_R(("cv", i), ("cv", i), memT)

            pe.wait_ge(S("rel_ready"), 1)
            done(mm(bank(("bias",))[0:4, :], C("rel", 0, 4)[0:33], K("oh")[0:33], start=True, stop=True), ("bias",))
            pe.wait_ge(S("ml_rows"), 1)
            pe.wait_ge(S("ml_em"), 1)
            b = bank(("mgT",))
            for q in range(2):
                for t in range(NT):
                    i = 2 * q + t
                    ins = nc.tensor.transpose(b[:, 4 * i:4 * i + 4], gi[0:4, 2 + q, t * P:(t + 1) * P], ident[0:4, 0:4])
            done(ins, ("mgT",))
            ML = [(0, [0, 1], slice(0, T)), (0, [2, 3], slice(0, T)), (1, [0, 1, 2, 3], slice(P, T))]
            pe.wait_ge(S("sel_ready"), 1)
            for u, (s, heads, tok) in enumerate(ML):
                n = tok.stop - tok.start
                b = bank(("mD", u))
                for i, h in enumerate(heads):
                    ins = mm(b[:, i * n:(i + 1) * n], sel4[0:4, h, :], gi[0:4, 6, tok], start=True, stop=True)
                done(ins, ("mD", u))
                b = bank(("mQK", u))
                for i in EVEN_ODD[len(heads)]:
                    h = heads[i]
                    if i == 1:
                        fence(ins)
                    r = slice((h % 2) * HD, (h % 2) * HD + HD)
                    ins = mm(b[:, i * n:(i + 1) * n], TT["mk"][r, h // 2, s * P:(s + 1) * P], TT["mq"][r, h // 2, tok],
                             start=True, stop=True)
                done(ins, ("mQK", u))
            pe.wait_ge(S("ml_w"), 3)
            pe.wait_ge(S("r1_copied"), 1)
            for t in range(NT):
                b = bank(("mO", t))
                for h in range(4):
                    o = b[:, h * 65:(h + 1) * 65]
                    w0 = WT[:, h // 2, (h % 2) * T + t * P:(h % 2) * T + (t + 1) * P]
                    ins = mm(o, w0, v1[:, 0, h, :], start=True, stop=t == 0)
                    if t:
                        ins = mm(o, WT[:, 2, h * P:(h + 1) * P], v1[:, 1, h, :], start=False, stop=True)
                done(ins, ("mO", t))
            for lv in range(LV):
                pe.wait_ge(S("hg_x"), lv + 1)
                for t in range(NT):
                    b = bank(("hG", lv, t))
                    for h in EVEN_ODD[4]:
                        if h == 1:
                            fence(ins)
                        r = slice((h % 2) * HD, (h % 2) * HD + HD)
                        at = (h // 2) * T + t * P
                        if lv == 0:
                            ks, qs = hk[r, at:at + P], TT["hq"][r, h // 2, t * P:(t + 1) * P]
                        else:
                            ks = qs = hgX[r, lv % 2, at:at + P]
                        ins = mm(b[:, h * P:(h + 1) * P], ks, qs, start=True, stop=True)
                    done(ins, ("hG", lv, t))
            pe.wait_ge(S("hg_x"), LV + 1)
            b = bank(("hOff",))
            for h in EVEN_ODD[4]:
                if h == 1:
                    fence(ins)
                r = slice((h % 2) * HD, (h % 2) * HD + HD)
                at = (h // 2) * T
                ins = mm(b[:, h * P:(h + 1) * P], hgX[r, LV % 2, at:at + P], hgX[r, LV % 2, at + P:at + T],
                         start=True, stop=True)
            done(ins, ("hOff",))
            pe.wait_ge(S("hg_off"), 1)
            for t in range(NT):
                b = bank(("hO", t))
                for h in range(4):
                    o = b[:, h * HD:(h + 1) * HD]
                    ins = mm(o, hgA[:, t, h, :], RR["hi"][:, t, h * HD:(h + 1) * HD], start=True, stop=t == 0)
                    if t:
                        ins = mm(o, hgA[:, 2, h, :], RR["hi"][:, 0, h * HD:(h + 1) * HD], start=False, stop=True)
                done(ins, ("hO", t))
            attention(ATT1, 0)
            for i, (src, sem, v) in enumerate(((hm, "hn_done", 1), (ya, "att_out", len(ATT1)), (ho, "hn_done", 2))):
                pe.wait_ge(S(sem), v)
                rows_to_T(("yT", i), src, 0)
            pe.wait_ge(S("yT_ready"), 3)
            pe.wait_ge(S("conv_done"), 1)
            proj_acc(1, [("mix", i) for i in range(4)], yT)
            norm_T(2)
            pe.wait_ge(S("xT_ready"), 12)
            for i in range(2):
                proj_T(("cq", i), ("cq", i), xT)
            pe.wait_ge(S("cq_copied"), 2)
            attention(ATT2, len(ATT1))
            pe.wait_ge(S("att_out"), len(ATT1) + len(ATT2))
            rows_to_T(("coT", 0), oc, 0)
            rows_to_T(("coT", 1), oc, 2)
            pe.wait_ge(S("coT_ready"), 2)
            proj_acc(2, [("co", i) for i in range(2)], memT[:, 4:8])
            norm_T(3)
            pe.wait_ge(S("xT_ready"), 16)
            for f in range(FC):
                proj_T(("up", f), ("up", f), xT)
            pe.wait_ge(S("ffn_hidden"), FC)
            proj_acc(3, [("down", i) for i in range(FC // 2)], hid)
            norm_T(4)
            pe.wait_ge(S("xT_ready"), 20)
            w = slot(("flog",))[:, 0:64].rearrange("p (c n) -> p c n", c=KC)
            b = bank(("flog",))
            for c in range(KC):
                ins = mm(b[0:8, 0:T], w[:, c, :], xT[:, c, :], start=c == 0, stop=c == KC - 1)
                if c == 0:
                    next_slot(ins, ("flog",))
            done(ins, ("flog",))
            T2 = [("fq", 0), ("fq", 1), ("fk", 0), ("fk", 1), ("nq", 0), ("nq", 1), ("kk",)]
            for i, key in enumerate(T2):
                proj_T(("T2", i), key, xT)
            proj_T(("kc",), ("kc",), xT)
            proj_T(("vc",), ("vc",), xT)
            for i in range(2):
                proj_R(("fv", i), ("fv", i), xT)
            proj_R(("vv",), ("vv",), xT)
            proj_R(("ngate",), ("ngate",), xT, 24)
            pe.wait_ge(S("t2_copied"), 9)
            for i in range(3):
                b = bank(("rope", i)).rearrange("p (k t) -> p k t", k=2)
                for k in range(2):
                    ins = mm(b[:, k, :], K("rot"), t2[:, 8 + 2 * i + k, :], start=True, stop=True)
                done(ins, ("rope", i))
            for j in range(2):
                w = slot(("cw1", j)).rearrange("p (l n) -> p l n", l=16)
                b = bank(("chid", j))
                for lp in range(16):
                    ins = mm(b[:, 32:33], w[:, lp, :], C("pos", 16 * j + lp), start=lp == 0, stop=lp == 15)
                    if lp == 0:
                        next_slot(ins, ("cw1", j))
                for lp in range(16):
                    ins = mm(b[:, 0:2 * NCMP].rearrange("p (g n) -> p g n", g=2), w[:, lp, :],
                             kc2[:, j, :, 2 * lp:2 * lp + 16 * (NCMP - 1) + 1:16], start=lp == 0, stop=lp == 15)
                done(ins, ("chid", j))
            pe.wait_ge(S("chid_done"), 2)
            done(mm(bank(("ck2",))[:, 0:30], C("w2k", 0, 128), chid[:, 0, 0:30], start=True, stop=True), ("ck2",))
            pe.wait_ge(S("ck2_done"), 1)
            done(mm(bank(("crot",))[:, 0:30], K("rot"), ckc[:, 0, 0:30], start=True, stop=True), ("crot",))
            b = bank(("cv2",))
            for g in range(2):
                ins = mm(b[0:NCMP, g * HD:(g + 1) * HD], chid[:, 1, g * NCMP:(g + 1) * NCMP], C("w2v", 0, 64),
                         start=True, stop=True)
            done(ins, ("cv2",))
            for i in range(8):
                proj_R(("merge", i), ("merge", i), xT)
            pe.wait_ge(S("roped_all"), 1)
            pe.wait_ge(S("fox_rows"), 1)
            pe.wait_ge(S("r2_copied"), 4)
            pe.wait_ge(S("cv2_done"), 1)
            pe.wait_ge(S("cmpk_ready"), 1)
            attention(ATT3, len(ATT1) + len(ATT2))
            pe.wait_ge(S("att_out"), len(UNITS))
            for i in range(4):
                rows_to_T(("ysT", i), ofox if i < 2 else onsa, 2 * (i % 2))
            pe.wait_ge(S("ysT_ready"), 4)
            proj_acc(4, [("branch", i) for i in range(2)], yT)
            proj_acc(5, [("branch", i) for i in range(2, 4)], yT[:, 4:8])
            pe.wait_ge(S("merged"), 1)
            for i in range(4):
                rows_to_T(("mT", i), mg[:, :, 0, :], 2 * i)
            pe.wait_ge(S("mT_ready"), 4)
            proj_acc(6, [("wout", i) for i in range(4)], yT)
            norm_T(5)
            pe.wait_ge(S("xT_ready"), 24)
            for i in range(8):
                proj_T(("pq", i), ("pq", i), xT)
            pe.wait_ge(S("pq_copied"), 8)
            w = slot(("keys",)).rearrange("p (k n) -> p k n", k=16)
            for t in range(NT):
                for q in range(4):
                    b = bank(("ps", t, q))
                    for k in range(4):
                        ins = mm(b[:, k * P:(k + 1) * P], pqT[:, 4 * q + k, t * P:(t + 1) * P], w[:, 4 * q + k, :],
                                 start=True, stop=True)
                    done(ins, ("ps", t, q))
            for t in range(NT):
                b = bank(("rT", t))
                pe.wait_ge(S("routes"), t + 1)
                for k in range(3):
                    ins = nc.tensor.transpose(b[:, k * P:(k + 1) * P], rout[:, k, :], ident)
                done(ins, ("rT", t))
            n0 = len(JOBS)
            pe.wait_ge(S("rT_copied"), 2)
            for q in range(NB):
                _, sem, value = JOBS[n0 - NB + q]
                if sem != "pad_free":
                    pe.wait_ge(S(sem), value)
            pe.nop().then_inc(S("hot_used"), 2)
            with pe.Fori(0, T // (4 * NB)) as i:
                for q in range(NB):
                    pe.wait_ge(S("hot_ready"), NB * i + q + 1)
                    pe.wait_ge(S("tabled"), NB * i + q - NB + 5)
                    for k in range(4):
                        ins = mm(ring[:, q, k * NKEY:(k + 1) * NKEY], hot[:, q % 2, 0, k, :], hot[:, q % 2, 1, k, :],
                                 start=True, stop=True)
                    ins.then_inc(S("hot_used"), 1)
            pe.wait_ge(S("acc_free"), 6)
            pe.wait_ge(S("zrow_ready"), 1)
            for t in range(NT):
                for n in range(2):
                    mm(acc[:, t, n, :], zrow[0:1, 0:P], zrow[0:1, 0:512], start=True, stop=False)
            pe.wait_ge(S("tabled"), T // 4 + 4)

            def hidden(e, b):
                pe.wait_ge(S(f"u{b}"), e)
                for c in range(KC):
                    ins = mm(ring[:, b, 0:T], uring[:, b, c, :], xT[:, c, :], start=c == 0, stop=c == KC - 1)
                ins.then_inc(S("ex_hidden"), 1)

            def spread(b, e, used, stop=False):
                pe.wait_ge(S(f"v{b}"), e)
                pe.wait_ge(S("ex_coef"), used)
                for t in range(NT):
                    for n in range(2):
                        ins = mm(acc[:, t, n, :], coef[:, b % 2, t * P:(t + 1) * P], vring[:, b, n * 512:(n + 1) * 512],
                                 start=False, stop=stop)
                ins.then_inc(S("acc_ready" if stop else "ex_used"), 1)

            pe.nop().then_inc(S("ex_used"), 2)
            hidden(16, 0)
            with pe.Fori(0, NKEY // EU - 1) as i:
                for b in range(EU):
                    hidden(16 * i + (16 if b < EU - 1 else 32), (b + 1) % EU)
                    spread(b, 16 * i + 16, EU * i + b + 1)
            last = NKEY // EU - 1
            for b in range(EU):
                if b < EU - 1:
                    hidden(16 * last + 16, b + 1)
                spread(b, 16 * last + 16, EU * last + b + 1, stop=b == EU - 1)

        @block.scalar
        def _(act):
            link = stepper(act, "act_step")
            A = nc.scalar.activation

            def squares(src, lo):
                for t in range(NT):
                    link(A(tmp, src[:, t, :], ACT.Square, accum_out=ss[:, lo + t:lo + t + 1]),
                         "sumsq" if t == NT - 1 else "act_step")

            def root(k):
                act.wait_ge(S("meansq"), k)
                link(A(rms, ms, ACT.Sqrt), "rms")

            def norm_T(k, dst, g):
                for c in range(4):
                    b = got(act, ("xn", k, c)).rearrange("p (c t) -> p c t", c=2)
                    A(dst[:, 2 * c, :], b[:, 0, :], ACT.Copy, scale=C(g, 2 * c))
                    link(A(dst[:, 2 * c + 1, :], b[:, 1, :], ACT.Copy, scale=C(g, 2 * c + 1)), "xT_ready")

            def acc_squares(use):
                act.wait_ge(S("acc_ready"), use)
                for t in range(NT):
                    for n in range(2):
                        link(A(tmp[:, 0:512], acc[:, t, n, :], ACT.Square, accum_out=ss[:, 2 * t + n:2 * t + n + 1]),
                             "sumsq" if (t, n) == (1, 1) else "act_step")

            def copy_job(name, dst, sem, func=ACT.Copy):
                b = got(act, name)
                link(A(dst, b[:, 0:dst.free_size()] if dst.ndim == 2 else
                       b.rearrange("p (k t) -> p k t", k=2)[:, :, 0:dst.shape[2]], func), sem)

            def attention(units, u0):
                for i in range(len(units) + 1):
                    if i < len(units):
                        u = u0 + i
                        kind, t, heads, n = UNITS[u]
                        act.wait_ge(S("att_max"), u + 1)
                        for k in range(len(heads)):
                            ins = A(attP[:, u % 2, k * n:(k + 1) * n], attS[:, u % 2, k * n:(k + 1) * n], ACT.Exp,
                                    bias=amx[:, u % 4, k:k + 1], accum_out=asum[:, u % 4, k:k + 1])
                        link(ins, "att_exp")
                    if i >= 1:
                        u = u0 + i - 1
                        kind, t, heads, n = UNITS[u]
                        b = got(act, ("turn", u))
                        k = min(n, P)
                        m = len(heads) * n // k * P
                        if u >= 2:
                            got(act, ("pv", u - 2))
                        link(A(attT[0:k, u % 2, 0:m], b[0:k, 0:m], ACT.Copy), "att_turned")

            act.wait_ge(S("ld_x"), 16)
            squares(x, 0)
            act.wait_ge(S("ld_mem"), 16)
            squares(memr, 2)
            root(1)
            root(2)
            act.wait_ge(S("ld_cols"), 16)
            norm_T(0, xT, "g_mix")
            b = got(act, ("gate",)).rearrange("p (k t) -> p k t", k=2)
            link(A(gi[0:4, 0, :], b[0:4, 0, :], ACT.Identity, bias=C("bi")[0:4]))
            link(A(gi[0:4, 1, :], b[0:4, 1, :], ACT.Identity, bias=C("bf")[0:4]), "gates_copied")
            link(A(gi[0:4, 2, :], gi[0:4, 1, :], ACT.Abs))
            link(A(gi[0:4, 2, :], gi[0:4, 2, :], ACT.Exp, scale=-1.0))
            link(A(gi[0:4, 2, :], gi[0:4, 2, :], ACT.Ln, bias=1.0), "ml_ln")
            for i, (name, _) in enumerate(T1):
                b = got(act, ("T1", i)).rearrange("p (k t) -> p k t", k=2)
                func = {"hf": ACT.Sigmoid, "hq": ACT.Silu}.get(name, ACT.Identity)
                A(TT[name][:, 0, :], b[:, 0, :], func, bias=C("b1", 2 * i))
                link(A(TT[name][:, 1, :], b[:, 1, :], func, bias=C("b1", 2 * i + 1)), "t1_copied")
            norm_T(1, memT, "g_mem")
            act.wait_ge(S("lb_shift"), 1)
            link(A(lbw[:, 2:4], lbw[:, 0:2], ACT.Exp), "lb_exp")
            act.wait_ge(S("hg_f"), 1)
            link(A(hgX[:, 1, :], hgX[:, 0, :], ACT.Ln), "hg_ln")
            act.wait_ge(S("ml_rows"), 1)
            link(A(gi[0:4, 3, :], gi[0:4, 7, :], ACT.Exp, scale=-1.0), "ml_em")
            for i in range(2):
                copy_job(("ck", i), ckT[:, 2 * i:2 * i + 2, :], "ckv_copied")
            for i in range(2):
                copy_job(("cv", i), cv[:, :, 256 * i:256 * i + 256], "ckv_copied")
            link(A(relv[0:4, :], got(act, ("bias",))[0:4, :], ACT.Copy), "relvec_copied")
            act.wait_ge(S("r1_copied"), 5)
            link(A(RR["mo"], RR["mo"], ACT.Sigmoid))
            link(A(RR["hg"], RR["hg"], ACT.Silu), "gates_ready")
            for u in range(3):
                act.wait_ge(S("ml_arg"), u + 1)
                link(A(EW[:, u % 2, :], EW[:, u % 2, :], ACT.Exp), "ml_exp")
            for lv in range(1, LV + 1):
                act.wait_ge(S("hg_d"), lv)
                link(A(hgD[:, lv % 2, :], hgD[:, lv % 2, :], ACT.Exp), "hg_e")
            for k in range(2):
                act.wait_ge(S("hn_ms"), k + 1)
                link(A(hnr, hnm, ACT.Sqrt), "hn_rt")
            attention(ATT1, 0)
            for i in range(3):
                copy_job(("yT", i), yT[:, (0, 4, 6)[i]:(0, 4, 6)[i] + 2, :], "yT_ready")

            acc_squares(1)
            root(3)
            act.wait_ge(S("resid"), 1)
            squares(x, 0)
            root(4)
            norm_T(2, xT, "g_cross")
            for i in range(2):
                copy_job(("cq", i), memT[:, 2 * i:2 * i + 2, :], "cq_copied")
            attention(ATT2, len(ATT1))
            for i in range(2):
                copy_job(("coT", i), memT[:, 4 + 2 * i:6 + 2 * i, :], "coT_ready")
            acc_squares(2)
            root(5)
            act.wait_ge(S("resid"), 2)
            squares(x, 0)
            root(6)
            norm_T(3, xT, "g_ffn")
            act.wait_ge(S("gpad_zero"), 1)
            for f in range(FC + 1):
                if f < FC:
                    b = got(act, ("up", f))
                    link(A(gpad[:, f % 2, 2:258], b[:, 0:T], ACT.Copy), "ff_gate")
                if f:
                    act.wait_ge(S("ff_conv"), f)
                    g = (f - 1) % 2
                    link(A(fa[:, g, :], fa[:, g, :], ACT.Silu), "ff_silu")
            acc_squares(3)
            root(7)
            act.wait_ge(S("resid"), 3)
            squares(x, 0)
            root(8)
            norm_T(4, xT, "g_mix2")
            link(A(cb[0:8, 0, :], got(act, ("flog",))[0:8, 0:T], ACT.Identity, bias=C("foxb")[0:8]), "flog_copied")
            link(A(cb[0:8, 1, :], cb[0:8, 0, :], ACT.Abs))
            link(A(cb[0:8, 1, :], cb[0:8, 1, :], ACT.Exp, scale=-1.0))
            link(A(cb[0:8, 1, :], cb[0:8, 1, :], ACT.Ln, bias=1.0), "fox_ln")
            for i in range(7):
                copy_job(("T2", i), t2[:, 2 * i:2 * i + 2, :], "t2_copied")
            for j, name in enumerate((("kc",), ("vc",))):
                b = got(act, name).rearrange("p (k t) -> p k t", k=2)
                A(kc2[0:HD, j, :, :], b[0:HD], ACT.Copy)
                link(A(kc2[HD:P, j, :, 0:T - 1], b[HD:P, :, 1:T], ACT.Copy), "t2_copied")
            for i in range(2):
                copy_job(("fv", i), fv[:, :, 256 * i:256 * i + 256], "r2_copied")
            copy_job(("vv",), vv, "r2_copied")
            copy_job(("ngate",), ng, "r2_copied", ACT.Sigmoid)
            for j in range(2):
                b = got(act, ("chid", j))
                link(A(cbias[:, j:j + 1], b[:, 32:33], ACT.Copy))
                link(A(chid[:, j, 0:30], b[:, 0:30], ACT.Gelu, bias=cbias[:, j:j + 1]), "chid_done")
            link(A(ckc[:, 0, 0:30], got(act, ("ck2",))[:, 0:30], ACT.Copy), "ck2_done")
            link(A(cvr[0:NCMP].rearrange("p g d -> p (g d)"), got(act, ("cv2",))[0:NCMP, 0:P], ACT.Copy), "cv2_done")
            for i in range(8):
                b = got(act, ("merge", i)).rearrange("p (t n) -> p t n", t=2)
                link(A(mg[:, :, i // 4, (i % 4) * 256:(i % 4) * 256 + 256], b, ACT.Sigmoid), "merge_gated")
            attention(ATT3, len(ATT1) + len(ATT2))
            for i in range(4):
                copy_job(("ysT", i), yT[:, 2 * i:2 * i + 2, :], "ysT_ready")
            for i in range(4):
                copy_job(("mT", i), yT[:, 2 * i:2 * i + 2, :], "mT_ready")
            act.wait_ge(S("resid"), 4)
            squares(x, 0)
            root(9)
            norm_T(5, xT, "g_ffn2")
            for i in range(8):
                copy_job(("pq", i), pqT[:, 2 * i:2 * i + 2, :], "pq_copied")
            for t in range(NT):
                for q in range(4):
                    b = got(act, ("ps", t, q))
                    link(A(ps[:, t, 4 * q:4 * q + 4, :].rearrange("p k n -> p (k n)"), b, ACT.Copy), "ps_copied")
            for t in range(NT):
                act.wait_ge(S("best_ready"), t + 1)
                link(A(best, best, ACT.Exp), "best_exp")
            act.wait_ge(S("rT_copied"), 2)
            act.wait_ge(S("hot_ready"), 1)
            act.nop().then_inc(S("tabled"), 4)
            with act.Fori(0, T // (4 * NB)) as i:
                for q in range(NB):
                    act.wait_ge(S("hot_used"), NB * i + q + 3)
                    A(table[:, bass.ds(4 * (NB * i + q), 4), :], ring[:, q, :].rearrange("p (t n) -> p t n", t=4),
                      ACT.Copy).then_inc(S("tabled"), 1)
            with act.Fori(0, NKEY // EU) as i:
                for b in range(EU):
                    act.wait_ge(S("ex_hidden"), EU * i + b + 1)
                    act.wait_ge(S("ex_used"), EU * i + b + 1)
                    A(coef[:, b % 2, :], ring[:, b, 0:T], ACT.Gelu).then_inc(S("ex_gelu"), 1)
            act.wait_ge(S("resid"), 5)
            squares(x, 0)
            root(10)

        @block.vector
        def _(dve):
            link = stepper(dve, "dve_step")
            V = nc.vector
            tt, ts, stt = V.tensor_tensor, V.tensor_scalar, V.scalar_tensor_tensor

            def inv_root(k, lo, n, width=DM):
                dve.wait_ge(S("sumsq"), k)
                if n == 4:
                    link(V.tensor_reduce(ms, ss.rearrange("p (t n) -> p t n", t=2), AX.X, ALU.add))
                    link(ts(ms, ms, 1.0 / width, EPS, ALU.mult, ALU.add), "meansq")
                else:
                    link(ts(ms, ss[:, lo:lo + 2], 1.0 / width, EPS, ALU.mult, ALU.add), "meansq")
                dve.wait_ge(S("rms"), k)
                link(V.reciprocal(rstd, rms))

            def normed(src):
                ts(xn[:, 0, :], src[:, 0, :], rstd[:, 0:1], None, ALU.mult)
                link(ts(xn[:, 1, :], src[:, 1, :], rstd[:, 1:2], None, ALU.mult), "xn_ready")

            def post_norm(k, use):
                inv_root(k, 0, 4)
                dve.wait_ge(S("ld_gain"), 16 * use)
                for t in range(NT):
                    link(stt(out=tmp, in0=accf[:, t, :], scalar=rstd[:, t:t + 1], in1=gain, op0=ALU.mult, op1=ALU.mult),
                         "acc_free" if t == NT - 1 else "dve_step")
                    link(tt(x[:, t, :], x[:, t, :], tmp, ALU.add), "resid" if t == NT - 1 else "dve_step")

            def attention(units, u0):
                for i in range(len(units) + 2):
                    if i < len(units):
                        u = u0 + i
                        kind, t, heads, n = UNITS[u]
                        m = len(heads)
                        b = got(dve, ("score", u))[:, 0:m * n].rearrange("p (h s) -> p h s", h=m)
                        if u >= 2:
                            dve.wait_ge(S("att_exp"), u - 1)
                        o = attS[:, u % 2, 0:m * n].rearrange("p (h s) -> p h s", h=m)
                        scale = P ** -0.5 if kind == "cross" else HD ** -0.5
                        if kind == "moba":
                            bias = (rel0 if t == 0 else rel1)[:, heads[0]:heads[0] + m, :]
                        elif kind == "cmp":
                            bias = K("maskC", t * NCMP, NCMP).unsqueeze(1).to_broadcast([P, m, n])
                        else:
                            bias = K("maskR", t * 256, n).unsqueeze(1).to_broadcast([P, m, n])
                        if kind == "cross":
                            link(ts(o, b, scale, None, ALU.mult), "att_scaled")
                        else:
                            link(stt(out=o, in0=b, scalar=scale, in1=bias, op0=ALU.mult, op1=ALU.add), "att_scaled")
                        link(V.tensor_reduce(amx[:, u % 4, 0:m], o, AX.X, ALU.max, negate=True), "att_max")
                    if i >= 2:
                        u = u0 + i - 2
                        kind, t, heads, n = UNITS[u]
                        m = len(heads)
                        d = P if kind == "cross" else HD
                        dve.wait_ge(S("att_exp"), u + 1)
                        link(V.reciprocal(ars[:, 0:m], asum[:, u % 4, 0:m]))
                        if kind in ("cmp", "slc", "win"):
                            g = ng[:, t, :].rearrange("p (h k) -> p h k", k=3)[:, heads[0]:heads[0] + m,
                                                                              ("cmp", "slc", "win").index(kind)]
                            link(tt(ars[:, 0:m], ars[:, 0:m], g, ALU.mult))
                            if kind == "cmp":
                                link(ts(ars[:, 0:m], ars[:, 0:m], K("valid", t, 1), None, ALU.mult))
                        b = got(dve, ("pv", u))[:, 0:m * d].rearrange("p (h d) -> p h d", h=m)
                        r = ars[:, 0:m].unsqueeze(2).to_broadcast([P, m, d])
                        at = slice(heads[0] * d, (heads[0] + m) * d)
                        dst = {"moba": ya, "cross": oc, "fox": ofox}.get(kind, onsa)[:, t, at]
                        dst3 = dst.rearrange("p (h d) -> p h d", h=m)
                        if kind in ("slc", "win"):
                            o = ott[:, 0:m * d]
                            link(tt(o.rearrange("p (h d) -> p h d", h=m), b, r, ALU.mult))
                            link(tt(dst, dst, o, ALU.add), "att_out")
                        else:
                            link(tt(dst3, b, r, ALU.mult), "att_out")

            def head_norm(k, src, g, gates):
                s8 = src.rearrange("p t (h d) -> p (t h) d", h=4)
                sq = tmp[:, 0:512].rearrange("p (k d) -> p k d", k=8)
                link(tt(sq, s8, s8, ALU.mult))
                link(V.tensor_reduce(hnm, sq, AX.X, ALU.add))
                link(ts(hnm, hnm, 1.0 / HD, EPS, ALU.mult, ALU.add), "hn_ms")
                dve.wait_ge(S("hn_rt"), k)
                link(V.reciprocal(hnm, hnr))
                link(tt(s8, s8, hnm.unsqueeze(2).to_broadcast([P, 8, HD]), ALU.mult))
                link(tt(src, src, g.unsqueeze(1).to_broadcast([P, NT, GW]), ALU.mult))
                link(tt(src, src, gates, ALU.mult), "hn_done")

            inv_root(1, 0, 2)
            normed(x)
            inv_root(2, 2, 2)
            dve.wait_ge(S("xT_ready"), 4)
            normed(memr)
            dve.wait_ge(S("ld_cols"), 16)
            dve.wait_ge(S("ld_const"), 16)
            link(V.memset(C("rel", 0, 4)[32:33], NEG), "rel_ready")
            link(V.tensor_copy(sel4[0:4], ident[0:4, 0:4].unsqueeze(2).to_broadcast([4, 4, P])), "sel_ready")
            link(tt(lbw[:, 0:2], C("lb", 0, 2), C("lb", 0, 2), ALU.subtract), "lb_shift")
            row = [gi[0:4, k, :] for k in range(8)]
            dve.wait_ge(S("ml_ln"), 1)
            link(ts(row[3], row[1], 0.0, None, ALU.min))
            link(tt(row[3], row[3], row[2], ALU.subtract))
            link(V.memset(row[7], 1.0))
            link(V.tensor_tensor_scan(row[4], row[7], row[3], 0.0, ALU.mult, ALU.add))
            link(tt(row[2], row[0], row[4], ALU.subtract))
            link(V.memset(row[7], 0.0))
            link(V.tensor_tensor_scan(row[5], row[7], row[2], 0.0, ALU.max, ALU.max))
            link(ts(row[6], row[5], -1.0, None, ALU.mult))
            link(tt(row[7], row[4], row[5], ALU.add), "ml_rows")
            dve.wait_ge(S("lb_exp"), 1)
            link(V.reciprocal(lbw[:, 4:6], lbw[:, 2:4]))
            link(tt(lbw[:, 4:6], lbw[:, 4:6], lbw[:, 2:4], ALU.mult))
            link(tt(lbw[:, 6:8], lbw[:, 4:6], lbw[:, 4:6], ALU.subtract))
            link(ts(lbw[:, 0:2], lbw[:, 6:8], -1.0, 1.0, ALU.mult, ALU.add))
            dve.wait_ge(S("t1_copied"), 2)
            g = TT["hf"].rearrange("p c t -> p (c t)")
            hq = TT["hq"].rearrange("p c t -> p (c t)")
            for c in range(2):
                link(ts(TT["hf"][:, c, :], TT["hf"][:, c, :], lbw[:, c:c + 1], lbw[:, 6 + c:7 + c], ALU.mult, ALU.add))
            link(ts(hgX[:, 0, :], g, 1e-18, None, ALU.max), "hg_f")
            link(ts(hk, g, -1.0, 1.0, ALU.mult, ALU.add), "hg_x")
            dve.wait_ge(S("hg_ln"), 1)
            link(V.tensor_tensor_scan(g, K("reset"), hgX[:, 1, :], 0.0, ALU.mult, ALU.add))
            dve.wait_ge(S("t1_copied"), 9)
            link(V.memset(pad[:, :, 0:2], 0.0))
            link(tt(pad[:, :, 2:258], TT["cc"], TT["ch"], ALU.mult))
            for c in range(2):
                o = yT[:, 2 + c, :]
                link(ts(o, pad[:, c, 0:256], C("sconv", c), None, ALU.mult))
                link(stt(out=o, in0=pad[:, c, 1:257], scalar=C("sconv", 2 + c), in1=o, op0=ALU.mult, op1=ALU.add))
                link(stt(out=o, in0=pad[:, c, 2:258], scalar=C("sconv", 4 + c), in1=o, op0=ALU.mult, op1=ALU.add))
            link(tt(yT[:, 2:4, :], yT[:, 2:4, :], TT["cb"], ALU.mult), "conv_done")
            dve.wait_ge(S("ld_rows1"), 16)
            link(V.memset(v1[:, :, :, 64:65], 1.0))
            for i, (name, _) in enumerate(R1):
                b = got(dve, ("R1", i)).rearrange("p (t n) -> p t n", t=2)
                bias = rows1[:, i * GW:(i + 1) * GW]
                if name == "mv":
                    for t in range(NT):
                        ins = tt(v1[:, t, :, 0:HD], b[:, t, :].rearrange("p (h d) -> p h d", h=4),
                                 bias.rearrange("p (h d) -> p h d", h=4), ALU.add)
                        link(ins, "r1_copied" if t else "dve_step")
                else:
                    link(tt(RR[name], b, bias.unsqueeze(1).to_broadcast([P, NT, GW]), ALU.add), "r1_copied")
            link(V.tensor_copy(rc.rearrange("p q t h -> p (q t h)"), got(dve, ("mgT",))[:, 0:16]), "mgT_copied")
            ML = [(0, [0, 1], T), (0, [2, 3], T), (1, [0, 1, 2, 3], P)]
            for u, (s, heads, n) in enumerate(ML):
                b = got(dve, ("mD", u))
                for i, h in enumerate(heads):
                    ins = stt(out=EW[:, u % 2, i * n:(i + 1) * n], in0=b[:, i * n:(i + 1) * n], scalar=rc[:, 0, s, h:h + 1],
                              in1=K("maskT", 0, n), op0=ALU.add, op1=ALU.add)
                link(ins, "ml_arg")
                dve.wait_ge(S("ml_exp"), u + 1)
                link(stt(out=WT[:, u, :], in0=got(dve, ("mQK", u)), scalar=HD ** -0.5, in1=EW[:, u % 2, :],
                         op0=ALU.mult, op1=ALU.mult), "ml_w")
            for t in range(NT):
                b = got(dve, ("mO", t))[:, 0:260].rearrange("p (h d) -> p h d", h=4)
                link(stt(out=den[:, 0:4], in0=b[:, :, 64], scalar=-1.0, in1=rc[:, 1, t, :], op0=ALU.mult, op1=ALU.max))
                link(tt(den[:, 0:4], b[:, :, 64], den[:, 0:4], ALU.max))
                link(V.reciprocal(den[:, 4:8], den[:, 0:4]))
                link(tt(hm3[:, t], b[:, :, 0:HD], den[:, 4:8].unsqueeze(2).to_broadcast([P, 4, HD]), ALU.mult), "ml_h")
            link(V.memset(hgA[:, 0:2], 0.0))

            def exponents(lv):
                D = hgD[:, lv % 2, :]
                if lv <= 7:
                    B = 2 ** lv
                    h = B // 2
                    Dv, gv = D.rearrange("p (n b) -> p n b", b=B), g.rearrange("p (n b) -> p n b", b=B)
                    mid = gv[:, :, h - 1:h].to_broadcast([P, 512 // B, h])
                    tt(Dv[:, :, 0:h], mid, gv[:, :, 0:h], ALU.subtract)
                    if lv <= 6:
                        link(tt(Dv[:, :, h:B], gv[:, :, h:B], mid, ALU.subtract), "hg_d")
                    else:
                        link(V.tensor_copy(Dv[:, :, h:B], gv[:, :, h:B]), "hg_d")
                else:
                    Dv, gv = (z.rearrange("p (c k t) -> p c k t", c=2, k=4) for z in (D, g))
                    last = [gv[:, :, k, 63:64].to_broadcast([P, 2, 64]) for k in range(4)]
                    tt(Dv[:, :, 1, :], last[1], gv[:, :, 1, :], ALU.subtract)
                    V.tensor_copy(Dv[:, :, 2, :], gv[:, :, 2, :])
                    tt(Dv[:, :, 3, :], gv[:, :, 3, :], last[2], ALU.add)
                    link(tt(Dv[:, :, 0, :], last[0], gv[:, :, 0, :], ALU.subtract))
                    link(tt(Dv[:, :, 0, :], Dv[:, :, 0, :], last[1], ALU.add), "hg_d")

            exponents(1)
            for lv in range(1, LV + 1):
                if lv < LV:
                    exponents(lv + 1)
                B = 2 ** lv
                h = B // 2
                D, X, kv, qv = (z.rearrange("p (n b) -> p n b", b=B) for z in
                                (hgD[:, lv % 2, :], hgX[:, lv % 2, :], hk, hq))
                dve.wait_ge(S("hg_e"), lv)
                if lv == 1:
                    dve.wait_ge(S("hg_ln"), 1)
                tt(X[:, :, 0:h], D[:, :, 0:h], kv[:, :, 0:h], ALU.mult)
                link(tt(X[:, :, h:B], D[:, :, h:B], qv[:, :, h:B], ALU.mult), "hg_x")
                for t in range(NT):
                    b = got(dve, ("hG", lv - 1, t)).rearrange("p (h t) -> p h t", h=4)
                    mask = K("lvl", (lv - 1) * P, P).bitcast(U32).unsqueeze(1).to_broadcast([P, 4, P])
                    link(V.copy_predicated(hgA[:, t], mask, b), "hg_kept")
            link(V.tensor_copy(hgA[:, 2], got(dve, ("hOff",)).rearrange("p (h t) -> p h t", h=4)), "hg_off")
            for t in range(NT):
                link(V.tensor_copy(ho[:, t, :], got(dve, ("hO", t))[:, 0:GW]), "hg_out")
            dve.wait_ge(S("gates_ready"), 1)
            head_norm(1, hm, rows1[:, 5 * GW:6 * GW], RR["mo"])
            head_norm(2, ho, rows1[:, 6 * GW:7 * GW], RR["hg"])
            dve.wait_ge(S("ld_rel"), 16 * 8)
            attention(ATT1, 0)
            post_norm(3, 1)
            inv_root(4, 0, 2)
            normed(x)
            attention(ATT2, len(ATT1))
            post_norm(5, 2)
            inv_root(6, 0, 2)
            normed(x)
            link(V.memset(gpad[:, :, 0:2], 0.0), "gpad_zero")
            for f in range(FC + 1):
                if f < FC:
                    dve.wait_ge(S("ff_gate"), f + 1)
                    o, p = fa[:, f % 2, :], gpad[:, f % 2, :]
                    link(ts(o, p[:, 0:256], C("fconv", f), C("fb", f), ALU.mult, ALU.add))
                    link(stt(out=o, in0=p[:, 1:257], scalar=C("fconv", 22 + f), in1=o, op0=ALU.mult, op1=ALU.add))
                    link(stt(out=o, in0=p[:, 2:258], scalar=C("fconv", 44 + f), in1=o, op0=ALU.mult, op1=ALU.add),
                         "ff_conv")
                if f:
                    dve.wait_ge(S("ff_silu"), f)
                    b = got(dve, ("up", f - 1))
                    link(tt(hid[:, f - 1, :], fa[:, (f - 1) % 2, :], b[:, T:2 * T], ALU.mult), "ffn_hidden")
            post_norm(7, 3)
            inv_root(8, 0, 2)
            normed(x)
            link(V.tensor_copy(sel8[0:8], ident[0:8, 0:8].unsqueeze(2).to_broadcast([8, 8, T])))
            r8 = [cb[0:8, k, :] for k in range(6)]
            dve.wait_ge(S("fox_ln"), 1)
            link(ts(r8[2], r8[0], 0.0, None, ALU.min))
            link(tt(r8[2], r8[2], r8[1], ALU.subtract))
            link(V.memset(r8[4], 1.0))
            link(V.tensor_tensor_scan(r8[3], r8[4], r8[2], 0.0, ALU.mult, ALU.add))
            link(ts(r8[4], r8[3], HD ** 0.5, None, ALU.mult))
            link(ts(r8[5], r8[3], -HD ** 0.5, None, ALU.mult))
            for k in (4, 5):
                link(V.tensor_copy(cb[HD:HD + 8, k, :], r8[k]))
            link(V.tensor_copy(sel8[HD:HD + 8], sel8[0:8]), "fox_rows")
            for i in range(3):
                b = got(dve, ("rope", i)).rearrange("p (k t) -> p k t", k=2)
                o = t2[:, 8 + 2 * i:10 + 2 * i, :]
                r = rt[:, i % 2, :].rearrange("p (k t) -> p k t", k=2)
                link(tt(r, b, K("sinq").unsqueeze(1).to_broadcast([P, 2, T]), ALU.mult), "roped")
                link(tt(o, o, K("cosq").unsqueeze(1).to_broadcast([P, 2, T]), ALU.mult))
                link(tt(o, o, r, ALU.add), "roped_all" if i == 2 else "dve_step")
            link(tt(ckc[:, 1, 0:30], got(dve, ("crot",))[:, 0:30], K("sinc"), ALU.mult), "crot_done")
            link(tt(ckc[:, 2, 0:30], ckc[:, 0, 0:30], K("cosc"), ALU.mult))
            link(tt(ckc[:, 2, 0:30], ckc[:, 2, 0:30], ckc[:, 1, 0:30], ALU.add), "cmpk_ready")
            dve.wait_ge(S("r2_copied"), 4)
            attention(ATT3, len(ATT1) + len(ATT2))
            dve.wait_ge(S("merge_gated"), 8)
            for br in range(2):
                dve.wait_ge(S("acc_ready"), 4 + br)
                for t in range(NT):
                    o = mg[:, t, br, :]
                    link(tt(o, o, accf[:, t, :], ALU.mult), "acc_free" if t else "dve_step")
            link(tt(mg[:, :, 0, :], mg[:, :, 0, :], mg[:, :, 1, :], ALU.add), "merged")
            dve.wait_ge(S("acc_ready"), 6)
            for t in range(NT):
                link(tt(x[:, t, :], x[:, t, :], accf[:, t, :], ALU.add), "acc_free" if t else "dve_step")
            dve.nop().then_inc(S("resid"), 1)
            inv_root(9, 0, 2)
            normed(x)
            topu, bestu = topi.bitcast(U32), besti.bitcast(U32)
            partu = part.bitcast(U32)
            lists = range(16)
            for t in range(NT):
                dve.wait_ge(S("ps_copied"), 4 * (t + 1))
                for k in lists:
                    ins = V.max(top[:, k, 0:8], ps[:, t, k, :])
                link(ins)
                for k in lists:
                    V.max_index(topu[:, k, 0:8], top[:, k, 0:8], ps[:, t, k, :])
                    ins = V.match_replace(ps[:, t, k, :], top[:, k, 0:8], ps[:, t, k, :], -3e38)
                link(ins)
                for k in lists:
                    ins = V.max(top[:, k, 8:16], ps[:, t, k, :])
                link(ins)
                for k in lists:
                    ins = V.max_index(topu[:, k, 8:16], top[:, k, 8:16], ps[:, t, k, :])
                link(ins)
                link(V.tensor_copy(topi, topu))
                for h in range(PH):
                    ins = tt(cand[:, h, :].rearrange("p (a b) -> p a b", a=TOPK),
                             top[:, 2 * h, :].unsqueeze(2).to_broadcast([P, TOPK, TOPK]),
                             top[:, 2 * h + 1, :].unsqueeze(1).to_broadcast([P, TOPK, TOPK]), ALU.add)
                link(ins)
                for h in range(PH):
                    ins = V.max(best[:, h, 0:8], cand[:, h, :])
                link(ins)
                for h in range(PH):
                    V.max_index(bestu[:, h, 0:8], best[:, h, 0:8], cand[:, h, :])
                    ins = V.match_replace(cand[:, h, :], best[:, h, 0:8], cand[:, h, :], -3e38)
                link(ins)
                for h in range(PH):
                    ins = V.max(best[:, h, 8:16], cand[:, h, :])
                link(ins)
                for h in range(PH):
                    ins = V.max_index(bestu[:, h, 8:16], best[:, h, 8:16], cand[:, h, :])
                link(ins)
                link(ts(wneg, best[:, :, 0], -1.0, None, ALU.mult))
                link(tt(best, best, wneg.unsqueeze(2).to_broadcast([P, PH, TOPK]), ALU.add), "best_ready")
                link(ts(partu[:, 0], bestu, 4, None, ALU.logical_shift_right))
                link(ts(partu[:, 1], bestu, 15, None, ALU.bitwise_and))
                link(V.tensor_copy(part, partu))
                for side in range(2):
                    link(tt(pick.rearrange("p h k j -> p (h k) j"),
                            part[:, side].rearrange("p h k -> p (h k)").unsqueeze(2).to_broadcast([P, P, TOPK]),
                            K("iota16").unsqueeze(1).to_broadcast([P, P, TOPK]), ALU.is_equal))
                    num = topi.rearrange("p (h s) n -> p h s n", s=2)[:, :, side, :]
                    link(tt(pick, pick, num.unsqueeze(2).to_broadcast([P, PH, TOPK, TOPK]), ALU.mult))
                    link(V.tensor_reduce(rout[:, side, :], pick.rearrange("p h k j -> p (h k) j"), AX.X, ALU.add))
                dve.wait_ge(S("best_exp"), t + 1)
                link(V.tensor_reduce(wsum, best, AX.X, ALU.add))
                link(V.reciprocal(wrec, wsum))
                link(tt(rout[:, 2, :].rearrange("p (h k) -> p h k", h=PH), best,
                        wrec.unsqueeze(2).to_broadcast([P, PH, TOPK]), ALU.mult), "routes")
                b = got(dve, ("rT", t))[:, 0:3 * P].rearrange("p (k t) -> p k t", k=3)
                link(V.tensor_copy(rT[:, :, t * P:(t + 1) * P], b), "rT_copied")
            link(V.memset(coef, 0.0), "zrow_ready")
            with dve.Fori(0, T // (4 * NB)) as i:
                for q in range(NB):
                    dve.wait_ge(S("hot_used"), NB * i + q + 1)
                    for k in range(4):
                        def at(r):
                            return rT[:, r, bass.ds(4 * NB * i + (4 * q + k), 1)]
                        ts(hot[:, q % 2, 0, k, :], K("iota"), at(0), at(2), ALU.is_equal, ALU.mult)
                        ins = ts(hot[:, q % 2, 1, k, :], K("iota"), at(1), None, ALU.is_equal)
                    ins.then_inc(S("hot_ready"), 1)
            dve.wait_ge(S("tabled"), T // 4 + 4)
            with dve.Fori(0, NKEY // EU) as i:
                for b in range(EU):
                    dve.wait_ge(S("ex_gelu"), EU * i + b + 1)
                    tt(coef[:, b % 2, :], coef[:, b % 2, :], table[:, :, bass.ds(EU * i + b, 1)].rearrange("p t o -> p (t o)"),
                       ALU.mult).then_inc(S("ex_coef"), 1)
            dve.wait_ge(S("acc_ready"), 7)
            for t in range(NT):
                link(tt(x[:, t, :], x[:, t, :], accf[:, t, :], ALU.add), "resid5" if t else "dve_step")
            dve.nop().then_inc(S("resid"), 1)
            inv_root(10, 0, 2)
            dve.wait_ge(S("ld_gain"), 64)
            for t in range(NT):
                link(stt(out=x[:, t, :], in0=x[:, t, :], scalar=rstd[:, t:t + 1], in1=area[:, 0:DM],
                         op0=ALU.mult, op1=ALU.mult), "out_rows2" if t == 0 else "out_rows")


def constants():
    c = np.zeros((P, NCONST), np.float32)

    def put(name, v):
        at, w = CONST[name]
        c[:v.shape[0], at:at + w] = v.reshape(v.shape[0], w)

    p = np.arange(P)
    put("ident", np.eye(P, dtype=np.float32))
    t = (np.arange(NT)[None, :] * P + p[:, None])[:, :, None]
    put("maskR", np.where(np.arange(T)[None, None, :] <= t, 0.0, NEG).astype(np.float32))
    put("maskT", np.where(np.arange(T)[None, :] >= p[:, None], 0.0, NEG).astype(np.float32))
    u = np.arange(512)
    dist = u - 255
    n = np.maximum(dist, 1).astype(np.float32)
    large = 16 + (np.log(n / np.float32(16)) / np.float32(np.log(8.0)) * np.float32(16)).astype(np.int32)
    bucket = np.where(np.maximum(dist, 0) < 16, np.maximum(dist, 0), np.minimum(large, 31))
    oh = np.zeros((33, 512), np.float32)
    for j in range(512):
        d = 255 - j
        if d < 0:
            oh[32, j] = 1.0
        else:
            oh[bucket[d + 255], j] = 1.0
    put("oh", oh)
    s_, t_ = p[:, None], p[None, :]
    lv = np.zeros((P, 8, P), np.float32)
    lv[:, 0] = np.eye(P)
    for k in range(1, 8):
        B = 2 ** k
        lv[:, k] = (s_ // B == t_ // B) & (s_ % B < B // 2) & (t_ % B >= B // 2)
    put("lvl", lv)
    put("reset", np.broadcast_to((np.arange(512) % 64 != 0).astype(np.float32), (P, 512)))
    inv = np.power(np.float32(500000.0), -np.arange(0, 16, 2, dtype=np.float32) / np.float32(16))

    def rope(pos):
        ang = pos.astype(np.float32)[:, None] * inv[None, :]
        cos, sin = np.ones((P, len(pos)), np.float32), np.zeros((P, len(pos)), np.float32)
        for g in range(2):
            for half in range(2):
                at = 64 * g + 8 * half
                cos[at:at + 8], sin[at:at + 8] = np.cos(ang).T, np.sin(ang).T
        return cos, sin

    cq, sq = rope(np.arange(T))
    put("cosq", cq)
    put("sinq", sq)
    rot = np.zeros((P, P), np.float32)
    for g in range(2):
        for j in range(8):
            rot[64 * g + 8 + j, 64 * g + j] = -1.0
            rot[64 * g + j, 64 * g + 8 + j] = 1.0
    put("rot", rot)
    end = np.tile(np.arange(NCMP) * 16 + 31, 2)
    cc, sc = rope(end)
    put("cosc", cc)
    put("sinc", sc)
    put("iota", np.broadcast_to(np.arange(128, dtype=np.float32), (P, 128)))
    put("iota16", np.broadcast_to(np.arange(16, dtype=np.float32), (P, 16)))
    put("maskC", np.where(end[None, None, :NCMP] <= t, 0.0, NEG).astype(np.float32))
    put("valid", (t[:, :, 0] >= 31).astype(np.float32))
    return c


def layout(inp):
    f = {k: np.asarray(v) for k, v in inp.items()}
    w1, w2 = f["w_in"][0], f["w_in_2"][0]

    def chunked(w, cols):
        w = w[:, cols]
        return w.reshape(-1, P, w.shape[1]).transpose(1, 0, 2).reshape(P, -1)

    def span(a, n=256):
        return np.arange(a, a + n)

    nq = np.concatenate([np.concatenate([span(Q_NQ + HD * b, HD), span(Q_NQ + HD * (4 + b), HD)]) for b in range(4)])

    def doubled(at):
        return np.concatenate([span(at + HD * g, HD) for g in (0, 0, 1, 1)])

    up = f["w_ffn_in"][0]

    def two_chunks(w, i):
        return chunked(w[256 * i:256 * i + 256], slice(None))

    def slot(key):
        kind, i = key[0], (key[1] if len(key) > 1 else 0)
        s = span(256 * i)
        if kind == "gate":
            return chunked(w1, span(O_GI, 8))
        if kind in ("T1", "R1"):
            return chunked(w1, span((T1 if kind == "T1" else R1)[i][1]))
        if kind in ("ck", "cv", "cq"):
            return chunked(f["w_" + kind][0], s)
        if kind == "mix":
            return two_chunks(f["w_mix_out"][0], i)
        if kind == "co":
            return two_chunks(f["w_co"][0], i)
        if kind == "up":
            return chunked(up, np.concatenate([span(P * i, P), span(DFF + P * i, P)]))
        if kind == "down":
            return two_chunks(f["w_ffn_out"][0], i)
        if kind == "flog":
            return chunked(w2, span(Q_FL, 8))
        if kind in ("fq", "fk", "fv"):
            return chunked(w2, {"fq": Q_FQ, "fk": Q_FK, "fv": Q_FV}[kind] + s)
        if kind == "nq":
            return chunked(w2, nq[256 * i:256 * i + 256])
        if kind == "kk":
            return chunked(w2, np.concatenate([span(Q_KS, P), span(Q_KW, P)]))
        if kind in ("kc", "vc"):
            return chunked(w2, doubled(Q_KC if kind == "kc" else Q_VC))
        if kind == "vv":
            return chunked(w2, np.concatenate([span(Q_VS, P), span(Q_VW, P)]))
        if kind == "ngate":
            return chunked(w2, span(Q_GATE, 24))
        if kind == "cw1":
            return f["nsa_cmp_w1_2"][0, i].reshape(16, P, P).transpose(1, 0, 2).reshape(P, -1)
        if kind == "merge":
            return chunked(w2, Q_MERGE + s)
        if kind == "branch":
            return two_chunks(f["w_branch_2"][0, i // 2], i % 2)
        if kind == "wout":
            return two_chunks(f["w_out_2"][0], i)
        if kind == "pq":
            return chunked(f["peer_wq_2"][0], s)
        assert kind == "keys"
        return f["peer_subkeys_2"][0].transpose(3, 0, 1, 2).reshape(P, -1)

    ws = np.zeros((len(SLOTS), P, SLOT), np.float32)
    for n, key in enumerate(SLOTS):
        v = slot(key)
        ws[n, :, :v.shape[1]] = v

    cols = np.zeros((P, NCOLS), np.float32)

    def put(name, v):
        at, w = COLS[name]
        cols[:v.shape[0], at:at + w] = v.reshape(v.shape[0], w)

    def col(v):
        return v.reshape(-1, P).T

    b = f["b_in"][0]
    put("b1", np.concatenate([col(b[o:o + GW]) for _, o in T1], axis=1))
    put("bi", b[O_GI:O_GI + 4, None])
    put("bf", b[O_GF:O_GF + 4, None])
    for name, key in (("g_mix", "norm_mix_pre"), ("g_mem", "mem_norm"), ("g_cross", "norm_cross_pre"),
                      ("g_ffn", "norm_ffn_pre"), ("g_mix2", "norm_mix_2"), ("g_ffn2", "norm_ffn_2"),
                      ("sconv", "sconv_w"), ("lb", "hgrn_lb_logits"), ("fconv", "ffn_conv_w"), ("fb", "ffn_conv_b")):
        put(name, col(f[key][0]))
    put("foxb", f["fox_f_bias_2"][0][:, None])
    put("rel", f["rel_bias"])
    cw2 = f["nsa_cmp_w2_2"][0]
    put("w2k", np.concatenate([cw2[0], cw2[0]], axis=1))
    put("w2v", cw2[1])
    put("pos", f["nsa_cmp_pos_2"][0].reshape(2, 16, P).transpose(2, 0, 1))
    rows1 = np.concatenate([b[o:o + GW] for _, o in R1] + [f["mlstm_norm"][0], f["hgrn_norm"][0]])
    gains = np.stack([f["norm_mix_post"][0], f["norm_cross_post"][0], f["norm_ffn_post"][0], f["norm_final_2"]])
    u = f["peer_u_2"][0].reshape(NKEY, NKEY, KC, P).transpose(1, 3, 2, 0).reshape(NKEY, P, KC * NKEY)
    v = f["peer_v_2"][0].reshape(NKEY, NKEY, DM).transpose(1, 0, 2)
    return {"x": f["x"], "mem": f["mem"], "consts": constants(), "cols": cols, "wstream": ws,
            "rows1": rows1, "gains": gains, "u": np.ascontiguousarray(u), "v": np.ascontiguousarray(v)}


def kernel(**inputs):
    import concourse.bacc as bacc
    from concourse.bass_utils import run_bass_kernel_spmd

    arrays = {k: np.ascontiguousarray(v) for k, v in layout(inputs).items()}
    nc = bacc.Bacc("TRN2", target_bir_lowering=False, num_devices=1)
    a = {k: nc.dram_tensor(k, v.shape, mybir.dt.from_np(v.dtype), kind="ExternalInput").ap()
         for k, v in arrays.items()}
    a["out"] = nc.dram_tensor("out", (1, T, DM), F32, kind="ExternalOutput").ap()
    build(nc, a)
    return run_bass_kernel_spmd(nc, [arrays], core_ids=[0]).results[0]["out"]
```

```python
from contextlib import ExitStack

import numpy as np
import concourse.bass as bass
from concourse import mybir

P = 128
T = 256
NT = T // P
DM = 1024
KC = DM // P
PC = 1024
NR = 4
NB = 4
HD = 64
EPS = 1e-6
NEG = -1e30
DFF = 2816
FC = DFF // P
NCMP = 15
NKEY = 128
PH = 8
TOPK = 16
NE = NKEY * NKEY

F32 = mybir.dt.float32
F32R = mybir.dt.float32r
U32 = mybir.dt.uint32
ALU = mybir.AluOpType
ACT = mybir.ActivationFunctionType
AX = mybir.AxisListType

GW = 256
O_MQ, O_MK, O_MV, O_MO = 0, GW, 2 * GW, 3 * GW
O_GI, O_GF = 4 * GW, 4 * GW + 4
O_C = 4 * GW + 8
O_CB, O_CC, O_CH, O_AQ, O_AK, O_AV, O_HQ, O_HF, O_HI, O_HG = (O_C + k * GW for k in range(10))
T1 = [("hf", O_HF), ("hq", O_HQ), ("mq", O_MQ), ("mk", O_MK), ("aq", O_AQ), ("ak", O_AK),
      ("cb", O_CB), ("cc", O_CC), ("ch", O_CH)]
R1 = [("mv", O_MV), ("hi", O_HI), ("av", O_AV), ("mo", O_MO), ("hg", O_HG)]
BW = 512
Q_FQ, Q_FK, Q_FV, Q_FL = 0, BW, 2 * BW, 3 * BW
Q_NQ = 3 * BW + 8
Q_KC, Q_VC, Q_KS, Q_VS, Q_KW, Q_VW = (Q_NQ + BW + k * 128 for k in range(6))
Q_GATE = Q_NQ + BW + 768
Q_MERGE = Q_GATE + 24

CONST = {}
_at = 0
for _name, _w in [("ident", 128), ("iota", 128), ("maskR", 2 * 256), ("maskT", 256), ("oh", 512), ("lvl", 8 * 128),
                  ("reset", 512), ("cosq", 256), ("sinq", 256), ("rot", 128), ("cosc", 30), ("sinc", 30),
                  ("iota16", 16), ("maskC", 2 * NCMP), ("valid", 2)]:
    CONST[_name] = (_at, _w)
    _at += _w
NCONST = _at

COLS = {}
_at = 0
for _name, _w in [("b1", 18), ("bi", 1), ("bf", 1), ("g_mix", 8), ("g_mem", 8), ("g_cross", 8), ("g_ffn", 8),
                  ("g_mix2", 8), ("g_ffn2", 8), ("sconv", 6), ("lb", 2), ("fconv", 66), ("fb", 22), ("foxb", 1), ("rel", 4), ("w2k", 128), ("w2v", 64), ("wg1", 64), ("wg2", 256), ("pos", 64)]:
    COLS[_name] = (_at, _w)
    _at += _w
NCOLS = _at


def slots():
    s = [("T1", i) for i in range(len(T1))] + [("R1", i) for i in range(len(R1))]
    s += [("ck", i) for i in range(2)] + [("cv", i) for i in range(2)]
    s += [("mix", i) for i in range(4)]
    s += [("cq", i) for i in range(2)] + [("co", i) for i in range(2)]
    s += [("up", i) for i in range(FC)] + [("down", i) for i in range(FC // 2)]
    s += [("fq", i) for i in range(2)] + [("fk", i) for i in range(2)] + [("nq", i) for i in range(2)]
    s += [("kk",), ("kc",), ("vc",)] + [("fv", i) for i in range(2)] + [("vv",)]
    s += [("cw1", j) for j in range(2)]
    s += [("merge", i) for i in range(8)]
    s += [("branch", i) for i in range(4)] + [("wout", i) for i in range(4)]
    s += [("pq", i) for i in range(8)]
    return s


SLOTS = slots()
SLOT_AT = {k: n for n, k in enumerate(SLOTS)}
E0 = 2 * len(SLOTS)
AHEAD_TOPK = (16, 16)
AHEAD_TABLE = 16
AHEAD = sum(AHEAD_TOPK) + AHEAD_TABLE
EB = E0 + AHEAD
EC = EB + AHEAD
REST = NKEY - AHEAD
NPIECE = E0 + 2 * NKEY


def piece_u(n):
    return E0 + n if n < AHEAD else EC + max(2 * (n - AHEAD) - 1, 0)


def piece_v(n):
    return EB + n if n < AHEAD else EC + min(2 * (n - AHEAD) + 2, 2 * REST - 1)


def att_units(kind):
    if kind == "moba":
        return [(kind, 0, [0, 1, 2, 3], 128), (kind, 1, [0, 1], 256), (kind, 1, [2, 3], 256)]
    if kind == "cross":
        return [(kind, t, [2 * i, 2 * i + 1], 256) for t in range(2) for i in range(2)]
    if kind == "cmp":
        return [(kind, t, list(range(4 * g, 4 * g + 4)), NCMP) for t in range(2) for g in range(2)]
    return [(kind, 0, list(range(4 * g, 4 * g + 4)), 128) for g in range(2)] + \
        [(kind, 1, [2 * i, 2 * i + 1], 256) for i in range(4)]


ATT1 = att_units("moba")
ATT2 = att_units("cross")
ATT3 = att_units("fox") + att_units("cmp") + att_units("slc") + att_units("win")
UNITS = ATT1 + ATT2 + ATT3
LV = 8
MEM_AT = {1: ("ck", 0), 2: ("ck", 1), 3: ("cv", 0), 4: ("cv", 1)}
EVEN_ODD = {2: (0, 1), 4: (0, 2, 1, 3)}


def jobs():
    out = []
    n = {}

    def job(name, sem):
        n[sem] = n.get(sem, 0) + 1
        out.append((name, sem, n[sem]))

    def attention(units, u0):
        for i in range(len(units) + 2):
            if i < len(units):
                job(("score", u0 + i), "att_scaled")
            if 1 <= i <= len(units):
                job(("turn", u0 + i - 1), "att_turned")
            if i >= 2:
                job(("pv", u0 + i - 2), "att_out")

    def norm(k):
        for c in range(4):
            job(("xn", k, c), "xT_ready")

    norm(0)
    job(("gate",), "grow_copied")
    job(("gateT",), "gates_copied")
    for i in range(len(T1)):
        job(("T1", i), "t1_copied")
    for i in range(len(R1)):
        job(("R1", i), "r1_copied")
    norm(1)
    job(("bias",), "relvec_copied")
    job(("mgT",), "mgT_copied")
    for u in range(3):
        job(("mD", u), "ml_arg")
        job(("mQK", u), "ml_w")
    for t in range(NT):
        job(("mO", t), "ml_h")
    for lv in range(LV):
        for t in range(NT):
            job(("hG", lv, t), "hg_kept")
        if lv in MEM_AT:
            job(MEM_AT[lv], "ckv_copied")
    job(("hOff",), "hg_off")
    for t in range(NT):
        job(("hO", t), "hg_out")
    attention(ATT1, 0)
    for i in range(3):
        job(("yT", i), "yT_ready")
    norm(2)
    for i in range(2):
        job(("cq", i), "cq_copied")
    attention(ATT2, len(ATT1))
    job(("coT", 0), "coT_ready")
    job(("coT", 1), "coT_ready")
    norm(3)
    for f in range(FC):
        job(("up", f), "ffn_hidden")
    norm(4)
    job(("gate2",), "grow2_copied")
    job(("gate2T",), "flog_copied")
    for i in range(7):
        job(("T2", i), "t2_copied")
    job(("kc",), "t2_copied")
    job(("vc",), "t2_copied")
    for i in range(2):
        job(("fv", i), "r2_copied")
    job(("vv",), "r2_copied")
    for i in range(3):
        job(("rope", i), "roped")
    for j in range(2):
        job(("chid", j), "chid_done")
    job(("ck2",), "ck2_done")
    job(("crot",), "crot_done")
    job(("cv2",), "cv2_done")
    for i in range(8):
        job(("merge", i), "merge_gated")
    attention(ATT3, len(ATT1) + len(ATT2))
    for i in range(4):
        job(("ysT", i), "ysT_ready")
    for i in range(4):
        job(("mT", i), "mT_ready")
    norm(5)
    for i in range(8):
        job(("pq", i), "pq_copied")
    for t in range(NT):
        for b in range(4):
            job(("ps", t, b), "ps_copied")
    for t in range(NT):
        job(("rT", t), "rT_copied")
    while len(out) % NB:
        job(("pad", len(out)), "pad_free")
    return out


JOBS = jobs()
JOB = {name: n for n, (name, _, _) in enumerate(JOBS)}


def build(nc, a):
    with ExitStack() as ctx:
        sems = {}

        def S(name):
            if name not in sems:
                sems[name] = ctx.enter_context(nc.semaphore(name))
            return sems[name]

        BASE = -(-nc.sbuf_base // 32) * 32

        def sb(name, at, n, dt=F32):
            return nc.alloc_sbuf_tensor_at("sb_" + name, [P, n], dt, offset=BASE + 4 * at)[:]

        small = sb("small", 0, 160)
        wide = max(-(-NCOLS // 8) * 8, 3 * T)
        columns = sb("cols", 160, wide)
        cols = columns[:, 0:NCOLS]
        at = 160 + wide
        fixc = sb("fixc", at, 256)
        at += 256
        raw = sb("raw", at, NR * PC).rearrange("p (r n) -> p r n", r=NR)
        hi = sb("hi", at + NR * PC, NR * PC, F32R).rearrange("p (r n) -> p r n", r=NR)
        lo = sb("lo", at + 2 * NR * PC, NR * PC, F32R).rearrange("p (r n) -> p r n", r=NR)
        at += 3 * NR * PC
        XH = sb("XH", at, KC * T, F32R).rearrange("p (c t) -> p c t", c=KC)
        XL = sb("XL", at + KC * T, KC * T, F32R).rearrange("p (c t) -> p c t", c=KC)
        at += 2 * KC * T
        gwh, gwl = sb("gwh", at, 320, F32R), sb("gwl", at + 320, 320, F32R)
        at += 640
        early = sb("early", at - 640, 2 * T).rearrange("p (b t) -> p b t", b=2)
        AREA_AT = at
        AREA = (nc.sbuf_usable_end - BASE) // 32 * 8 - AREA_AT
        area = sb("area", AREA_AT, AREA)
        ring = ctx.enter_context(nc.psum_tensor("ring", [P, NB, 512], F32))[:]
        acc = ctx.enter_context(nc.psum_tensor("acc", [P, NT, 2, 512], F32))[:]
        accf = acc.rearrange("p t n c -> p t (n c)")

        class Place:
            def __init__(self, at):
                self.at = at

            def take(self, n):
                at, self.at = self.at, self.at + -(-n // 8) * 8
                assert self.at <= AREA, (self.at, AREA)
                return area[:, at:at + n]

        def K(name, lo=0, n=None):
            at, w = CONST[name]
            if at < 256:
                return fixc[:, at + lo:at + (w if n is None else lo + n)]
            at -= 256
            return const[:, at + lo:at + (w if n is None else lo + n)]

        def C(name, lo=0, n=1):
            at, _ = COLS[name]
            return cols[:, at + lo:at + lo + n]

        ident = K("ident")

        pl = Place(0)
        x = pl.take(NT * DM).rearrange("p (t d) -> p t d", t=NT)
        const = pl.take(NCONST - 256)
        xn = pl.take(NT * DM).rearrange("p (t d) -> p t d", t=NT)
        tmp = pl.take(DM)
        gain = pl.take(DM)
        att = pl.take(3 * 1024)
        attS, attP, attT = (att[:, k * 1024:(k + 1) * 1024].rearrange("p (b n) -> p b n", b=2) for k in range(3))
        squared = att[:, 0:DM]
        stage = pl.at

        def split(name, pl, n):
            at = AREA_AT + pl.at
            pl.take(2 * n)
            return sb(name + "h", at, n, F32R), sb(name + "l", at + n, n, F32R)

        yc = pl.take(2 * T).rearrange("p (c t) -> p c t", c=2)
        grow = pl.take(16).rearrange("p (t n) -> p t n", t=NT)
        t1 = pl.take(18 * T).rearrange("p (k t) -> p k t", k=18)
        TT = {name: t1[:, 2 * i:2 * i + 2, :] for i, (name, _) in enumerate(T1)}
        v1 = pl.take(NT * 4 * 65).rearrange("p (t h d) -> p t h d", t=NT, h=4)
        r1 = pl.take(4 * NT * GW).rearrange("p (k t n) -> p k t n", k=4, t=NT)
        RR = {"hi": r1[:, 0], "av": r1[:, 1], "mo": r1[:, 2], "hg": r1[:, 3]}
        rows1 = pl.take(7 * GW)
        relb = pl.take(4 * 384)
        rel0 = relb[:, 0:512].rearrange("p (h s) -> p h s", h=4)
        rel1 = relb[:, 512:1536].rearrange("p (h s) -> p h s", h=4)
        ckT = pl.take(4 * T).rearrange("p (k t) -> p k t", k=4)
        cv = pl.take(NT * 512).rearrange("p (t n) -> p t n", t=NT)
        ya = pl.take(NT * GW).rearrange("p (t n) -> p t n", t=NT)
        gi = pl.take(8 * T).rearrange("p (k t) -> p k t", k=8)
        ml = att[:, 0:5 * 512].rearrange("p (k n) -> p k n", k=5)
        EW, WT = ml[:, 0:2], ml[:, 2:5]
        hm = pl.take(NT * GW).rearrange("p (t n) -> p t n", t=NT)
        ho = pl.take(NT * GW).rearrange("p (t n) -> p t n", t=NT)
        hgD = pl.take(1024).rearrange("p (b n) -> p b n", b=2)
        hgX = pl.take(1024).rearrange("p (b n) -> p b n", b=2)
        hgA = pl.take(3 * 512).rearrange("p (k h t) -> p k h t", k=3, h=4)
        hk = pl.take(512)
        memr = area[:, pl.at - NT * DM:pl.at].rearrange("p (t d) -> p t d", t=NT)
        pad = pl.take(2 * 258).rearrange("p (k t) -> p k t", k=2)
        oc = hgD
        relv = gain[:, 0:512]
        sel4 = pl.take(512).rearrange("p (h t) -> p h t", h=4)
        cqT = t1[:, 0:4]
        pl = Place(stage)
        hidh, hidl = (z.rearrange("p (k t) -> p k t", k=FC) for z in split("hid", pl, FC * T))
        ht = pl.take(T)
        gpad = pl.take(2 * 258).rearrange("p (k t) -> p k t", k=2)
        fa = pl.take(2 * T).rearrange("p (k t) -> p k t", k=2)
        pl = Place(stage)
        t2 = pl.take(14 * T).rearrange("p (k t) -> p k t", k=14)
        fqT, fkT, nqT, kkT = t2[:, 0:4], t2[:, 4:8], t2[:, 8:12], t2[:, 12:14]
        kc2 = pl.take(4 * T).rearrange("p (j g t) -> p j g t", j=2, g=2)
        kw = pl.take(2 * 16 * 2 * NCMP).rearrange("p (j l n g) -> p j l n g", j=2, l=16, n=NCMP)
        kwh, kwl = (z.rearrange("p (j l n) -> p j l n", j=2, l=16) for z in split("kw", pl, 2 * 16 * 2 * NCMP))
        grow2 = pl.take(64).rearrange("p (t n) -> p t n", t=NT)
        fv = pl.take(NT * 512).rearrange("p (t n) -> p t n", t=NT)
        vv = pl.take(NT * 256).rearrange("p (t n) -> p t n", t=NT)
        ng = pl.take(NT * 24).rearrange("p (t n) -> p t n", t=NT)
        rt = pl.take(2 * 512).rearrange("p (b n) -> p b n", b=2)
        cb = pl.take(6 * T).rearrange("p (k t) -> p k t", k=6)
        sel8 = pl.take(8 * T).rearrange("p (h t) -> p h t", h=8)
        chid = pl.take(64).rearrange("p (j n) -> p j n", j=2)
        ckc = pl.take(96).rearrange("p (k n) -> p k n", k=3)
        cvr = pl.take(128).rearrange("p (g d) -> p g d", g=2)
        ofox = pl.take(NT * 512).rearrange("p (t n) -> p t n", t=NT)
        onsa = pl.take(NT * 512).rearrange("p (t n) -> p t n", t=NT)
        ott = pl.take(512)
        mg = pl.take(NT * 2 * DM).rearrange("p (t b n) -> p t b n", t=NT, b=2)
        pl = Place(stage)
        pqT = pl.take(16 * T).rearrange("p (k t) -> p k t", k=16)
        keys = pl.take(16 * NKEY).rearrange("p (k n) -> p k n", k=16)
        ps = pl.take(NT * 16 * NKEY).rearrange("p (t k n) -> p t k n", t=NT, k=16)
        top = pl.take(16 * TOPK).rearrange("p (k n) -> p k n", k=16)
        topi = pl.take(16 * TOPK).rearrange("p (k n) -> p k n", k=16)
        best = pl.take(PH * TOPK).rearrange("p (h n) -> p h n", h=PH)
        besti = pl.take(PH * TOPK).rearrange("p (h n) -> p h n", h=PH)
        part = pl.take(2 * PH * TOPK).rearrange("p (k h n) -> p k h n", k=2, h=PH)
        pick = pl.take(PH * TOPK * TOPK).rearrange("p (h k j) -> p h k j", h=PH, k=TOPK)
        cand = pick.rearrange("p h k j -> p h (k j)")
        rout = pl.take(3 * PH * TOPK).rearrange("p (k n) -> p k n", k=3)
        pl = Place(0)
        table = pl.take(T * NKEY).rearrange("p (t j) -> p t j", t=T)
        EU = 4
        rT = columns[:, 0:3 * T].rearrange("p (k t) -> p k t", k=3)
        free = pl.at
        gel = pl.take(2 * T).rearrange("p (r t) -> p r t", r=2)
        ch, cl = (z.rearrange("p (r t) -> p r t", r=2) for z in split("coef", pl, 2 * T))
        pl = Place(free)
        pl.take(2 * T)
        zrow = pl.take(512)
        pl = Place(free)
        hot = pl.take(2 * 2 * 4 * NKEY).rearrange("p (b s q n) -> p b s q n", b=2, s=2, q=4)

        hm3 = hm.rearrange("p t (h d) -> p t h d", h=4)
        relvec = nc.dram_tensor("relvec", [4, P, 512], F32).ap()
        xkeep = nc.dram_tensor("xkeep", [P, NT * DM], F32).ap()
        ahead = nc.dram_tensor("ahead", [AHEAD, P, T], F32).ap()
        ss, ms, rms, rstd = small[:, 0:4], small[:, 4:6], small[:, 6:8], small[:, 8:10]
        lbw = small[:, 10:18]
        hnm, hnr = small[:, 18:26], small[:, 26:34]
        amx = small[:, 36:68].rearrange("p (b n) -> p b n", b=4)
        asum = small[:, 68:100].rearrange("p (b n) -> p b n", b=4)
        ars = small[:, 100:108]
        rc = small[:, 108:124].rearrange("p (q t h) -> p q t h", q=2, t=2)
        den = small[:, 124:132]
        wsum, wrec, wneg = small[:, 134:142], small[:, 142:150], small[:, 150:158]
        zero = small[0:1, 158:159]

        bank_ready = [S(f"bank{b}_ready") for b in range(NB)]

        def got(eng, name):
            n = JOB[name]
            eng.wait_ge(bank_ready[n % NB], n // NB + 1)
            return ring[:, n % NB, :]

        def stepper(eng, chain):
            counts = {}

            def link(ins, name=chain):
                counts[name] = counts.get(name, 0) + 1
                ins.then_inc(S(name), 1)
                eng.wait_ge(S(name), counts[name])
            return link

        block = ctx.enter_context(nc.Block())
        npiece = NPIECE

        @block.sync
        def _(sp):
            sp.dma_start(x, a["x"].rearrange("o (t p) d -> p (o t) d", p=P)).then_inc(S("ld_x"), 16)
            sp.dma_start(cols, a["cols"]).then_inc(S("ld_cols"), 16)
            sp.dma_start(fixc, a["consts"][:, 0:256]).then_inc(S("ld_const"), 16)

            def load(q, b):
                sp.dma_start(raw[:, b, :], a["wstream"][q]).then_inc(S(f"raw{b}"), 16)

            for q in range(min(NR, npiece)):
                load(q, q)
            sp.dma_start(const, a["consts"][:, 256:NCONST]).then_inc(S("ld_masks"), 16)
            rounds = npiece // NR - 1
            if rounds > 0:
                with sp.Fori(0, rounds) as i:
                    for b in range(NR):
                        sp.wait_ge(S("lo_ready"), NR * i + b + 1)
                        load(NR * i + NR + b, b)
            for q in range(NR + max(rounds, 0) * NR, npiece):
                sp.wait_ge(S("lo_ready"), q - NR + 1)
                load(q, q % NR)
            sp.wait_ge(S("x_wanted"), 1)
            sp.dma_start(x.rearrange("p t d -> p (t d)"), xkeep).then_inc(S("x_back"), 16)
            sp.wait_ge(S("out_rows"), 1)
            sp.dma_start(a["out"].rearrange("o (t p) d -> p (o t) d", p=P), x).then_inc(S("stored"), 16)
            sp.wait_ge(S("stored"), 16)

        @block.gpsimd
        def _(pool):
            def remainder(b, q):
                pool.wait_ge(S("hi_ready"), q + 1)
                nc.gpsimd.tensor_tensor(lo[:, b, :], raw[:, b, :], hi[:, b, :].bitcast(F32), ALU.subtract
                                        ).then_inc(S("lo_ready"), 1)

            with pool.Fori(0, npiece // NR) as i:
                for b in range(NR):
                    remainder(b, NR * i + b)
            for q in range(npiece // NR * NR, npiece):
                remainder(q % NR, q)

        @block.tensor
        def _(pe):
            mm = nc.tensor.matmul

            def bank(name):
                n = JOB[name]
                if n >= NB:
                    _, sem, value = JOBS[n - NB]
                    pe.wait_ge(S(sem), value)
                return ring[:, n % NB, :]

            def done(ins, name):
                ins.then_inc(bank_ready[JOB[name] % NB], 1)

            fences = [0]

            def fence(ins):
                fences[0] += 1
                ins.then_inc(S("pe_fence"), 1)
                pe.wait_ge(S("pe_fence"), fences[0])

            def piece(key, k):
                q = 2 * SLOT_AT[key] + k
                pe.wait_ge(S("lo_ready"), q + 1)
                return q, q % NR

            def mm3(out, w, x, first, last, q=0):
                ins = mm(out, w[0], x[0], start=first, stop=False)
                if q > 0:
                    ins.then_inc(S("piece_free"), 1)
                mm(out, w[0], x[1], start=False, stop=False)
                return mm(out, w[1], x[0], start=False, stop=last)

            def part(b, f):
                return f(hi[:, b, :]), f(lo[:, b, :])

            X2 = (XH, XL)

            def norm_T(k):
                pe.wait_ge(S("xn_ready"), k + 1)
                for c in range(4):
                    b = bank(("xn", k, c)).rearrange("p (c t) -> p c t", c=2)
                    for ci in range(2):
                        for t in range(NT):
                            ins = nc.tensor.transpose(b[:, ci, t * P:(t + 1) * P],
                                                      xn[:, t, (2 * c + ci) * P:(2 * c + ci + 1) * P], ident)
                    done(ins, ("xn", k, c))

            def proj_T(name, key):
                b = bank(name).rearrange("p (k t) -> p k t", k=2)
                for k in range(2):
                    q, r = piece(key, k)
                    for c in range(KC):
                        ins = mm3(b[:, k, :], part(r, lambda z: z[:, c * P:(c + 1) * P]), (XH[:, c, :], XL[:, c, :]),
                                  c == 0, c == KC - 1, q if c == 0 else 0)
                done(ins, name)

            def proj_R(name, key):
                b = bank(name).rearrange("p (t n) -> p t n", t=2)
                (q0, r0), (q1, r1_) = piece(key, 0), piece(key, 1)
                for t in range(NT):
                    tok = slice(t * P, (t + 1) * P)
                    for c in range(KC):
                        k = c % 4
                        q = q0 if (t, c) == (0, 0) else q1 if (t, c) == (1, 4) else 0
                        ins = mm3(b[:, t, :], (XH[:, c, tok], XL[:, c, tok]),
                                  part(r0 if c < 4 else r1_, lambda z: z[:, k * 256:(k + 1) * 256]),
                                  c == 0, c == KC - 1, q)
                done(ins, name)

            def proj_acc(use, keys, src):
                if use > 1:
                    pe.wait_ge(S("acc_free"), use - 1)
                last = 2 * len(keys) - 1
                for i, key in enumerate(keys):
                    for k in range(2):
                        c = 2 * i + k
                        q, r = piece(key, k)
                        for t in range(NT):
                            for n in range(2):
                                tok = slice(t * P, (t + 1) * P)
                                ins = mm3(acc[:, t, n, :], (src[0][:, c, tok], src[1][:, c, tok]),
                                          part(r, lambda z: z[:, n * 512:(n + 1) * 512]), c == 0, c == last,
                                          q if (t, n) == (0, 0) else 0)
                ins.then_inc(S("acc_ready"), 1)

            def gate_rows(name, w, n):
                b = bank(name)[:, 0:2 * n].rearrange("p (t n) -> p t n", t=2)
                for t in range(NT):
                    for c in range(KC):
                        tok = slice(t * P, (t + 1) * P)
                        ins = mm3(b[:, t, :], (XH[:, c, tok], XL[:, c, tok]), (w[0][:, c, :], w[1][:, c, :]),
                                  c == 0, c == KC - 1)
                done(ins, name)

            def rows_to_T(name, src, c0, n=2):
                b = bank(name).rearrange("p (c t) -> p c t", c=2)
                for ci in range(n):
                    for t in range(NT):
                        ins = nc.tensor.transpose(b[:, ci, t * P:(t + 1) * P],
                                                  src[:, t, (c0 + ci) * P:(c0 + ci + 1) * P], ident)
                done(ins, name)

            def score(u):
                kind, t, heads, n = UNITS[u]
                b = bank(("score", u))
                tok = slice(t * P, (t + 1) * P)
                for i in EVEN_ODD[len(heads)]:
                    h = heads[i]
                    if i == 1 and kind in ("moba", "fox"):
                        fence(ins)
                    o = b[:, i * n:(i + 1) * n]
                    r = slice((h % 2) * HD, (h % 2) * HD + HD)
                    if kind == "moba":
                        ins = mm(o, TT["aq"][r, h // 2, tok], TT["ak"][r, h // 2, 0:n], start=True, stop=True)
                    elif kind == "cross":
                        ins = mm(o, cqT[:, h, tok], ckT[:, h, :], start=True, stop=True)
                    elif kind == "fox":
                        mm(o, fqT[r, h // 2, tok], fkT[r, h // 2, 0:n], start=True, stop=False)
                        e = slice((h % 2) * HD, (h % 2) * HD + 8)
                        mm(o, cb[e, 4, tok], sel8[e, h, 0:n], start=False, stop=False)
                        ins = mm(o, sel8[e, h, 0:P], cb[e, 5, 0:n], start=False, stop=True)
                    else:
                        g, hp = h // 4, h % 4
                        r = slice(g * HD, g * HD + HD)
                        if kind == "cmp":
                            k = ckc[r, 2, g * NCMP:(g + 1) * NCMP]
                        else:
                            k = kkT[r, 0 if kind == "slc" else 1, 0:n]
                        ins = mm(o, nqT[r, hp, tok], k, start=True, stop=True)
                done(ins, ("score", u))

            def turn(u):
                kind, t, heads, n = UNITS[u]
                b = bank(("turn", u))
                pe.wait_ge(S("att_exp"), u + 1)
                k = min(n, P)
                for i in range(len(heads) * n // k):
                    ins = nc.tensor.transpose(b[0:k, i * P:(i + 1) * P], attP[:, u % 2, i * k:(i + 1) * k], ident)
                done(ins, ("turn", u))

            def pv(u):
                kind, t, heads, n = UNITS[u]
                b = bank(("pv", u))
                pe.wait_ge(S("att_turned"), u + 1)
                k = min(n, P)
                nk = n // k
                d = P if kind == "cross" else HD
                for i, h in enumerate(heads):
                    for j in range(nk):
                        if kind == "moba":
                            v = RR["av"][:, j, h * HD:(h + 1) * HD]
                        elif kind == "cross":
                            v = cv[:, j, h * P:(h + 1) * P]
                        elif kind == "fox":
                            v = fv[:, j, h * HD:(h + 1) * HD]
                        elif kind == "cmp":
                            v = cvr[0:NCMP, h // 4, :]
                        else:
                            at = (0 if kind == "slc" else P) + (h // 4) * HD
                            v = vv[:, j, at:at + HD]
                        ins = mm(b[:, i * d:(i + 1) * d], attT[0:k, u % 2, (i * nk + j) * P:(i * nk + j + 1) * P], v,
                                 start=j == 0, stop=j == nk - 1)
                done(ins, ("pv", u))

            def attention(units, u0):
                for i in range(len(units) + 2):
                    if i < len(units):
                        score(u0 + i)
                    if 1 <= i <= len(units):
                        turn(u0 + i - 1)
                    if i >= 2:
                        pv(u0 + i - 2)

            pe.wait_ge(S("ld_const"), 16)
            norm_T(0)
            pe.wait_ge(S("xT_ready"), 4)
            pe.wait_ge(S("gw_split"), 1)
            gw1 = tuple(z[:, 0:64].rearrange("p (c n) -> p c n", c=KC) for z in (gwh, gwl))
            gate_rows(("gate",), gw1, 8)
            pe.wait_ge(S("grow_copied"), 1)
            b = bank(("gateT",)).rearrange("p (k t) -> p k t", k=2)
            for k in range(2):
                for t in range(NT):
                    ins = nc.tensor.transpose(b[0:4, k, t * P:(t + 1) * P], grow[:, t, 4 * k:4 * k + 4], ident)
            done(ins, ("gateT",))
            for i in range(len(T1)):
                proj_T(("T1", i), ("T1", i))
            for i in range(len(R1)):
                proj_R(("R1", i), ("R1", i))
            norm_T(1)

            pe.wait_ge(S("rel_ready"), 1)
            done(mm(bank(("bias",))[0:4, :], C("rel", 0, 4)[0:33], K("oh")[0:33], start=True, stop=True), ("bias",))
            pe.wait_ge(S("ml_rows"), 1)
            pe.wait_ge(S("ml_em"), 1)
            b = bank(("mgT",))
            for q in range(2):
                for t in range(NT):
                    i = 2 * q + t
                    ins = nc.tensor.transpose(b[:, 4 * i:4 * i + 4], gi[0:4, 2 + q, t * P:(t + 1) * P], ident[0:4, 0:4])
            done(ins, ("mgT",))
            ML = [(0, [0, 1], slice(0, T)), (0, [2, 3], slice(0, T)), (1, [0, 1, 2, 3], slice(P, T))]
            pe.wait_ge(S("sel_ready"), 1)
            for u, (s, heads, tok) in enumerate(ML):
                n = tok.stop - tok.start
                b = bank(("mD", u))
                for i, h in enumerate(heads):
                    ins = mm(b[:, i * n:(i + 1) * n], sel4[0:4, h, :], gi[0:4, 6, tok], start=True, stop=True)
                done(ins, ("mD", u))
                b = bank(("mQK", u))
                for i in EVEN_ODD[len(heads)]:
                    h = heads[i]
                    if i == 1:
                        fence(ins)
                    r = slice((h % 2) * HD, (h % 2) * HD + HD)
                    ins = mm(b[:, i * n:(i + 1) * n], TT["mk"][r, h // 2, s * P:(s + 1) * P], TT["mq"][r, h // 2, tok],
                             start=True, stop=True)
                done(ins, ("mQK", u))
            pe.wait_ge(S("ml_w"), 3)
            pe.wait_ge(S("r1_copied"), 1)
            for t in range(NT):
                b = bank(("mO", t))
                for h in range(4):
                    o = b[:, h * 65:(h + 1) * 65]
                    w0 = WT[:, h // 2, (h % 2) * T + t * P:(h % 2) * T + (t + 1) * P]
                    ins = mm(o, w0, v1[:, 0, h, :], start=True, stop=t == 0)
                    if t:
                        ins = mm(o, WT[:, 2, h * P:(h + 1) * P], v1[:, 1, h, :], start=False, stop=True)
                done(ins, ("mO", t))
            for lv in range(LV):
                pe.wait_ge(S("hg_x"), lv + 1)
                for t in range(NT):
                    b = bank(("hG", lv, t))
                    for h in EVEN_ODD[4]:
                        if h == 1:
                            fence(ins)
                        r = slice((h % 2) * HD, (h % 2) * HD + HD)
                        at = (h // 2) * T + t * P
                        if lv == 0:
                            ks, qs = hk[r, at:at + P], TT["hq"][r, h // 2, t * P:(t + 1) * P]
                        else:
                            ks = qs = hgX[r, lv % 2, at:at + P]
                        ins = mm(b[:, h * P:(h + 1) * P], ks, qs, start=True, stop=True)
                    done(ins, ("hG", lv, t))
                if lv in MEM_AT:
                    pe.wait_ge(S("xT_ready"), 8)
                    (proj_T if MEM_AT[lv][0] == "ck" else proj_R)(MEM_AT[lv], MEM_AT[lv])
            pe.wait_ge(S("hg_x"), LV + 1)
            b = bank(("hOff",))
            for h in EVEN_ODD[4]:
                if h == 1:
                    fence(ins)
                r = slice((h % 2) * HD, (h % 2) * HD + HD)
                at = (h // 2) * T
                ins = mm(b[:, h * P:(h + 1) * P], hgX[r, LV % 2, at:at + P], hgX[r, LV % 2, at + P:at + T],
                         start=True, stop=True)
            done(ins, ("hOff",))
            pe.wait_ge(S("hg_off"), 1)
            for t in range(NT):
                b = bank(("hO", t))
                for h in range(4):
                    o = b[:, h * HD:(h + 1) * HD]
                    ins = mm(o, hgA[:, t, h, :], RR["hi"][:, t, h * HD:(h + 1) * HD], start=True, stop=t == 0)
                    if t:
                        ins = mm(o, hgA[:, 2, h, :], RR["hi"][:, 0, h * HD:(h + 1) * HD], start=False, stop=True)
                done(ins, ("hO", t))
            attention(ATT1, 0)
            for i, (src, sem, v) in enumerate(((hm, "hn_done", 1), (ya, "att_out", len(ATT1)), (ho, "hn_done", 2))):
                pe.wait_ge(S(sem), v)
                rows_to_T(("yT", i), src, 0)
            pe.wait_ge(S("yT_ready"), 3)
            pe.wait_ge(S("conv_split"), 1)
            proj_acc(1, [("mix", i) for i in range(4)], X2)
            norm_T(2)
            pe.wait_ge(S("xT_ready"), 12)
            for i in range(2):
                proj_T(("cq", i), ("cq", i))
            pe.wait_ge(S("cq_copied"), 2)
            attention(ATT2, len(ATT1))
            pe.wait_ge(S("att_out"), len(ATT1) + len(ATT2))
            rows_to_T(("coT", 0), oc, 0)
            rows_to_T(("coT", 1), oc, 2)
            pe.wait_ge(S("coT_ready"), 2)
            proj_acc(2, [("co", i) for i in range(2)], X2)
            norm_T(3)
            pe.wait_ge(S("xT_ready"), 16)
            for f in range(FC):
                proj_T(("up", f), ("up", f))
            pe.wait_ge(S("ffn_hidden"), FC)
            proj_acc(3, [("down", i) for i in range(FC // 2)], (hidh, hidl))
            norm_T(4)
            pe.wait_ge(S("xT_ready"), 20)
            gw2 = tuple(z[:, 64:320].rearrange("p (c n) -> p c n", c=KC) for z in (gwh, gwl))
            gate_rows(("gate2",), gw2, 32)
            pe.wait_ge(S("grow2_copied"), 1)
            b = bank(("gate2T",))
            for t in range(NT):
                ins = nc.tensor.transpose(b[0:8, t * P:(t + 1) * P], grow2[:, t, 0:8], ident)
            done(ins, ("gate2T",))
            T2 = [("fq", 0), ("fq", 1), ("fk", 0), ("fk", 1), ("nq", 0), ("nq", 1), ("kk",)]
            for i, key in enumerate(T2):
                proj_T(("T2", i), key)
            proj_T(("kc",), ("kc",))
            proj_T(("vc",), ("vc",))
            for i in range(2):
                proj_R(("fv", i), ("fv", i))
            proj_R(("vv",), ("vv",))
            pe.wait_ge(S("t2_copied"), 9)
            for i in range(3):
                b = bank(("rope", i)).rearrange("p (k t) -> p k t", k=2)
                for k in range(2):
                    ins = mm(b[:, k, :], K("rot"), t2[:, 8 + 2 * i + k, :], start=True, stop=True)
                done(ins, ("rope", i))
            pe.wait_ge(S("kw_split"), 1)
            for j in range(2):
                b = bank(("chid", j))
                (q0, r0), (q1, r1_) = piece(("cw1", j), 0), piece(("cw1", j), 1)
                for lp in range(16):
                    k = lp % 8
                    ins = mm3(b[:, 0:2 * NCMP], part(r0 if lp < 8 else r1_, lambda z: z[:, k * P:(k + 1) * P]),
                              (kwh[:, j, lp, :], kwl[:, j, lp, :]), lp == 0, lp == 15,
                              q0 if lp == 0 else q1 if lp == 8 else 0)
                done(ins, ("chid", j))
            pe.wait_ge(S("chid_done"), 2)
            done(mm(bank(("ck2",))[:, 0:30], C("w2k", 0, 128), chid[:, 0, 0:30], start=True, stop=True), ("ck2",))
            pe.wait_ge(S("ck2_done"), 1)
            done(mm(bank(("crot",))[:, 0:30], K("rot"), ckc[:, 0, 0:30], start=True, stop=True), ("crot",))
            b = bank(("cv2",))
            for g in range(2):
                ins = mm(b[0:NCMP, g * HD:(g + 1) * HD], chid[:, 1, g * NCMP:(g + 1) * NCMP], C("w2v", 0, 64),
                         start=True, stop=True)
            done(ins, ("cv2",))
            for i in range(8):
                proj_R(("merge", i), ("merge", i))
            pe.wait_ge(S("roped_all"), 1)
            pe.wait_ge(S("fox_rows"), 1)
            pe.wait_ge(S("r2_copied"), 3)
            pe.wait_ge(S("cv2_done"), 1)
            pe.wait_ge(S("cmpk_ready"), 1)
            attention(ATT3, len(ATT1) + len(ATT2))
            pe.wait_ge(S("att_out"), len(UNITS))
            for i in range(4):
                rows_to_T(("ysT", i), ofox if i < 2 else onsa, 2 * (i % 2))
            pe.wait_ge(S("ysT_ready"), 4)
            proj_acc(4, [("branch", i) for i in range(2)], X2)
            proj_acc(5, [("branch", i) for i in range(2, 4)], (XH[:, 4:8], XL[:, 4:8]))
            pe.wait_ge(S("merged"), 1)
            for i in range(4):
                rows_to_T(("mT", i), mg[:, :, 0, :], 2 * i)
            pe.wait_ge(S("mT_ready"), 4)
            proj_acc(6, [("wout", i) for i in range(4)], X2)
            norm_T(5)
            pe.wait_ge(S("xT_ready"), 24)
            for i in range(8):
                proj_T(("pq", i), ("pq", i))
            pe.wait_ge(S("pq_copied"), 8)
            pe.wait_ge(S("ld_keys"), 16)
            for t in range(NT):
                for q in range(4):
                    b = bank(("ps", t, q))
                    for k in range(4):
                        ins = mm(b[:, k * P:(k + 1) * P], pqT[:, 4 * q + k, t * P:(t + 1) * P], keys[:, 4 * q + k, :],
                                 start=True, stop=True)
                    done(ins, ("ps", t, q))
            pe.wait_ge(S("acc_free"), 6)

            def hidden_ahead(n, k, chunks=range(KC)):
                r = (E0 + k) % NR
                if chunks[0] == 0:
                    pe.wait_ge(S("lo_ready"), E0 + n + 1)
                    pe.wait_ge(S("early_gelu"), n + 1)
                o = acc[:, k % 2, 0, 0:T]
                for c in chunks:
                    w = part(r, lambda z: z[:, c * P:(c + 1) * P])
                    ins = mm(o, w[0], XH[:, c, :], start=c == 0, stop=False)
                    if c == 0:
                        ins.then_inc(S("piece_free"), 1)
                    mm(o, w[0], XL[:, c, :], start=False, stop=False)
                    ins = mm(o, w[1], XH[:, c, :], start=False, stop=c == KC - 1)
                if chunks[-1] == KC - 1:
                    ins.then_inc(S("early_hidden"), 1)

            pe.nop().then_inc(S("early_gelu"), 2)
            for t in range(NT):
                n0 = sum(AHEAD_TOPK[:t])
                with pe.Fori(n0 // 4, (n0 + AHEAD_TOPK[t]) // 4) as i:
                    for k in range(4):
                        hidden_ahead(4 * i + k, k)
                b = bank(("rT", t))
                pe.wait_ge(S("routes"), t + 1)
                for k in range(3):
                    ins = nc.tensor.transpose(b[:, k * P:(k + 1) * P], rout[:, k, :], ident)
                done(ins, ("rT", t))
            n0 = len(JOBS)
            pe.wait_ge(S("rT_copied"), 2)
            for q in range(NB):
                _, sem, value = JOBS[n0 - NB + q]
                if sem != "pad_free":
                    pe.wait_ge(S(sem), value)
            pe.nop().then_inc(S("hot_used"), 2)
            with pe.Fori(0, AHEAD_TABLE // 4) as i:
                for j in range(4):
                    for q in range(NB):
                        g = NB * (4 * i + j) + q
                        pe.wait_ge(S("hot_ready"), g + 1)
                        pe.wait_ge(S("tabled"), g - NB + 5)
                        for k in range(4):
                            ins = mm(ring[:, q, k * NKEY:(k + 1) * NKEY], hot[:, q % 2, 0, k, :],
                                     hot[:, q % 2, 1, k, :], start=True, stop=True)
                        ins.then_inc(S("hot_used"), 1)
                        hidden_ahead(4 * i + (sum(AHEAD_TOPK) + j), j, range(2 * q, 2 * q + 2))
            pe.wait_ge(S("early_gelu"), AHEAD + 2)
            pe.wait_ge(S("zrow_ready"), 1)
            for t in range(NT):
                for n in range(2):
                    ins = mm(acc[:, t, n, :], zrow[0:1, 0:P], zrow[0:1, 0:512], start=True, stop=False)
            ins.then_inc(S("ex_used"), 2)
            pe.wait_ge(S("tabled"), T // 4 + 4)

            def hidden(q, r, b):
                pe.wait_ge(S("lo_ready"), q + 1)
                for c in range(KC):
                    w = part(r, lambda z: z[:, c * P:(c + 1) * P])
                    ins = mm(ring[:, b, 0:T], w[0], XH[:, c, :], start=c == 0, stop=False)
                    if c == 0:
                        ins.then_inc(S("piece_free"), 1)
                    mm(ring[:, b, 0:T], w[0], XL[:, c, :], start=False, stop=False)
                    ins = mm(ring[:, b, 0:T], w[1], XH[:, c, :], start=False, stop=c == KC - 1)
                ins.then_inc(S("ex_hidden"), 1)

            def spread(n, b, q, r, stop=False):
                pe.wait_ge(S("lo_ready"), q + 1)
                pe.wait_ge(S("ex_coef"), n + 3)
                for t in range(NT):
                    tok = slice(t * P, (t + 1) * P)
                    for n_ in range(2):
                        v = part(r, lambda z: z[:, n_ * 512:(n_ + 1) * 512])
                        o = acc[:, t, n_, :]
                        ins = mm(o, ch[:, b % 2, tok], v[0], start=False, stop=False, skip_group_check=True)
                        if (t, n_) == (0, 0):
                            ins.then_inc(S("piece_free"), 1)
                        mm(o, ch[:, b % 2, tok], v[1], start=False, stop=False, skip_group_check=True)
                        ins = mm(o, cl[:, b % 2, tok], v[0], start=False, stop=stop)
                ins.then_inc(S("acc_ready" if stop else "ex_used"), 1)

            with pe.Fori(0, AHEAD // EU) as i:
                for b in range(EU):
                    spread(EU * i + b, b, EU * i + (EB + b), (EB + b) % NR)
            hidden(EC, EC % NR, 0)
            with pe.Fori(0, REST // EU - 1) as i:
                for b in range(EU):
                    q = 2 * b + 1
                    hidden(EC + q + 2 * EU * i, (EC + q) % NR, (b + 1) % EU)
                    spread(EU * i + (AHEAD + b), b, EC + q + 1 + 2 * EU * i, (EC + q + 1) % NR)
            for n in range(NKEY - EU, NKEY):
                if n < NKEY - 1:
                    hidden(piece_u(n + 1), piece_u(n + 1) % NR, (n + 1) % EU)
                spread(n, n % EU, piece_v(n), piece_v(n) % NR, stop=n == NKEY - 1)

        @block.scalar
        def _(act):
            link = stepper(act, "act_step")
            A = nc.scalar.activation

            def squares(src, lo, resid=0):
                for t in range(NT):
                    if resid:
                        act.wait_ge(S("resid" if t else "resid_first"), resid)
                    link(A(squared, src[:, t, :], ACT.Square, accum_out=ss[:, lo + t:lo + t + 1]),
                         "sumsq" if t == NT - 1 else "act_step")

            def root(k):
                link(A(small[:, 159:160], fixc[:, 0:1], ACT.Sqrt))
                act.wait_ge(S("meansq"), k)
                link(A(rms, ms, ACT.Sqrt), "rms")

            def round_piece(q, r):
                act.wait_ge(S(f"raw{r}"), 16 * (q // NR + 1) if isinstance(q, int) else q[1])
                if not isinstance(q, int) or q >= NR:
                    act.wait_ge(S("piece_free"), (q if isinstance(q, int) else q[0]) - NR + 1)
                A(hi[:, r, :], raw[:, r, :], ACT.Copy).then_inc(S("hi_ready"), 1)

            def feed(key):
                q = 2 * SLOT_AT[key] + 2
                for q in (q, q + 1):
                    if q < npiece:
                        round_piece(q, q % NR)

            def norm_T(k, g):
                for c in range(4):
                    b = got(act, ("xn", k, c)).rearrange("p (c t) -> p c t", c=2)
                    A(XH[:, 2 * c, :], b[:, 0, :], ACT.Copy, scale=C(g, 2 * c))
                    link(A(XH[:, 2 * c + 1, :], b[:, 1, :], ACT.Copy, scale=C(g, 2 * c + 1)), "xh_ready")

            def turned(name, c):
                b = got(act, name).rearrange("p (c t) -> p c t", c=2)
                link(A(XH[:, c:c + 2, :], b, ACT.Copy), "xh_ready")

            def acc_squares(use):
                act.wait_ge(S("acc_ready"), use)
                for t in range(NT):
                    link(A(squared, accf[:, t, :], ACT.Square, accum_out=ss[:, t:t + 1]), "sumsq" if t else "act_step")

            def copy_job(name, dst, sem, func=ACT.Copy):
                b = got(act, name)
                link(A(dst, b[:, 0:dst.free_size()] if dst.ndim == 2 else
                       b.rearrange("p (k t) -> p k t", k=2)[:, :, 0:dst.shape[2]], func), sem)

            def attention(units, u0):
                for i in range(len(units) + 1):
                    if i < len(units):
                        u = u0 + i
                        kind, t, heads, n = UNITS[u]
                        act.wait_ge(S("att_max"), u + 1)
                        for k in range(len(heads)):
                            ins = A(attP[:, u % 2, k * n:(k + 1) * n], attS[:, u % 2, k * n:(k + 1) * n], ACT.Exp,
                                    bias=amx[:, u % 4, k:k + 1], accum_out=asum[:, u % 4, k:k + 1])
                        link(ins, "att_exp")
                    if i >= 1:
                        u = u0 + i - 1
                        kind, t, heads, n = UNITS[u]
                        b = got(act, ("turn", u))
                        k = min(n, P)
                        m = len(heads) * n // k * P
                        if u >= 2:
                            got(act, ("pv", u - 2))
                        link(A(attT[0:k, u % 2, 0:m], b[0:k, 0:m], ACT.Copy), "att_turned")

            act.dma_start(rows1, bass.AP(a["rows1"].tensor, 0, [[0, P], [1, 7 * GW]])).then_inc(S("ld_rows1"), 16)

            def load_gain(k, dst):
                act.dma_start(dst, bass.AP(a["gains"].tensor, k * DM, [[0, P], [1, DM]])).then_inc(S("ld_gain"), 16)

            act.wait_ge(S("ld_x"), 16)
            act.dma_start(memr, a["mem"].rearrange("o (t p) d -> p (o t) d", p=P)).then_inc(S("ld_mem"), 16)
            squares(x, 0)
            act.wait_ge(S("ld_const"), 16)
            act.wait_ge(S("ld_cols"), 16)
            link(A(gwh, cols[:, COLS["wg1"][0]:COLS["wg1"][0] + 320], ACT.Copy), "gwh_ready")
            root(1)
            for q in range(2):
                round_piece(q, q)
            norm_T(0, "g_mix")
            act.wait_ge(S("ld_mem"), 16)
            squares(memr, 2)
            root(2)
            link(A(grow, got(act, ("gate",))[:, 0:16].rearrange("p (t n) -> p t n", t=2), ACT.Copy), "grow_copied")
            b = got(act, ("gateT",)).rearrange("p (k t) -> p k t", k=2)
            link(A(gi[0:4, 0, :], b[0:4, 0, :], ACT.Identity, bias=C("bi")[0:4]))
            link(A(gi[0:4, 1, :], b[0:4, 1, :], ACT.Identity, bias=C("bf")[0:4]), "gates_copied")
            link(A(gi[0:4, 2, :], gi[0:4, 1, :], ACT.Abs))
            link(A(gi[0:4, 2, :], gi[0:4, 2, :], ACT.Exp, scale=-1.0))
            link(A(gi[0:4, 2, :], gi[0:4, 2, :], ACT.Ln, bias=1.0), "ml_ln")
            for i, (name, _) in enumerate(T1):
                feed(("T1", i))
                b = got(act, ("T1", i)).rearrange("p (k t) -> p k t", k=2)
                func = {"hf": ACT.Sigmoid, "hq": ACT.Silu}.get(name, ACT.Identity)
                A(TT[name][:, 0, :], b[:, 0, :], func, bias=C("b1", 2 * i))
                link(A(TT[name][:, 1, :], b[:, 1, :], func, bias=C("b1", 2 * i + 1)), "t1_copied")
            act.wait_ge(S("lb_shift"), 1)
            link(A(lbw[:, 2:4], lbw[:, 0:2], ACT.Exp), "lb_exp")
            act.wait_ge(S("hg_f"), 1)
            link(A(hgX[:, 1, :], hgX[:, 0, :], ACT.Ln), "hg_ln")
            act.wait_ge(S("ml_rows"), 1)
            link(A(gi[0:4, 3, :], gi[0:4, 7, :], ACT.Exp, scale=-1.0), "ml_em")
            for i in range(len(R1)):
                feed(("R1", i))
            norm_T(1, "g_mem")
            link(A(relv[0:4, :], got(act, ("bias",))[0:4, :], ACT.Copy), "relvec_copied")
            act.dma_start(relvec, relv[0:4, :].unsqueeze(1).to_broadcast([4, P, 512])).then_inc(S("relvec_out"), 16)
            act.wait_ge(S("relvec_out"), 16)
            for h in range(4):
                for tt, tile_, n in ((0, rel0, 128), (1, rel1, 256)):
                    act.dma_start(tile_[:, h, :], bass.AP(relvec.tensor, h * P * 512 + 255 - tt * P, [[511, P], [1, n]])
                                  ).then_inc(S("ld_rel"), 16)
            load_gain(0, gain)
            act.wait_ge(S("r1_copied"), 5)
            link(A(RR["mo"], RR["mo"], ACT.Sigmoid))
            link(A(RR["hg"], RR["hg"], ACT.Silu), "gates_ready")
            for u in range(3):
                act.wait_ge(S("ml_arg"), u + 1)
                link(A(EW[:, u % 2, :], EW[:, u % 2, :], ACT.Exp), "ml_exp")
            for lv in range(1, LV + 1):
                act.wait_ge(S("hg_d"), lv)
                link(A(hgD[:, lv % 2, :], hgD[:, lv % 2, :], ACT.Exp), "hg_e")
                if lv - 2 in MEM_AT:
                    kind, i = name = MEM_AT[lv - 2]
                    feed(name)
                    copy_job(name, ckT[:, 2 * i:2 * i + 2, :] if kind == "ck" else cv[:, :, 256 * i:256 * i + 256],
                             "ckv_copied")
            for k in range(2):
                act.wait_ge(S("hn_ms"), k + 1)
                link(A(hnr, hnm, ACT.Sqrt), "hn_rt")
            attention(ATT1, 0)
            for i in range(3):
                turned(("yT", i), (0, 4, 6)[i])

            for i in range(4):
                feed(("mix", i))
            acc_squares(1)
            root(3)
            squares(x, 0, 1)
            load_gain(1, gain)
            root(4)
            norm_T(2, "g_cross")
            for i in range(2):
                feed(("cq", i))
                copy_job(("cq", i), cqT[:, 2 * i:2 * i + 2, :], "cq_copied")
            attention(ATT2, len(ATT1))
            for i in range(2):
                turned(("coT", i), 2 * i)
            for i in range(2):
                feed(("co", i))
            acc_squares(2)
            root(5)
            squares(x, 0, 2)
            load_gain(2, gain)
            root(6)
            norm_T(3, "g_ffn")
            act.wait_ge(S("gpad_zero"), 1)
            for f in range(FC + 1):
                if f < FC:
                    feed(("up", f))
                    b = got(act, ("up", f))
                    link(A(gpad[:, f % 2, 2:258], b[:, 0:T], ACT.Copy), "ff_gate")
                if f:
                    act.wait_ge(S("ff_conv"), f)
                    g = (f - 1) % 2
                    link(A(fa[:, g, :], fa[:, g, :], ACT.Silu), "ff_silu")
            for i in range(FC // 2):
                feed(("down", i))
            acc_squares(3)
            root(7)
            squares(x, 0, 3)
            root(8)
            norm_T(4, "g_mix2")
            link(A(grow2, got(act, ("gate2",))[:, 0:64].rearrange("p (t n) -> p t n", t=2), ACT.Copy), "grow2_copied")
            link(A(ng, grow2[:, :, 8:32], ACT.Sigmoid), "ng_ready")
            link(A(cb[0:8, 0, :], got(act, ("gate2T",))[0:8, 0:T], ACT.Identity, bias=C("foxb")[0:8]), "flog_copied")
            link(A(cb[0:8, 1, :], cb[0:8, 0, :], ACT.Abs))
            link(A(cb[0:8, 1, :], cb[0:8, 1, :], ACT.Exp, scale=-1.0))
            link(A(cb[0:8, 1, :], cb[0:8, 1, :], ACT.Ln, bias=1.0), "fox_ln")
            T2 = [("fq", 0), ("fq", 1), ("fk", 0), ("fk", 1), ("nq", 0), ("nq", 1), ("kk",)]
            for i in range(7):
                feed(T2[i])
                copy_job(("T2", i), t2[:, 2 * i:2 * i + 2, :], "t2_copied")
            for j, name in enumerate((("kc",), ("vc",))):
                feed(name)
                b = got(act, name).rearrange("p (k t) -> p k t", k=2)
                A(kc2[0:HD, j, :, :], b[0:HD], ACT.Copy)
                A(kc2[HD:P, j, :, T - 1:T], b[HD:P, :, T - 1:T], ACT.Copy)
                link(A(kc2[HD:P, j, :, 0:T - 1], b[HD:P, :, 1:T], ACT.Copy), "t2_copied")
            for i in range(2):
                feed(("fv", i))
                copy_job(("fv", i), fv[:, :, 256 * i:256 * i + 256], "r2_copied")
            feed(("vv",))
            copy_job(("vv",), vv, "r2_copied")
            for j in range(2):
                feed(("cw1", j))
                b = got(act, ("chid", j))
                link(A(chid[:, j, 0:30].rearrange("p (g n) -> p n g", g=2), b[:, 0:30].rearrange("p (n g) -> p n g", g=2), ACT.Gelu), "chid_done")
            link(A(ckc[:, 0, 0:30], got(act, ("ck2",))[:, 0:30], ACT.Copy), "ck2_done")
            link(A(cvr[0:NCMP].rearrange("p g d -> p (g d)"), got(act, ("cv2",))[0:NCMP, 0:P], ACT.Copy), "cv2_done")
            for i in range(8):
                feed(("merge", i))
                b = got(act, ("merge", i)).rearrange("p (t n) -> p t n", t=2)
                link(A(mg[:, :, i // 4, (i % 4) * 256:(i % 4) * 256 + 256], b, ACT.Sigmoid), "merge_gated")
            attention(ATT3, len(ATT1) + len(ATT2))
            for i in range(4):
                turned(("ysT", i), 2 * i)
            for i in range(4):
                feed(("branch", i))
            for i in range(4):
                turned(("mT", i), 2 * i)
            act.dma_start(keys.rearrange("p k n -> p (k n)"), a["keys"]).then_inc(S("ld_keys"), 16)
            for i in range(4):
                feed(("wout", i))
            squares(x, 0, 4)
            root(9)
            norm_T(5, "g_ffn2")
            act.dma_start(xkeep, x.rearrange("p t d -> p (t d)")).then_inc(S("x_out"), 16)
            for i in range(8):
                feed(("pq", i))
                copy_job(("pq", i), pqT[:, 2 * i:2 * i + 2, :], "pq_copied")
            for t in range(NT):
                for q in range(4):
                    b = got(act, ("ps", t, q))
                    link(A(ps[:, t, 4 * q:4 * q + 4, :].rearrange("p k n -> p (k n)"), b, ACT.Copy), "ps_copied")

            def activate_ahead(n0, k, i):
                m = n0 + k
                q = E0 + m + 2
                round_piece((q + 4 * i, 16 * (q // NR + 1) + 16 * i), q % NR)
                n = m + 4 * i
                act.wait_ge(S("early_hidden"), n + 1)
                act.wait_ge(S(f"early_out{k % 2}"), 16 * (m // 2 + 1) + 32 * i)
                A(early[:, k % 2, :], acc[:, k % 2, 0, 0:T], ACT.Gelu).then_inc(S("early_gelu"), 1)
                act.wait_ge(S("early_gelu"), n + 3)
                act.dma_start(ahead[bass.ds(n, 1)].rearrange("o p t -> (o p) t"), early[:, k % 2, :]
                              ).then_inc(S(f"early_out{k % 2}"), 16)

            for k in range(2):
                act.nop().then_inc(S(f"early_out{k}"), 16)
            for t in range(NT):
                n0 = sum(AHEAD_TOPK[:t])
                with act.Fori(0, AHEAD_TOPK[t] // 4) as i:
                    for k in range(4):
                        activate_ahead(n0, k, i)
                act.wait_ge(S("best_ready"), t + 1)
                link(A(best, best, ACT.Exp), "best_exp")
            act.wait_ge(S("rT_copied"), 2)
            act.wait_ge(S("hot_ready"), 1)
            act.wait_ge(S("x_out"), 16)
            act.nop().then_inc(S("tabled"), 4)
            with act.Fori(0, AHEAD_TABLE // 4) as i:
                for j in range(4):
                    for q in range(NB):
                        g = 4 * NB * i + (NB * j + q)
                        act.wait_ge(S("hot_used"), g + 3)
                        A(table[:, bass.ds(4 * g, 4), :], ring[:, q, :].rearrange("p (t n) -> p t n", t=4),
                          ACT.Copy).then_inc(S("tabled"), 1)
                    activate_ahead(sum(AHEAD_TOPK), j, i)

            def activate(n, b):
                act.wait_ge(S("ex_hidden"), n - (AHEAD - 1))
                act.wait_ge(S("ex_coef"), n + 1)
                A(gel[:, b % 2, :], ring[:, b, 0:T], ACT.Gelu).then_inc(S("ex_gelu"), 1)

            for k in range(2):
                act.wait_ge(S(f"early_out{k}"), 16 * (AHEAD // 2 + 1))
            act.wait_ge(S("hot_used"), T // 4 + 2)
            with act.Fori(0, AHEAD // EU) as i:
                for b in range(EU):
                    act.wait_ge(S("ex_coef"), EU * i + b + 1)
                    act.dma_start(gel[:, b % 2, :], ahead[bass.ds(EU * i + b, 1)].rearrange("o p t -> (o p) t")
                                  ).then_inc(S(f"gel_in{b % 2}"), 16)
                    q = EB + b + 2
                    round_piece((q + EU * i, 16 * (q // NR + 1) + 16 * (EU // NR) * i), q % NR)
            with act.Fori(0, REST // EU - 1) as i:
                for b in range(EU):
                    q = EC + 2 * b + 2
                    round_piece((q + 2 * EU * i, 16 * (q // NR + 1) + 16 * (2 * EU // NR) * i), q % NR)
                    activate(EU * i + (AHEAD + b), b)
                    q += 1
                    round_piece((q + 2 * EU * i, 16 * (q // NR + 1) + 16 * (2 * EU // NR) * i), q % NR)
            for n in range(NKEY - EU, NKEY):
                q = EC + 2 * (n - AHEAD) + 2
                if n < NKEY - 1:
                    round_piece(q, q % NR)
                activate(n, n % EU)
                if n < NKEY - 1:
                    round_piece(q + 1, (q + 1) % NR)
            act.wait_ge(S("x_wanted"), 1)
            load_gain(3, gain)
            squares(x, 0, 5)
            root(10)

        @block.vector
        def _(dve):
            link = stepper(dve, "dve_step")
            V = nc.vector
            tt, ts, stt = V.tensor_tensor, V.tensor_scalar, V.scalar_tensor_tensor

            def inv_root(k, lo, width=DM):
                dve.wait_ge(S("sumsq"), k)
                link(ts(ms, ss[:, lo:lo + 2], 1.0 / width, EPS, ALU.mult, ALU.add), "meansq")
                dve.wait_ge(S("rms"), k)
                link(V.reciprocal(rstd, rms))

            def normed(src):
                ts(xn[:, 0, :], src[:, 0, :], rstd[:, 0:1], None, ALU.mult)
                link(ts(xn[:, 1, :], src[:, 1, :], rstd[:, 1:2], None, ALU.mult), "xn_ready")

            def rest_norm(k, g):
                for c in range(4):
                    b = got(dve, ("xn", k, c)).rearrange("p (c t) -> p c t", c=2)
                    rest[0] += 1
                    dve.wait_ge(S("xh_ready"), rest[0])
                    for ci in range(2):
                        ins = stt(out=XL[:, 2 * c + ci, :], in0=b[:, ci, :], scalar=C(g, 2 * c + ci),
                                  in1=XH[:, 2 * c + ci, :].bitcast(F32), op0=ALU.mult, op1=ALU.subtract)
                    link(ins, "xT_ready")

            def rest_turned(name, c, sem):
                b = got(dve, name).rearrange("p (c t) -> p c t", c=2)
                rest[0] += 1
                dve.wait_ge(S("xh_ready"), rest[0])
                link(tt(XL[:, c:c + 2, :], b, XH[:, c:c + 2, :].bitcast(F32), ALU.subtract), sem)

            rest = [0]

            def post_norm(k, use):
                inv_root(k, 0)
                dve.wait_ge(S("ld_gain"), 16 * use)
                for t in range(NT):
                    link(stt(out=tmp, in0=accf[:, t, :], scalar=rstd[:, t:t + 1], in1=gain, op0=ALU.mult, op1=ALU.mult),
                         "acc_free" if t == NT - 1 else "dve_step")
                    link(tt(x[:, t, :], x[:, t, :], tmp, ALU.add), "resid" if t else "resid_first")

            def attention(units, u0):
                for i in range(len(units) + 2):
                    if i < len(units):
                        u = u0 + i
                        kind, t, heads, n = UNITS[u]
                        m = len(heads)
                        b = got(dve, ("score", u))[:, 0:m * n].rearrange("p (h s) -> p h s", h=m)
                        if u >= 2:
                            dve.wait_ge(S("att_exp"), u - 1)
                        o = attS[:, u % 2, 0:m * n].rearrange("p (h s) -> p h s", h=m)
                        scale = P ** -0.5 if kind == "cross" else HD ** -0.5
                        if kind == "moba":
                            bias = (rel0 if t == 0 else rel1)[:, heads[0]:heads[0] + m, :]
                        elif kind == "cmp":
                            bias = K("maskC", t * NCMP, NCMP).unsqueeze(1).to_broadcast([P, m, n])
                        else:
                            bias = K("maskR", t * 256, n).unsqueeze(1).to_broadcast([P, m, n])
                        if kind == "cross":
                            link(ts(o, b, scale, None, ALU.mult), "att_scaled")
                        else:
                            link(stt(out=o, in0=b, scalar=scale, in1=bias, op0=ALU.mult, op1=ALU.add), "att_scaled")
                        link(V.tensor_reduce(amx[:, u % 4, 0:m], o, AX.X, ALU.max, negate=True), "att_max")
                    if i >= 2:
                        u = u0 + i - 2
                        kind, t, heads, n = UNITS[u]
                        m = len(heads)
                        d = P if kind == "cross" else HD
                        dve.wait_ge(S("att_exp"), u + 1)
                        link(V.reciprocal(ars[:, 0:m], asum[:, u % 4, 0:m]))
                        if kind in ("cmp", "slc", "win"):
                            g = ng[:, t, :].rearrange("p (h k) -> p h k", k=3)[:, heads[0]:heads[0] + m,
                                                                              ("cmp", "slc", "win").index(kind)]
                            link(tt(ars[:, 0:m], ars[:, 0:m], g, ALU.mult))
                            if kind == "cmp":
                                link(ts(ars[:, 0:m], ars[:, 0:m], K("valid", t, 1), None, ALU.mult))
                        b = got(dve, ("pv", u))[:, 0:m * d].rearrange("p (h d) -> p h d", h=m)
                        r = ars[:, 0:m].unsqueeze(2).to_broadcast([P, m, d])
                        at = slice(heads[0] * d, (heads[0] + m) * d)
                        dst = {"moba": ya, "cross": oc, "fox": ofox}.get(kind, onsa)[:, t, at]
                        dst3 = dst.rearrange("p (h d) -> p h d", h=m)
                        if kind in ("slc", "win"):
                            o = ott[:, 0:m * d]
                            link(tt(o.rearrange("p (h d) -> p h d", h=m), b, r, ALU.mult))
                            link(tt(dst, dst, o, ALU.add), "att_out")
                        else:
                            link(tt(dst3, b, r, ALU.mult), "att_out")

            def head_norm(k, src, g, gates):
                s8 = src.rearrange("p t (h d) -> p (t h) d", h=4)
                sq = tmp[:, 0:512].rearrange("p (k d) -> p k d", k=8)
                link(tt(sq, s8, s8, ALU.mult))
                link(V.tensor_reduce(hnm, sq, AX.X, ALU.add))
                link(ts(hnm, hnm, 1.0 / HD, EPS, ALU.mult, ALU.add), "hn_ms")
                dve.wait_ge(S("hn_rt"), k)
                link(V.reciprocal(hnm, hnr))
                link(tt(s8, s8, hnm.unsqueeze(2).to_broadcast([P, 8, HD]), ALU.mult))
                link(tt(src, src, g.unsqueeze(1).to_broadcast([P, NT, GW]), ALU.mult))
                link(tt(src, src, gates, ALU.mult), "hn_done")

            dve.wait_ge(S("ld_cols"), 16)
            dve.wait_ge(S("gwh_ready"), 1)
            gw = cols[:, COLS["wg1"][0]:COLS["wg1"][0] + 320]
            link(tt(gwl, gw, gwh.bitcast(F32), ALU.subtract), "gw_split")
            inv_root(1, 0)
            normed(x)
            rest_norm(0, "g_mix")
            inv_root(2, 2)
            normed(memr)
            dve.wait_ge(S("ld_const"), 16)
            dve.wait_ge(S("ld_masks"), 16)
            link(V.memset(C("rel", 0, 4)[32:33], NEG), "rel_ready")
            link(V.tensor_copy(sel4[0:4], ident[0:4, 0:4].unsqueeze(2).to_broadcast([4, 4, P])), "sel_ready")
            link(tt(lbw[:, 0:2], C("lb", 0, 2), C("lb", 0, 2), ALU.subtract), "lb_shift")
            row = [gi[0:4, k, :] for k in range(8)]
            dve.wait_ge(S("ml_ln"), 1)
            link(ts(row[3], row[1], 0.0, None, ALU.min))
            link(tt(row[3], row[3], row[2], ALU.subtract))
            link(V.memset(row[7], 1.0))
            link(V.tensor_tensor_scan(row[4], row[7], row[3], 0.0, ALU.mult, ALU.add))
            link(tt(row[2], row[0], row[4], ALU.subtract))
            link(V.memset(row[7], 0.0))
            link(V.tensor_tensor_scan(row[5], row[7], row[2], 0.0, ALU.max, ALU.max))
            link(ts(row[6], row[5], -1.0, None, ALU.mult))
            link(tt(row[7], row[4], row[5], ALU.add), "ml_rows")
            dve.wait_ge(S("lb_exp"), 1)
            link(V.reciprocal(lbw[:, 4:6], lbw[:, 2:4]))
            link(tt(lbw[:, 4:6], lbw[:, 4:6], lbw[:, 2:4], ALU.mult))
            link(tt(lbw[:, 6:8], lbw[:, 4:6], lbw[:, 4:6], ALU.subtract))
            link(ts(lbw[:, 0:2], lbw[:, 6:8], -1.0, 1.0, ALU.mult, ALU.add))
            dve.wait_ge(S("t1_copied"), 2)
            g = TT["hf"].rearrange("p c t -> p (c t)")
            hq = TT["hq"].rearrange("p c t -> p (c t)")
            for c in range(2):
                link(ts(TT["hf"][:, c, :], TT["hf"][:, c, :], lbw[:, c:c + 1], lbw[:, 6 + c:7 + c], ALU.mult, ALU.add))
            link(ts(hgX[:, 0, :], g, 1e-18, None, ALU.max), "hg_f")
            link(ts(hk, g, -1.0, 1.0, ALU.mult, ALU.add), "hg_x")
            dve.wait_ge(S("hg_ln"), 1)
            link(V.tensor_tensor_scan(g, K("reset"), hgX[:, 1, :], 0.0, ALU.mult, ALU.add))
            dve.wait_ge(S("t1_copied"), 9)
            link(V.memset(pad[:, :, 0:2], 0.0))
            link(tt(pad[:, :, 2:258], TT["cc"], TT["ch"], ALU.mult))
            for c in range(2):
                o = yc[:, c, :]
                link(ts(o, pad[:, c, 0:256], C("sconv", c), None, ALU.mult))
                link(stt(out=o, in0=pad[:, c, 1:257], scalar=C("sconv", 2 + c), in1=o, op0=ALU.mult, op1=ALU.add))
                link(stt(out=o, in0=pad[:, c, 2:258], scalar=C("sconv", 4 + c), in1=o, op0=ALU.mult, op1=ALU.add))
            link(tt(yc, yc, TT["cb"], ALU.mult), "dve_step")
            dve.wait_ge(S("ld_rows1"), 16)
            link(V.memset(v1[:, :, :, 64:65], 1.0))
            for i, (name, _) in enumerate(R1):
                b = got(dve, ("R1", i)).rearrange("p (t n) -> p t n", t=2)
                bias = rows1[:, i * GW:(i + 1) * GW]
                if name == "mv":
                    for t in range(NT):
                        ins = tt(v1[:, t, :, 0:HD], b[:, t, :].rearrange("p (h d) -> p h d", h=4),
                                 bias.rearrange("p (h d) -> p h d", h=4), ALU.add)
                        link(ins, "r1_copied" if t else "dve_step")
                else:
                    link(tt(RR[name], b, bias.unsqueeze(1).to_broadcast([P, NT, GW]), ALU.add), "r1_copied")
            rest_norm(1, "g_mem")
            link(V.tensor_copy(rc.rearrange("p q t h -> p (q t h)"), got(dve, ("mgT",))[:, 0:16]), "mgT_copied")
            ML = [(0, [0, 1], T), (0, [2, 3], T), (1, [0, 1, 2, 3], P)]
            for u, (s, heads, n) in enumerate(ML):
                b = got(dve, ("mD", u))
                for i, h in enumerate(heads):
                    ins = stt(out=EW[:, u % 2, i * n:(i + 1) * n], in0=b[:, i * n:(i + 1) * n], scalar=rc[:, 0, s, h:h + 1],
                              in1=K("maskT", 0, n), op0=ALU.add, op1=ALU.add)
                link(ins, "ml_arg")
                dve.wait_ge(S("ml_exp"), u + 1)
                link(stt(out=WT[:, u, :], in0=got(dve, ("mQK", u)), scalar=HD ** -0.5, in1=EW[:, u % 2, :],
                         op0=ALU.mult, op1=ALU.mult), "ml_w")
            for t in range(NT):
                b = got(dve, ("mO", t))[:, 0:260].rearrange("p (h d) -> p h d", h=4)
                link(stt(out=den[:, 0:4], in0=b[:, :, 64], scalar=-1.0, in1=rc[:, 1, t, :], op0=ALU.mult, op1=ALU.max))
                link(tt(den[:, 0:4], b[:, :, 64], den[:, 0:4], ALU.max))
                link(V.reciprocal(den[:, 4:8], den[:, 0:4]))
                link(tt(hm3[:, t], b[:, :, 0:HD], den[:, 4:8].unsqueeze(2).to_broadcast([P, 4, HD]), ALU.mult), "ml_h")
            link(V.memset(hgA[:, 0:2], 0.0))

            def exponents(lv):
                D = hgD[:, lv % 2, :]
                if lv <= 7:
                    B = 2 ** lv
                    h = B // 2
                    Dv, gv = D.rearrange("p (n b) -> p n b", b=B), g.rearrange("p (n b) -> p n b", b=B)
                    mid = gv[:, :, h - 1:h].to_broadcast([P, 512 // B, h])
                    tt(Dv[:, :, 0:h], mid, gv[:, :, 0:h], ALU.subtract)
                    if lv <= 6:
                        link(tt(Dv[:, :, h:B], gv[:, :, h:B], mid, ALU.subtract), "hg_d")
                    else:
                        link(V.tensor_copy(Dv[:, :, h:B], gv[:, :, h:B]), "hg_d")
                else:
                    Dv, gv = (z.rearrange("p (c k t) -> p c k t", c=2, k=4) for z in (D, g))
                    last = [gv[:, :, k, 63:64].to_broadcast([P, 2, 64]) for k in range(4)]
                    tt(Dv[:, :, 1, :], last[1], gv[:, :, 1, :], ALU.subtract)
                    V.tensor_copy(Dv[:, :, 2, :], gv[:, :, 2, :])
                    tt(Dv[:, :, 3, :], gv[:, :, 3, :], last[2], ALU.add)
                    link(tt(Dv[:, :, 0, :], last[0], gv[:, :, 0, :], ALU.subtract))
                    link(tt(Dv[:, :, 0, :], Dv[:, :, 0, :], last[1], ALU.add), "hg_d")

            exponents(1)
            for lv in range(1, LV + 1):
                if lv < LV:
                    exponents(lv + 1)
                B = 2 ** lv
                h = B // 2
                D, X, kv, qv = (z.rearrange("p (n b) -> p n b", b=B) for z in
                                (hgD[:, lv % 2, :], hgX[:, lv % 2, :], hk, hq))
                dve.wait_ge(S("hg_e"), lv)
                if lv == 1:
                    dve.wait_ge(S("hg_ln"), 1)
                tt(X[:, :, 0:h], D[:, :, 0:h], kv[:, :, 0:h], ALU.mult)
                link(tt(X[:, :, h:B], D[:, :, h:B], qv[:, :, h:B], ALU.mult), "hg_x")
                for t in range(NT):
                    b = got(dve, ("hG", lv - 1, t)).rearrange("p (h t) -> p h t", h=4)
                    mask = K("lvl", (lv - 1) * P, P).bitcast(U32).unsqueeze(1).to_broadcast([P, 4, P])
                    link(V.copy_predicated(hgA[:, t], mask, b), "hg_kept")
            got(dve, ("cv", 1))
            link(V.tensor_copy(XH[:, 2:4, :], yc))
            link(V.tensor_copy(hgA[:, 2], got(dve, ("hOff",)).rearrange("p (h t) -> p h t", h=4)), "hg_off")
            for t in range(NT):
                link(V.tensor_copy(ho[:, t, :], got(dve, ("hO", t))[:, 0:GW]), "hg_out")
            link(tt(XL[:, 2:4, :], yc, XH[:, 2:4, :].bitcast(F32), ALU.subtract), "conv_split")
            dve.wait_ge(S("gates_ready"), 1)
            head_norm(1, hm, rows1[:, 5 * GW:6 * GW], RR["mo"])
            head_norm(2, ho, rows1[:, 6 * GW:7 * GW], RR["hg"])
            dve.wait_ge(S("ld_rel"), 16 * 8)
            attention(ATT1, 0)
            for i in range(3):
                rest_turned(("yT", i), (0, 4, 6)[i], "yT_ready")
            post_norm(3, 1)
            inv_root(4, 0)
            normed(x)
            rest_norm(2, "g_cross")
            attention(ATT2, len(ATT1))
            for i in range(2):
                rest_turned(("coT", i), 2 * i, "coT_ready")
            post_norm(5, 2)
            inv_root(6, 0)
            normed(x)
            rest_norm(3, "g_ffn")
            link(V.memset(gpad[:, :, 0:2], 0.0), "gpad_zero")
            for f in range(FC + 1):
                if f < FC:
                    dve.wait_ge(S("ff_gate"), f + 1)
                    o, p = fa[:, f % 2, :], gpad[:, f % 2, :]
                    link(ts(o, p[:, 0:256], C("fconv", f), C("fb", f), ALU.mult, ALU.add))
                    link(stt(out=o, in0=p[:, 1:257], scalar=C("fconv", 22 + f), in1=o, op0=ALU.mult, op1=ALU.add))
                    link(stt(out=o, in0=p[:, 2:258], scalar=C("fconv", 44 + f), in1=o, op0=ALU.mult, op1=ALU.add),
                         "ff_conv")
                if f:
                    dve.wait_ge(S("ff_silu"), f)
                    b = got(dve, ("up", f - 1))
                    link(tt(ht, fa[:, (f - 1) % 2, :], b[:, T:2 * T], ALU.mult))
                    link(V.tensor_copy(hidh[:, f - 1, :], ht))
                    link(tt(hidl[:, f - 1, :], ht, hidh[:, f - 1, :].bitcast(F32), ALU.subtract), "ffn_hidden")
            post_norm(7, 3)
            inv_root(8, 0)
            normed(x)
            rest_norm(4, "g_mix2")
            link(V.tensor_copy(sel8[0:8], ident[0:8, 0:8].unsqueeze(2).to_broadcast([8, 8, T])))
            r8 = [cb[0:8, k, :] for k in range(6)]
            dve.wait_ge(S("fox_ln"), 1)
            link(ts(r8[2], r8[0], 0.0, None, ALU.min))
            link(tt(r8[2], r8[2], r8[1], ALU.subtract))
            link(V.memset(r8[4], 1.0))
            link(V.tensor_tensor_scan(r8[3], r8[4], r8[2], 0.0, ALU.mult, ALU.add))
            link(ts(r8[4], r8[3], HD ** 0.5, None, ALU.mult))
            link(ts(r8[5], r8[3], -HD ** 0.5, None, ALU.mult))
            for k in (4, 5):
                link(V.tensor_copy(cb[HD:HD + 8, k, :], r8[k]))
            link(V.tensor_copy(sel8[HD:HD + 8], sel8[0:8]), "fox_rows")
            dve.wait_ge(S("t2_copied"), 9)
            for j in range(2):
                for half in range(2):
                    v = kc2[:, j].rearrange("p g (a l e) -> p e l a g", l=8, e=2)[:, 0, :, half:half + NCMP, :]
                    at = slice(8 * half, 8 * half + 8)
                    pos = C("pos", 0, 64).rearrange("p (j l g) -> p j l g", j=2, l=16)[:, j, at, :]
                    link(tt(kw[:, j, at], v, pos.unsqueeze(2).to_broadcast([P, 8, NCMP, 2]), ALU.add))
            w = kw.rearrange("p j l n g -> p j l (n g)")
            link(V.tensor_copy(kwh, w))
            link(tt(kwl, w, kwh.bitcast(F32), ALU.subtract), "kw_split")
            for i in range(3):
                b = got(dve, ("rope", i)).rearrange("p (k t) -> p k t", k=2)
                o = t2[:, 8 + 2 * i:10 + 2 * i, :]
                r = rt[:, i % 2, :].rearrange("p (k t) -> p k t", k=2)
                link(tt(r, b, K("sinq").unsqueeze(1).to_broadcast([P, 2, T]), ALU.mult), "roped")
                link(tt(o, o, K("cosq").unsqueeze(1).to_broadcast([P, 2, T]), ALU.mult))
                link(tt(o, o, r, ALU.add), "roped_all" if i == 2 else "dve_step")
            link(tt(ckc[:, 1, 0:30], got(dve, ("crot",))[:, 0:30], K("sinc"), ALU.mult), "crot_done")
            link(tt(ckc[:, 2, 0:30], ckc[:, 0, 0:30], K("cosc"), ALU.mult))
            link(tt(ckc[:, 2, 0:30], ckc[:, 2, 0:30], ckc[:, 1, 0:30], ALU.add), "cmpk_ready")
            dve.wait_ge(S("ng_ready"), 1)
            attention(ATT3, len(ATT1) + len(ATT2))
            for i in range(4):
                rest_turned(("ysT", i), 2 * i, "ysT_ready")
            dve.wait_ge(S("merge_gated"), 8)
            for br in range(2):
                dve.wait_ge(S("acc_ready"), 4 + br)
                for t in range(NT):
                    o = mg[:, t, br, :]
                    link(tt(o, o, accf[:, t, :], ALU.mult), "acc_free" if t else "dve_step")
            link(tt(mg[:, :, 0, :], mg[:, :, 0, :], mg[:, :, 1, :], ALU.add), "merged")
            for i in range(4):
                rest_turned(("mT", i), 2 * i, "mT_ready")
            dve.wait_ge(S("acc_ready"), 6)
            for t in range(NT):
                link(tt(x[:, t, :], x[:, t, :], accf[:, t, :], ALU.add), "acc_free" if t else "resid_first")
            dve.nop().then_inc(S("resid"), 1)
            inv_root(9, 0)
            normed(x)
            rest_norm(5, "g_ffn2")
            topu, bestu = topi.bitcast(U32), besti.bitcast(U32)
            partu = part.bitcast(U32)
            lists = range(16)
            for t in range(NT):
                dve.wait_ge(S("ps_copied"), 4 * (t + 1))
                for k in lists:
                    ins = V.max(top[:, k, 0:8], ps[:, t, k, :])
                link(ins)
                for k in lists:
                    V.max_index(topu[:, k, 0:8], top[:, k, 0:8], ps[:, t, k, :])
                    ins = V.match_replace(ps[:, t, k, :], top[:, k, 0:8], ps[:, t, k, :], -3e38)
                link(ins)
                for k in lists:
                    ins = V.max(top[:, k, 8:16], ps[:, t, k, :])
                link(ins)
                for k in lists:
                    ins = V.max_index(topu[:, k, 8:16], top[:, k, 8:16], ps[:, t, k, :])
                link(ins)
                link(V.tensor_copy(topi, topu))
                for h in range(PH):
                    ins = tt(cand[:, h, :].rearrange("p (a b) -> p a b", a=TOPK),
                             top[:, 2 * h, :].unsqueeze(2).to_broadcast([P, TOPK, TOPK]),
                             top[:, 2 * h + 1, :].unsqueeze(1).to_broadcast([P, TOPK, TOPK]), ALU.add)
                link(ins)
                for h in range(PH):
                    ins = V.max(best[:, h, 0:8], cand[:, h, :])
                link(ins)
                for h in range(PH):
                    V.max_index(bestu[:, h, 0:8], best[:, h, 0:8], cand[:, h, :])
                    ins = V.match_replace(cand[:, h, :], best[:, h, 0:8], cand[:, h, :], -3e38)
                link(ins)
                for h in range(PH):
                    ins = V.max(best[:, h, 8:16], cand[:, h, :])
                link(ins)
                for h in range(PH):
                    ins = V.max_index(bestu[:, h, 8:16], best[:, h, 8:16], cand[:, h, :])
                link(ins)
                link(ts(wneg, best[:, :, 0], -1.0, None, ALU.mult))
                link(tt(best, best, wneg.unsqueeze(2).to_broadcast([P, PH, TOPK]), ALU.add), "best_ready")
                link(ts(partu[:, 0], bestu, 4, None, ALU.logical_shift_right))
                link(ts(partu[:, 1], bestu, 15, None, ALU.bitwise_and))
                link(V.tensor_copy(part, partu))
                for side in range(2):
                    link(tt(pick.rearrange("p h k j -> p (h k) j"),
                            part[:, side].rearrange("p h k -> p (h k)").unsqueeze(2).to_broadcast([P, P, TOPK]),
                            K("iota16").unsqueeze(1).to_broadcast([P, P, TOPK]), ALU.is_equal))
                    num = topi.rearrange("p (h s) n -> p h s n", s=2)[:, :, side, :]
                    link(tt(pick, pick, num.unsqueeze(2).to_broadcast([P, PH, TOPK, TOPK]), ALU.mult))
                    link(V.tensor_reduce(rout[:, side, :], pick.rearrange("p h k j -> p (h k) j"), AX.X, ALU.add))
                dve.wait_ge(S("best_exp"), t + 1)
                link(V.tensor_reduce(wsum, best, AX.X, ALU.add))
                link(V.reciprocal(wrec, wsum))
                link(tt(rout[:, 2, :].rearrange("p (h k) -> p h k", h=PH), best,
                        wrec.unsqueeze(2).to_broadcast([P, PH, TOPK]), ALU.mult), "routes")
                b = got(dve, ("rT", t))[:, 0:3 * P].rearrange("p (k t) -> p k t", k=3)
                link(V.tensor_copy(rT[:, :, t * P:(t + 1) * P], b), "rT_copied")
            with dve.Fori(0, T // (4 * NB)) as i:
                for q in range(NB):
                    dve.wait_ge(S("hot_used"), NB * i + q + 1)
                    for k in range(4):
                        def at(r):
                            return rT[:, r, bass.ds(4 * NB * i + (4 * q + k), 1)]
                        ts(hot[:, q % 2, 0, k, :], K("iota"), at(0), at(2), ALU.is_equal, ALU.mult)
                    tt(hot[:, q % 2, 1], K("iota").unsqueeze(1).to_broadcast([P, 4, NKEY]),
                       rT[:, 1, bass.ds(4 * NB * i + 4 * q, 4)].unsqueeze(2).to_broadcast([P, 4, NKEY]), ALU.is_equal
                       ).then_inc(S("hot_ready"), 1)
            dve.wait_ge(S("tabled"), T // 4 + 4)
            V.memset(zrow, 0.0).then_inc(S("zrow_ready"), 1)
            dve.nop().then_inc(S("ex_coef"), 2)

            def coefficients(n, b):
                g = gel[:, b % 2, :]
                tt(g, g, table[:, :, bass.ds(n, 1)].rearrange("p t o -> p (t o)"), ALU.mult).then_inc(S("ex_step"), 1)
                dve.wait_ge(S("ex_step"), 2 * n + 1)
                dve.wait_ge(S("ex_used"), n + 1)
                V.tensor_copy(ch[:, b % 2, :], g).then_inc(S("ex_step"), 1)
                dve.wait_ge(S("ex_step"), 2 * n + 2)
                tt(cl[:, b % 2, :], g, ch[:, b % 2, :].bitcast(F32), ALU.subtract).then_inc(S("ex_coef"), 1)

            with dve.Fori(0, AHEAD // EU) as i:
                for b in range(EU):
                    dve.wait_ge(S(f"gel_in{b % 2}"), 16 * (b // 2 + 1) + 16 * (EU // 2) * i)
                    coefficients(EU * i + b, b)
            with dve.Fori(0, REST // EU) as i:
                for b in range(EU):
                    dve.wait_ge(S("ex_gelu"), EU * i + b + 1)
                    coefficients(EU * i + (AHEAD + b), b)
            dve.wait_ge(S("ex_coef"), NKEY + 2)
            dve.nop().then_inc(S("x_wanted"), 1)
            dve.wait_ge(S("x_back"), 16)
            dve.wait_ge(S("acc_ready"), 7)
            for t in range(NT):
                link(tt(x[:, t, :], x[:, t, :], accf[:, t, :], ALU.add), "resid" if t else "resid_first")
            inv_root(10, 0)
            dve.wait_ge(S("ld_gain"), 64)
            for t in range(NT):
                link(stt(out=x[:, t, :], in0=x[:, t, :], scalar=rstd[:, t:t + 1], in1=gain,
                         op0=ALU.mult, op1=ALU.mult), "out_rows2" if t == 0 else "out_rows")


def constants():
    c = np.zeros((P, NCONST), np.float32)

    def put(name, v):
        at, w = CONST[name]
        c[:v.shape[0], at:at + w] = v.reshape(v.shape[0], w)

    p = np.arange(P)
    put("ident", np.eye(P, dtype=np.float32))
    t = (np.arange(NT)[None, :] * P + p[:, None])[:, :, None]
    put("maskR", np.where(np.arange(T)[None, None, :] <= t, 0.0, NEG).astype(np.float32))
    put("maskT", np.where(np.arange(T)[None, :] >= p[:, None], 0.0, NEG).astype(np.float32))
    u = np.arange(512)
    dist = u - 255
    n = np.maximum(dist, 1).astype(np.float32)
    large = 16 + (np.log(n / np.float32(16)) / np.float32(np.log(8.0)) * np.float32(16)).astype(np.int32)
    bucket = np.where(np.maximum(dist, 0) < 16, np.maximum(dist, 0), np.minimum(large, 31))
    oh = np.zeros((33, 512), np.float32)
    for j in range(512):
        d = 255 - j
        if d < 0:
            oh[32, j] = 1.0
        else:
            oh[bucket[d + 255], j] = 1.0
    put("oh", oh)
    s_, t_ = p[:, None], p[None, :]
    lv = np.zeros((P, 8, P), np.float32)
    lv[:, 0] = np.eye(P)
    for k in range(1, 8):
        B = 2 ** k
        lv[:, k] = (s_ // B == t_ // B) & (s_ % B < B // 2) & (t_ % B >= B // 2)
    put("lvl", lv)
    put("reset", np.broadcast_to((np.arange(512) % 64 != 0).astype(np.float32), (P, 512)))
    inv = np.power(np.float32(500000.0), -np.arange(0, 16, 2, dtype=np.float32) / np.float32(16))

    def rope(pos):
        ang = pos.astype(np.float32)[:, None] * inv[None, :]
        cos, sin = np.ones((P, len(pos)), np.float32), np.zeros((P, len(pos)), np.float32)
        for g in range(2):
            for half in range(2):
                at = 64 * g + 8 * half
                cos[at:at + 8], sin[at:at + 8] = np.cos(ang).T, np.sin(ang).T
        return cos, sin

    cq, sq = rope(np.arange(T))
    put("cosq", cq)
    put("sinq", sq)
    rot = np.zeros((P, P), np.float32)
    for g in range(2):
        for j in range(8):
            rot[64 * g + 8 + j, 64 * g + j] = -1.0
            rot[64 * g + j, 64 * g + 8 + j] = 1.0
    put("rot", rot)
    end = np.tile(np.arange(NCMP) * 16 + 31, 2)
    cc, sc = rope(end)
    put("cosc", cc)
    put("sinc", sc)
    put("iota", np.broadcast_to(np.arange(128, dtype=np.float32), (P, 128)))
    put("iota16", np.broadcast_to(np.arange(16, dtype=np.float32), (P, 16)))
    put("maskC", np.where(end[None, None, :NCMP] <= t, 0.0, NEG).astype(np.float32))
    put("valid", (t[:, :, 0] >= 31).astype(np.float32))
    return c


def layout(inp):
    f = {k: np.asarray(v) for k, v in inp.items()}
    w1, w2 = f["w_in"][0], f["w_in_2"][0]

    def chunked(w, cols):
        w = w[:, cols]
        return w.reshape(-1, P, w.shape[1]).transpose(1, 0, 2).reshape(P, -1)

    def span(a, n=256):
        return np.arange(a, a + n)

    nq = np.concatenate([np.concatenate([span(Q_NQ + HD * b, HD), span(Q_NQ + HD * (4 + b), HD)]) for b in range(4)])

    def doubled(at):
        return np.concatenate([span(at + HD * g, HD) for g in (0, 0, 1, 1)])

    up = f["w_ffn_in"][0]

    def two_chunks(w, i):
        return chunked(w[256 * i:256 * i + 256], slice(None))

    def blocks(v):
        return v.reshape(P, KC, 2, P).transpose(0, 2, 1, 3).reshape(P, -1)

    def slot(key):
        v = slot_rows(key)
        return blocks(v) if key[0] in ("T1", "ck", "cq", "up", "fq", "fk", "nq", "kk", "kc", "vc", "pq") else v

    def slot_rows(key):
        kind, i = key[0], (key[1] if len(key) > 1 else 0)
        s = span(256 * i)
        if kind in ("T1", "R1"):
            return chunked(w1, span((T1 if kind == "T1" else R1)[i][1]))
        if kind in ("ck", "cv", "cq"):
            return chunked(f["w_" + kind][0], s)
        if kind == "mix":
            return two_chunks(f["w_mix_out"][0], i)
        if kind == "co":
            return two_chunks(f["w_co"][0], i)
        if kind == "up":
            return chunked(up, np.concatenate([span(P * i, P), span(DFF + P * i, P)]))
        if kind == "down":
            return two_chunks(f["w_ffn_out"][0], i)
        if kind in ("fq", "fk", "fv"):
            return chunked(w2, {"fq": Q_FQ, "fk": Q_FK, "fv": Q_FV}[kind] + s)
        if kind == "nq":
            return chunked(w2, nq[256 * i:256 * i + 256])
        if kind == "kk":
            return chunked(w2, np.concatenate([span(Q_KS, P), span(Q_KW, P)]))
        if kind in ("kc", "vc"):
            return chunked(w2, doubled(Q_KC if kind == "kc" else Q_VC))
        if kind == "vv":
            return chunked(w2, np.concatenate([span(Q_VS, P), span(Q_VW, P)]))
        if kind == "cw1":
            return f["nsa_cmp_w1_2"][0, i].reshape(16, P, P).transpose(1, 0, 2).reshape(P, -1)
        if kind == "merge":
            return chunked(w2, Q_MERGE + s)
        if kind == "branch":
            return two_chunks(f["w_branch_2"][0, i // 2], i % 2)
        if kind == "wout":
            return two_chunks(f["w_out_2"][0], i)
        assert kind == "pq"
        return chunked(f["peer_wq_2"][0], s)

    ws = np.empty((NPIECE, P, PC), np.float32)
    for n, key in enumerate(SLOTS):
        ws[2 * n:2 * n + 2] = slot(key).reshape(P, 2, PC).transpose(1, 0, 2)
    u = f["peer_u_2"][0].reshape(NKEY, NKEY, KC, P).transpose(1, 3, 2, 0).reshape(NKEY, P, PC)
    v = f["peer_v_2"][0].reshape(NKEY, NKEY, DM).transpose(1, 0, 2)
    ws[[piece_u(n) for n in range(NKEY)]] = u
    ws[[piece_v(n) for n in range(NKEY)]] = v

    cols = np.zeros((P, NCOLS), np.float32)

    def put(name, v):
        at, w = COLS[name]
        cols[:v.shape[0], at:at + w] = v.reshape(v.shape[0], w)

    def col(v):
        return v.reshape(-1, P).T

    b = f["b_in"][0]
    put("b1", np.concatenate([col(b[o:o + GW]) for _, o in T1], axis=1))
    put("bi", b[O_GI:O_GI + 4, None])
    put("bf", b[O_GF:O_GF + 4, None])
    for name, key in (("g_mix", "norm_mix_pre"), ("g_mem", "mem_norm"), ("g_cross", "norm_cross_pre"),
                      ("g_ffn", "norm_ffn_pre"), ("g_mix2", "norm_mix_2"), ("g_ffn2", "norm_ffn_2"),
                      ("sconv", "sconv_w"), ("lb", "hgrn_lb_logits"), ("fconv", "ffn_conv_w"), ("fb", "ffn_conv_b")):
        put(name, col(f[key][0]))
    put("foxb", f["fox_f_bias_2"][0][:, None])
    put("rel", f["rel_bias"])
    cw2 = f["nsa_cmp_w2_2"][0]
    put("w2k", np.concatenate([cw2[0], cw2[0]], axis=1))
    put("w2v", cw2[1])
    put("pos", np.repeat(f["nsa_cmp_pos_2"][0].reshape(2, 16, P).transpose(2, 0, 1).reshape(P, 32), 2, axis=1))
    put("wg1", chunked(w1, span(O_GI, 8)))
    put("wg2", chunked(w2, np.concatenate([span(Q_FL, 8), span(Q_GATE, 24)])))
    rows1 = np.concatenate([b[o:o + GW] for _, o in R1] + [f["mlstm_norm"][0], f["hgrn_norm"][0]])
    gains = np.stack([f["norm_mix_post"][0], f["norm_cross_post"][0], f["norm_ffn_post"][0], f["norm_final_2"]])
    keys = f["peer_subkeys_2"][0].transpose(3, 0, 1, 2).reshape(P, -1)
    return {"x": f["x"], "mem": f["mem"], "consts": constants(), "cols": cols, "wstream": ws,
            "rows1": rows1, "gains": gains, "keys": keys}


def kernel(**inputs):
    import concourse.bacc as bacc
    from concourse.bass_utils import run_bass_kernel_spmd

    arrays = {k: np.ascontiguousarray(v) for k, v in layout(inputs).items()}
    nc = bacc.Bacc("TRN2", target_bir_lowering=False, num_devices=1)
    a = {k: nc.dram_tensor(k, v.shape, mybir.dt.from_np(v.dtype), kind="ExternalInput").ap()
         for k, v in arrays.items()}
    a["out"] = nc.dram_tensor("out", (1, T, DM), F32, kind="ExternalOutput").ap()
    build(nc, a)
    return run_bass_kernel_spmd(nc, [arrays], core_ids=[0]).results[0]["out"]
```
